# Optimizing a Trainium2 kernel written in Bass

```python
import jax, jax.numpy as jnp
from jax import lax
import numpy as np
import math
import jax
import jax.numpy as jnp

D_MODEL = 1024
BATCH = 1
SEQ = 256
DEPTH = 2

A_HEADS = 8
A_HEAD_DIM = 64
A_WIDTH = A_HEADS * A_HEAD_DIM
DILATED_PATTERNS = ((128, 1), (512, 4), (2048, 16))
A_HALF_STEPS = 64
A_BLOCK = 64
REL_BUCKETS = 32
REL_MAX_DISTANCE = 1024
B_HEADS = 4
B_KEY_DIM = 128
B_VAL_DIM = 256
B_K_WIDTH = B_HEADS * B_KEY_DIM
B_V_WIDTH = B_HEADS * B_VAL_DIM
B_GATE_RANK = 16
B_GATE_NORMALIZER = 16.0
C_HEADS = 12
C_HEAD_DIM = 128
C_WIDTH = C_HEADS * C_HEAD_DIM
MIX_WIDTH = A_WIDTH + B_V_WIDTH
AB_IN_WIDTH = 3 * A_WIDTH + 2 * B_K_WIDTH + B_V_WIDTH + 2 * B_GATE_RANK + MIX_WIDTH
C_IN_WIDTH = 5 * C_WIDTH
CHUNK = 32
N_EVEN = (DEPTH + 1) // 2
N_ODD = DEPTH // 2
NORM_EPS = 1e-5
DEEPNORM_ALPHA = (2 * DEPTH) ** 0.25
DEEPNORM_BETA = (8 * DEPTH) ** -0.25


def _split(t, sizes):
    out, start = [], 0
    for n in sizes:
        out.append(t[..., start:start + n])
        start += n
    return out

def _t5_bucket(rel):
    half = REL_BUCKETS // 2
    max_exact = half // 2
    n = np.abs(rel)
    large = max_exact + (np.log(np.maximum(n, 1) / max_exact)
                         / np.log(REL_MAX_DISTANCE / max_exact) * (half - max_exact)).astype(np.int32)
    large = np.minimum(large, half - 1)
    return np.where(rel > 0, half, 0) + np.where(n < max_exact, n, large)

def _dilated_band_attention(q, k, v, rel_bias, dilation):
    Bsz, S, H, E = q.shape
    L = S // dilation
    nb = -(-L // A_BLOCK)
    Lp = nb * A_BLOCK

    def to_sub(t):
        return t.reshape(Bsz, L, dilation, H, E).transpose(0, 2, 1, 3, 4)

    qs, ks, vs = to_sub(q), to_sub(k), to_sub(v)
    qs = jnp.pad(qs, ((0, 0), (0, 0), (0, Lp - L), (0, 0), (0, 0))).reshape(Bsz, dilation, nb, A_BLOCK, H, E)

    def band(t):
        t = jnp.pad(t, ((0, 0), (0, 0), (A_BLOCK, Lp - L + A_BLOCK), (0, 0), (0, 0)))
        t = t.reshape(Bsz, dilation, nb + 2, A_BLOCK, H, E)
        return jnp.concatenate([t[:, :, :-2], t[:, :, 1:-1], t[:, :, 2:]], axis=3)

    kb, vb = band(ks), band(vs)
    qi = np.arange(A_BLOCK)[:, None]
    kj = np.arange(3 * A_BLOCK)[None, :]
    off = kj - A_BLOCK - qi
    key_idx = np.arange(nb)[:, None, None] * A_BLOCK + kj[None] - A_BLOCK
    mask = (np.abs(off) <= A_HALF_STEPS)[None] & (key_idx >= 0) & (key_idx < L)
    bias = jnp.transpose(rel_bias.astype(jnp.float32)[_t5_bucket(off * dilation)], (2, 0, 1))
    s = jnp.einsum('brnqhe,brnkhe->brnhqk', qs, kb) * (E ** -0.5) + bias
    s = jnp.where(mask[None, None, :, None], s, -jnp.inf)
    lse = jax.nn.logsumexp(s, axis=-1)
    p = jnp.exp(s - lse[..., None])
    o = jnp.einsum('brnhqk,brnkhe->brnqhe', p, vb).reshape(Bsz, dilation, Lp, H, E)[:, :, :L]
    o = o.transpose(0, 2, 1, 3, 4).reshape(Bsz, S, H, E)
    lse = lse.transpose(0, 1, 2, 4, 3).reshape(Bsz, dilation, Lp, H)[:, :, :L]
    lse = lse.transpose(0, 2, 1, 3).reshape(Bsz, S, H)
    return o, lse

def dilated_attention(q, k, v, rel_bias):
    outs, lses = [], []
    for _, dilation in DILATED_PATTERNS:
        o, lse = _dilated_band_attention(q, k, v, rel_bias, dilation)
        outs.append(o)
        lses.append(lse)
    w = jax.nn.softmax(jnp.stack(lses, 0), axis=0)
    return jnp.einsum('pbsh,pbshe->bshe', w, jnp.stack(outs, 0))

def _chunk_gated_scan(q, k, v, log_g):
    Bsz, S, H, K = q.shape
    V = v.shape[-1]
    N = S // CHUNK
    c = lambda t: t.reshape(Bsz, N, CHUNK, H, t.shape[-1])
    q, k, v, log_g = c(q), c(k), c(v), c(log_g)
    b = jnp.cumsum(log_g, axis=2)
    ref = b[:, :, CHUNK // 2 - 1:CHUNK // 2]
    s = jnp.einsum('bnthk,bnshk->bnhts', q * jnp.exp(b - ref), k * jnp.exp(ref - b))
    s = jnp.where(np.tril(np.ones((CHUNK, CHUNK), bool)), s, 0.0)
    o_intra = jnp.einsum('bnhts,bnshv->bnthv', s, v)
    b_last = b[:, :, -1]
    q_dec = q * jnp.exp(b)
    k_dec = k * jnp.exp(b_last[:, :, None] - b)

    def step(state, xs):
        qd, kd, vc, bl = xs
        o = jnp.einsum('bthk,bhkv->bthv', qd, state)
        state = jnp.exp(bl)[..., None] * state + jnp.einsum('bthk,bthv->bhkv', kd, vc)
        return state, o

    xs = (jnp.moveaxis(q_dec, 1, 0), jnp.moveaxis(k_dec, 1, 0), jnp.moveaxis(v, 1, 0), jnp.moveaxis(b_last, 1, 0))
    _, o_inter = lax.scan(step, jnp.zeros((Bsz, H, K, V), jnp.float32), xs)
    return (o_intra + jnp.moveaxis(o_inter, 0, 1)).reshape(Bsz, S, H, V)

def bidirectional_gated_scan(q, k_fwd, g_fwd, k_bwd, g_bwd, v):
    fwd = _chunk_gated_scan(q, k_fwd, v, g_fwd)
    flip = lambda t: jnp.flip(t, axis=1)
    bwd = flip(_chunk_gated_scan(flip(q), flip(k_bwd), flip(v), flip(g_bwd)))
    diag = jnp.sum(q * k_bwd, axis=-1, keepdims=True) * v
    return fwd + bwd - diag

def _head_rmsnorm(o, gain):
    o = o * lax.rsqrt(jnp.mean(o * o, axis=-1, keepdims=True) + NORM_EPS)
    return o.reshape(o.shape[0], o.shape[1], -1) * gain.astype(jnp.float32)

def _layer_norm(z, g, b):
    z32 = z.astype(jnp.float32)
    mu = jnp.mean(z32, axis=-1, keepdims=True)
    var = jnp.mean(jnp.square(z32 - mu), axis=-1, keepdims=True)
    out = (z32 - mu) * lax.rsqrt(var + NORM_EPS) * g.astype(jnp.float32) + b.astype(jnp.float32)
    return out.astype(z.dtype)

def _mixer_ab(h, w_in, gate_up, gate_bias, norm_gain, w_out, rel_bias):
    Bsz, S, _ = h.shape
    proj = jnp.einsum('bsd,df->bsf', h, w_in).astype(jnp.float32)
    qa, ka, va, qb, kb, vb, lr_f, lr_b, gate = _split(
        proj, (A_WIDTH, A_WIDTH, A_WIDTH, B_K_WIDTH, B_K_WIDTH, B_V_WIDTH, B_GATE_RANK, B_GATE_RANK, MIX_WIDTH))
    heads = lambda t, n: t.reshape(Bsz, S, n, -1)
    oa = dilated_attention(heads(qa, A_HEADS), heads(ka, A_HEADS), heads(va, A_HEADS), rel_bias)
    oa = oa.reshape(Bsz, S, A_WIDTH)
    up = gate_up.astype(jnp.float32)
    gb_ = gate_bias.astype(jnp.float32)
    g_f = jax.nn.log_sigmoid(lr_f @ up[0] + gb_[0]) / B_GATE_NORMALIZER
    g_b = jax.nn.log_sigmoid(lr_b @ up[1] + gb_[1]) / B_GATE_NORMALIZER
    qh = heads(qb, B_HEADS) * (B_KEY_DIM ** -0.5)
    kh = heads(kb, B_HEADS)
    ob = bidirectional_gated_scan(qh, kh, heads(g_f, B_HEADS), kh, heads(g_b, B_HEADS), heads(vb, B_HEADS))
    ob = _head_rmsnorm(ob, norm_gain)
    y = jnp.concatenate([oa, ob], axis=-1) * jax.nn.silu(gate)
    return jnp.einsum('bsf,fd->bsd', y.astype(h.dtype), w_out)

def _mixer_c(h, w_in, lower_bounds, layer_idx, norm_gain, w_out):
    Bsz, S, _ = h.shape
    proj = jnp.einsum('bsd,df->bsf', h, w_in).astype(jnp.float32)
    q, f_f, f_b, i, gate = _split(proj, (C_WIDTH,) * 5)
    lb = jax.nn.softmax(lower_bounds.astype(jnp.float32), axis=0)
    lb = (jnp.cumsum(lb, axis=0) - lb[0])[layer_idx]
    heads = lambda t: t.reshape(Bsz, S, C_HEADS, C_HEAD_DIM)

    def forget(z):
        f = lb + (1.0 - lb) * jax.nn.sigmoid(z)
        return heads(1.0 - f), heads(jnp.log(f))

    k_f, g_f = forget(f_f)
    k_b, g_b = forget(f_b)
    qh = heads(jax.nn.silu(q)) * (C_HEAD_DIM ** -0.5)
    o = bidirectional_gated_scan(qh, k_f, g_f, k_b, g_b, heads(i))
    y = _head_rmsnorm(o, norm_gain) * jax.nn.silu(gate)
    return jnp.einsum('bsf,fd->bsd', y.astype(h.dtype), w_out)

def first_inputs(seed: int = 0) -> dict:
    key = jax.random.key(seed)
    ks = jax.random.split(key, 13)
    f32 = jnp.float32
    nrm = lambda k, shape, s: jax.random.normal(k, shape, f32) * s
    return {
        'x': nrm(ks[0], (BATCH, SEQ, D_MODEL), 1.0),
        'w_in_ab': nrm(ks[1], (N_EVEN, D_MODEL, AB_IN_WIDTH), D_MODEL ** -0.5),
        'gla_gate_up': nrm(ks[2], (N_EVEN, 2, B_GATE_RANK, B_K_WIDTH), B_GATE_RANK ** -0.5),
        'gla_gate_bias': nrm(ks[3], (N_EVEN, 2, B_K_WIDTH), 0.1),
        'gla_norm': 1.0 + nrm(ks[4], (N_EVEN, B_V_WIDTH), 0.02),
        'w_out_ab': nrm(ks[5], (N_EVEN, MIX_WIDTH, D_MODEL), MIX_WIDTH ** -0.5 * DEEPNORM_BETA),
        'w_in_c': nrm(ks[6], (N_ODD, D_MODEL, C_IN_WIDTH), D_MODEL ** -0.5),
        'hgrn_lower_bounds': nrm(ks[7], (DEPTH, C_WIDTH), 0.1),
        'hgrn_norm': 1.0 + nrm(ks[8], (N_ODD, C_WIDTH), 0.02),
        'w_out_c': nrm(ks[9], (N_ODD, C_WIDTH, D_MODEL), C_WIDTH ** -0.5 * DEEPNORM_BETA),
        'rel_bias': nrm(ks[10], (REL_BUCKETS, A_HEADS), 0.1),
        'ln_gain': 1.0 + nrm(ks[11], (DEPTH, D_MODEL), 0.02),
        'ln_bias': nrm(ks[12], (DEPTH, D_MODEL), 0.02),
    }

def first_block(x, w_in_ab, gla_gate_up, gla_gate_bias, gla_norm, w_out_ab, w_in_c,
              hgrn_lower_bounds, hgrn_norm, w_out_c, rel_bias, ln_gain, ln_bias):
    for layer in range(DEPTH):
        if layer % 2 == 0:
            e = layer // 2
            y = _mixer_ab(x, w_in_ab[e], gla_gate_up[e], gla_gate_bias[e], gla_norm[e], w_out_ab[e], rel_bias)
        else:
            o = layer // 2
            y = _mixer_c(x, w_in_c[o], hgrn_lower_bounds, layer, hgrn_norm[o], w_out_c[o])
        x = _layer_norm(DEEPNORM_ALPHA * x + y, ln_gain[layer], ln_bias[layer])
    return x


DN_HEADS = 8
DN_DK = 64
DN_DV = 64
DN_CHUNK = 64
CONV_W = 4
DN_QKV = DN_HEADS * (2 * DN_DK + DN_DV)
NSA_HEADS = 8
NSA_GROUPS = 2
NSA_HPG = NSA_HEADS // NSA_GROUPS
NSA_DH = 64
CMP_LEN = 32
CMP_STRIDE = 16
SEL_LEN = 64
SEL_TOP = 16
WINDOW = 512
NSA_Q_BLOCK = 64
ROPE_THETA = 10000.0
FFN_DIM = 3584
N_EXPERTS = 8
TOP_K = 2
EPS = 1e-6
NEG = -1e30
FORCE = 1e6

SPLIT_SIZES = (
    DN_QKV,
    DN_HEADS * DN_DV,
    DN_HEADS,
    DN_HEADS,
    NSA_HEADS * NSA_DH,
    NSA_GROUPS * NSA_DH,
    NSA_GROUPS * NSA_DH,
    NSA_GROUPS * NSA_DH,
    NSA_GROUPS * NSA_DH,
    NSA_GROUPS * NSA_DH,
    NSA_GROUPS * NSA_DH,
    3 * NSA_HEADS,
    2 * D_MODEL,
)
P_IN = sum(SPLIT_SIZES)


def rms_norm(x, w):
    xf = x.astype(jnp.float32)
    y = xf * lax.rsqrt(jnp.mean(xf * xf, -1, keepdims=True) + EPS)
    return (y * w.astype(jnp.float32)).astype(x.dtype)

def l2_norm(x):
    xf = x.astype(jnp.float32)
    return (xf * lax.rsqrt(jnp.sum(xf * xf, -1, keepdims=True) + EPS)).astype(x.dtype)

def rope_angles(pos):
    inv = 1.0 / (ROPE_THETA ** (jnp.arange(0, NSA_DH, 2, dtype=jnp.float32) / NSA_DH))
    ang = pos.astype(jnp.float32)[..., None] * inv
    return jnp.cos(ang)[:, :, None, :], jnp.sin(ang)[:, :, None, :]

def apply_rope(x, cos, sin):
    xf = x.astype(jnp.float32)
    x1, x2 = jnp.split(xf, 2, -1)
    return jnp.concatenate([x1 * cos - x2 * sin, x2 * cos + x1 * sin], -1).astype(x.dtype)

def masked_softmax(s, mask):
    s = jnp.where(mask, s.astype(jnp.float32), NEG)
    m = jnp.max(s, -1, keepdims=True)
    e = jnp.where(mask, jnp.exp(s - m), 0.0)
    return e / jnp.maximum(jnp.sum(e, -1, keepdims=True), 1e-30)

def causal_conv_silu(x, w):
    ch = x.shape[-1]
    y = lax.conv_general_dilated(x, w[:, None, :].astype(x.dtype), window_strides=(1,),
                                 padding=[(CONV_W - 1, 0)],
                                 dimension_numbers=('NWC', 'WIO', 'NWC'),
                                 feature_group_count=ch)
    return jax.nn.silu(y)

def gated_delta_rule(q, k, v, beta, g):
    b_, s_, h_, dk = q.shape
    dv = v.shape[-1]
    n, c = s_ // DN_CHUNK, DN_CHUNK
    f32 = jnp.float32
    qc = q.astype(f32).reshape(b_, n, c, h_, dk).transpose(1, 0, 3, 2, 4)
    kc = k.astype(f32).reshape(b_, n, c, h_, dk).transpose(1, 0, 3, 2, 4)
    vc = v.astype(f32).reshape(b_, n, c, h_, dv).transpose(1, 0, 3, 2, 4)
    bc = beta.astype(f32).reshape(b_, n, c, h_).transpose(1, 0, 3, 2)
    gc = jnp.cumsum(g.astype(f32).reshape(b_, n, c, h_).transpose(1, 0, 3, 2), axis=-1)
    tril = jnp.tril(jnp.ones((c, c), bool))
    strict = jnp.tril(jnp.ones((c, c), bool), -1)
    diff = gc[..., :, None] - gc[..., None, :]
    decay = jnp.where(tril, jnp.exp(jnp.where(tril, diff, 0.0)), 0.0)
    kb = kc * bc[..., None]
    lower = jnp.where(strict, jnp.einsum('nbhcd,nbhsd->nbhcs', kb, kc) * decay, 0.0)
    eye = jnp.eye(c, dtype=f32)
    tinv = lax.linalg.triangular_solve(eye + lower, jnp.broadcast_to(eye, lower.shape),
                                       left_side=True, lower=True, unit_diagonal=True)
    u = tinv @ (vc * bc[..., None])
    w = tinv @ (kb * jnp.exp(gc)[..., None])
    a_intra = jnp.where(tril, jnp.einsum('nbhcd,nbhsd->nbhcs', qc, kc) * decay, 0.0)
    q_dec = qc * jnp.exp(gc)[..., None]
    k_dec = kc * jnp.exp(gc[..., -1:] - gc)[..., None]
    g_last = jnp.exp(gc[..., -1])

    def step(state, xs):
        u_n, w_n, a_n, qd_n, kd_n, gl_n = xs
        v_new = u_n - w_n @ state
        o_n = qd_n @ state + a_n @ v_new
        state = state * gl_n[..., None, None] + jnp.swapaxes(kd_n, -1, -2) @ v_new
        return state, o_n

    s0 = jnp.zeros((b_, h_, dk, dv), f32)
    _, o = lax.scan(step, s0, (u, w, a_intra, q_dec, k_dec, g_last))
    return o.transpose(1, 0, 3, 2, 4).reshape(b_, s_, h_, dv).astype(q.dtype)

def compress_blocks(x, pos_emb, w1, w2):
    b_, s_ = x.shape[:2]
    n_cmp = (s_ - CMP_LEN) // CMP_STRIDE + 1
    idx = jnp.arange(n_cmp)[:, None] * CMP_STRIDE + jnp.arange(CMP_LEN)[None, :]
    blk = x[:, idx] + pos_emb[None, None, :, None, :]
    blk = blk.transpose(0, 1, 3, 2, 4).reshape(b_, n_cmp, NSA_GROUPS, CMP_LEN * NSA_DH)
    return jax.nn.silu(blk @ w1) @ w2

def nsa_core(q, k_c, v_c, k_s, v_s, k_w, v_w, gates):
    b_, s_ = q.shape[:2]
    n_cmp = k_c.shape[1]
    n_sel = s_ // SEL_LEN
    k_top = min(SEL_TOP, n_sel)
    qbk = NSA_Q_BLOCK
    scale = NSA_DH ** -0.5
    cmp_start = jnp.arange(n_cmp) * CMP_STRIDE
    cmp_end = cmp_start + CMP_LEN - 1
    blk_start = jnp.arange(n_sel) * SEL_LEN
    overlap = ((cmp_start[:, None] < blk_start[None, :] + SEL_LEN) &
               (cmp_start[:, None] + CMP_LEN > blk_start[None, :])).astype(jnp.float32)
    ks_blocks = k_s.reshape(b_, n_sel, SEL_LEN, NSA_GROUPS, NSA_DH).transpose(0, 3, 1, 2, 4)
    vs_blocks = v_s.reshape(b_, n_sel, SEL_LEN, NSA_GROUPS, NSA_DH).transpose(0, 3, 1, 2, 4)
    kw_pad = jnp.pad(k_w, ((0, 0), (WINDOW, 0), (0, 0), (0, 0)))
    vw_pad = jnp.pad(v_w, ((0, 0), (WINDOW, 0), (0, 0), (0, 0)))
    b_ix = jnp.arange(b_)[:, None, None, None]
    g_ix = jnp.arange(NSA_GROUPS)[None, :, None, None]
    jb = jnp.arange(n_sel)

    def block(s0):
        t = s0 + jnp.arange(qbk)
        qb = lax.dynamic_slice_in_dim(q, s0, qbk, 1).reshape(b_, qbk, NSA_GROUPS, NSA_HPG, NSA_DH) * scale
        s_c = jnp.einsum('bqghd,bcgd->bghqc', qb, k_c)
        p_c = masked_softmax(s_c, cmp_end[None, :] <= t[:, None])
        o_c = jnp.einsum('bghqc,bcgd->bqghd', p_c.astype(v_c.dtype), v_c)
        imp = jnp.einsum('bghqc,cj->bgqj', p_c, overlap)
        cur = t // SEL_LEN
        forced = (jb[None] == 0) | (jb[None] == cur[:, None]) | (jb[None] == cur[:, None] - 1)
        causal = blk_start[None] <= t[:, None]
        imp = jnp.where(forced, FORCE, jnp.where(causal, imp, -FORCE))
        _, sel = lax.top_k(imp, k_top)
        k_sel = ks_blocks[b_ix, g_ix, sel]
        v_sel = vs_blocks[b_ix, g_ix, sel]
        tok = sel[..., None] * SEL_LEN + jnp.arange(SEL_LEN)
        m_s = (tok <= t[:, None, None]).reshape(b_, NSA_GROUPS, 1, qbk, k_top * SEL_LEN)
        s_s = jnp.einsum('bqghd,bgqkld->bghqkl', qb, k_sel).reshape(
            b_, NSA_GROUPS, NSA_HPG, qbk, k_top * SEL_LEN)
        p_s = masked_softmax(s_s, m_s).reshape(b_, NSA_GROUPS, NSA_HPG, qbk, k_top, SEL_LEN)
        o_s = jnp.einsum('bghqkl,bgqkld->bqghd', p_s.astype(v_sel.dtype), v_sel)
        kw = lax.dynamic_slice_in_dim(kw_pad, s0, qbk + WINDOW, 1)
        vw = lax.dynamic_slice_in_dim(vw_pad, s0, qbk + WINDOW, 1)
        u = s0 - WINDOW + jnp.arange(qbk + WINDOW)
        dist = t[:, None] - u[None, :]
        m_w = (dist >= 0) & (dist < WINDOW) & (u[None, :] >= 0)
        s_w = jnp.einsum('bqghd,bkgd->bghqk', qb, kw)
        p_w = masked_softmax(s_w, m_w)
        o_w = jnp.einsum('bghqk,bkgd->bqghd', p_w.astype(vw.dtype), vw)
        gb = lax.dynamic_slice_in_dim(gates, s0, qbk, 1).reshape(b_, qbk, NSA_GROUPS, NSA_HPG, 3)
        o = gb[..., 0:1] * o_c + gb[..., 1:2] * o_s + gb[..., 2:3] * o_w
        return o.reshape(b_, qbk, NSA_HEADS * NSA_DH)

    out = lax.map(block, jnp.arange(s_ // qbk) * qbk)
    return out.transpose(1, 0, 2, 3).reshape(b_, s_, NSA_HEADS * NSA_DH)

def swiglu(h, w1, w3, w2):
    return (jax.nn.silu(h @ w1) * (h @ w3)) @ w2

def moe_ffn(h, w_router, w1, w3, w2):
    logits = (h @ w_router).astype(jnp.float32)
    top_val, top_idx = lax.top_k(logits, TOP_K)
    top_w = jax.nn.softmax(top_val, -1)
    combine = jnp.sum(jax.nn.one_hot(top_idx, N_EXPERTS, dtype=jnp.float32) * top_w[..., None], -2)
    out = jnp.zeros_like(h)
    for e in range(N_EXPERTS):
        out = out + combine[..., e:e + 1].astype(h.dtype) * swiglu(h, w1[e], w3[e], w2[e])
    return out

def second_inputs(seed: int = 0) -> dict:
    key = jax.random.key(seed)
    keys = iter(jax.random.split(key, 40))

    def nrm(shape, scale):
        return jax.random.normal(next(keys), shape, jnp.float32) * scale

    L, D = DEPTH, D_MODEL
    n_dense, n_moe = (DEPTH + 1) // 2, DEPTH // 2
    x = nrm((BATCH, SEQ, D), 1.0)
    c = nrm((BATCH, D), 1.0)
    positions = (jnp.arange(SEQ, dtype=jnp.int32)[None, :] +
                 jax.random.randint(next(keys), (BATCH, 1), 0, 1024, dtype=jnp.int32))
    w_ada = nrm((L, D, 6 * D), 0.5 * D ** -0.5)
    b_ada = nrm((L, 6 * D), 0.01)
    norm_mix = 1.0 + nrm((L, D), 0.05)
    norm_ffn = 1.0 + nrm((L, D), 0.05)
    w_in = nrm((L, D, P_IN), D ** -0.5)
    conv_w = nrm((L, CONV_W, DN_QKV), CONV_W ** -0.5)
    a_log = jnp.log(jax.random.uniform(next(keys), (L, DN_HEADS), jnp.float32, 1.0, 16.0))
    dt = jnp.exp(jax.random.uniform(next(keys), (L, DN_HEADS), jnp.float32,
                                    math.log(1e-3), math.log(1e-1)))
    dt_bias = dt + jnp.log(-jnp.expm1(-dt))
    dn_norm = 1.0 + nrm((L, DN_DV), 0.05)
    cmp_pos = nrm((L, 2, CMP_LEN, NSA_DH), 0.1)
    w_cmp1 = nrm((L, 2, CMP_LEN * NSA_DH, NSA_DH), (CMP_LEN * NSA_DH) ** -0.5)
    w_cmp2 = nrm((L, 2, NSA_DH, NSA_DH), NSA_DH ** -0.5)
    q_norm = 1.0 + nrm((L, NSA_DH), 0.05)
    k_norm = 1.0 + nrm((L, 3, NSA_DH), 0.05)
    w_oa = nrm((L, DN_HEADS * DN_DV, D), (DN_HEADS * DN_DV) ** -0.5)
    w_ob = nrm((L, NSA_HEADS * NSA_DH, D), (NSA_HEADS * NSA_DH) ** -0.5)
    w_out = nrm((L, D, D), D ** -0.5)
    w1_dense = nrm((n_dense, D, FFN_DIM), D ** -0.5)
    w3_dense = nrm((n_dense, D, FFN_DIM), D ** -0.5)
    w2_dense = nrm((n_dense, FFN_DIM, D), FFN_DIM ** -0.5)
    w_router = nrm((n_moe, D, N_EXPERTS), D ** -0.5)
    w1_moe = nrm((n_moe, N_EXPERTS, D, FFN_DIM), D ** -0.5)
    w3_moe = nrm((n_moe, N_EXPERTS, D, FFN_DIM), D ** -0.5)
    w2_moe = nrm((n_moe, N_EXPERTS, FFN_DIM, D), FFN_DIM ** -0.5)
    return {'x': x, 'c': c, 'positions': positions, 'w_ada': w_ada, 'b_ada': b_ada,
            'norm_mix': norm_mix, 'norm_ffn': norm_ffn, 'w_in': w_in, 'conv_w': conv_w,
            'a_log': a_log, 'dt_bias': dt_bias, 'dn_norm': dn_norm, 'cmp_pos': cmp_pos,
            'w_cmp1': w_cmp1, 'w_cmp2': w_cmp2, 'q_norm': q_norm, 'k_norm': k_norm,
            'w_oa': w_oa, 'w_ob': w_ob, 'w_out': w_out, 'w1_dense': w1_dense,
            'w3_dense': w3_dense, 'w2_dense': w2_dense, 'w_router': w_router,
            'w1_moe': w1_moe, 'w3_moe': w3_moe, 'w2_moe': w2_moe}

def second_block(x, c, positions, w_ada, b_ada, norm_mix, norm_ffn, w_in, conv_w, a_log, dt_bias,
              dn_norm, cmp_pos, w_cmp1, w_cmp2, q_norm, k_norm, w_oa, w_ob, w_out,
              w1_dense, w3_dense, w2_dense, w_router, w1_moe, w3_moe, w2_moe):
    b_, s_, _ = x.shape
    gq, dh = NSA_GROUPS, NSA_DH
    cos, sin = rope_angles(positions)
    n_cmp = (s_ - CMP_LEN) // CMP_STRIDE + 1
    cmp_end = jnp.arange(n_cmp) * CMP_STRIDE + CMP_LEN - 1
    cos_c, sin_c = rope_angles(positions[:, cmp_end])
    split_at = [int(i) for i in np.cumsum(SPLIT_SIZES)[:-1]]
    c_act = jax.nn.silu(c)
    for l in range(DEPTH):
        mod = c_act @ w_ada[l] + b_ada[l]
        sh_m, sc_m, g_m, sh_f, sc_f, g_f = [m[:, None, :] for m in jnp.split(mod, 6, -1)]
        h = rms_norm(x, norm_mix[l]) * (1.0 + sc_m) + sh_m
        proj = h @ w_in[l]
        (dn_qkv, dn_z, dn_b, dn_a, n_q, c_k, c_v, s_k, s_v, w_k, w_v, n_g, m_g) = \
            jnp.split(proj, split_at, -1)
        qkv = causal_conv_silu(dn_qkv, conv_w[l])
        d_q, d_k, d_v = jnp.split(qkv, [DN_HEADS * DN_DK, 2 * DN_HEADS * DN_DK], -1)
        d_q = l2_norm(d_q.reshape(b_, s_, DN_HEADS, DN_DK)) * (DN_DK ** -0.5)
        d_k = l2_norm(d_k.reshape(b_, s_, DN_HEADS, DN_DK))
        d_v = d_v.reshape(b_, s_, DN_HEADS, DN_DV)
        beta = jax.nn.sigmoid(dn_b)
        g_log = -jnp.exp(a_log[l].astype(jnp.float32)) * jax.nn.softplus(
            dn_a.astype(jnp.float32) + dt_bias[l].astype(jnp.float32))
        o_a = gated_delta_rule(d_q, d_k, d_v, beta, g_log)
        o_a = rms_norm(o_a, dn_norm[l]) * jax.nn.silu(dn_z.reshape(b_, s_, DN_HEADS, DN_DV))
        y_a = o_a.reshape(b_, s_, DN_HEADS * DN_DV) @ w_oa[l]
        n_q = apply_rope(rms_norm(n_q.reshape(b_, s_, NSA_HEADS, dh), q_norm[l]), cos, sin)
        k_c = compress_blocks(c_k.reshape(b_, s_, gq, dh), cmp_pos[l, 0], w_cmp1[l, 0], w_cmp2[l, 0])
        k_c = apply_rope(rms_norm(k_c, k_norm[l, 0]), cos_c, sin_c)
        v_c = compress_blocks(c_v.reshape(b_, s_, gq, dh), cmp_pos[l, 1], w_cmp1[l, 1], w_cmp2[l, 1])
        s_k = apply_rope(rms_norm(s_k.reshape(b_, s_, gq, dh), k_norm[l, 1]), cos, sin)
        w_k = apply_rope(rms_norm(w_k.reshape(b_, s_, gq, dh), k_norm[l, 2]), cos, sin)
        gates = jax.nn.sigmoid(n_g.reshape(b_, s_, NSA_HEADS, 3))
        o_b = nsa_core(n_q, k_c, v_c, s_k, s_v.reshape(b_, s_, gq, dh),
                       w_k, w_v.reshape(b_, s_, gq, dh), gates)
        y_b = o_b @ w_ob[l]
        gate_a, gate_b = jnp.split(jax.nn.sigmoid(m_g), 2, -1)
        y = (gate_a * y_a + gate_b * y_b) @ w_out[l]
        x = x + g_m * y
        h = rms_norm(x, norm_ffn[l]) * (1.0 + sc_f) + sh_f
        if l % 2 == 0:
            f = swiglu(h, w1_dense[l // 2], w3_dense[l // 2], w2_dense[l // 2])
        else:
            f = moe_ffn(h, w_router[l // 2], w1_moe[l // 2], w3_moe[l // 2], w2_moe[l // 2])
        x = x + g_f * f
    return x


def setup_inputs(seed=0):
    out = dict(first_inputs(seed))
    for name, value in second_inputs(seed + 1).items():
        if name != "x":
            out[name + "_2"] = value
    return out


def reference(
    x, w_in_ab, gla_gate_up, gla_gate_bias, gla_norm, w_out_ab, w_in_c, hgrn_lower_bounds,
    hgrn_norm, w_out_c, rel_bias, ln_gain, ln_bias, c_2, positions_2, w_ada_2, b_ada_2,
    norm_mix_2, norm_ffn_2, w_in_2, conv_w_2, a_log_2, dt_bias_2, dn_norm_2, cmp_pos_2,
    w_cmp1_2, w_cmp2_2, q_norm_2, k_norm_2, w_oa_2, w_ob_2, w_out_2, w1_dense_2, w3_dense_2,
    w2_dense_2, w_router_2, w1_moe_2, w3_moe_2, w2_moe_2,
):
    x = first_block(
        x, w_in_ab, gla_gate_up, gla_gate_bias, gla_norm, w_out_ab, w_in_c, hgrn_lower_bounds,
        hgrn_norm, w_out_c, rel_bias, ln_gain, ln_bias,
    )
    return second_block(
        x, c_2, positions_2, w_ada_2, b_ada_2, norm_mix_2, norm_ffn_2, w_in_2, conv_w_2,
        a_log_2, dt_bias_2, dn_norm_2, cmp_pos_2, w_cmp1_2, w_cmp2_2, q_norm_2, k_norm_2,
        w_oa_2, w_ob_2, w_out_2, w1_dense_2, w3_dense_2, w2_dense_2, w_router_2, w1_moe_2,
        w3_moe_2, w2_moe_2,
    )


_drawn_inputs = setup_inputs


def setup_inputs(seed=0):
    import zlib

    import numpy as np

    out = dict(_drawn_inputs(seed))
    spreads = {}
    factors = {'gla_gate_up': 2.699,
     'gla_gate_bias': 4.956,
     'gla_norm': 7.85,
     'hgrn_lower_bounds': 8.0,
     'hgrn_norm': 8.0,
     'rel_bias': 8.0,
     'b_ada_2': 3.366,
     'norm_mix_2': 2.7,
     'dn_norm_2': 6.5,
     'cmp_pos_2': 7.676,
     'q_norm_2': 8.0,
     'k_norm_2': 8.0,
     'norm_ffn_2': 4.588}
    for name, (base, spread) in spreads.items():
        noise = np.random.default_rng([zlib.crc32(name.encode()), seed]).standard_normal(out[name].shape)
        drawn = base * np.exp(spread * noise) if base else spread * noise
        out[name] = jnp.asarray(drawn.astype(out[name].dtype))
    for name, factor in factors.items():
        out[name] = (out[name] * factor).astype(out[name].dtype)
    return out
```

```python
from contextlib import ExitStack

import numpy as np

import concourse.bass as bass
from concourse import mybir

F32 = mybir.dt.float32
I32 = mybir.dt.int32
U8 = mybir.dt.uint8
U32 = mybir.dt.uint32
ALU = mybir.AluOpType
ACT = mybir.ActivationFunctionType
AX = mybir.AxisListType

P = 128
S = 256
NT = S // P
D = 1024
KC = D // P
DEPTH = 2

A_HEADS, A_DIM = 8, 64
B_HEADS, B_VAL = 4, 256
C_HEADS, C_VAL = 12, 128
CHUNK = 32
NCH = S // CHUNK
MIX = 1536
MC = MIX // P
GLA_NORM = 16.0
ALPHA = (2 * DEPTH) ** 0.25
LN_EPS = 1e-5
EPS = 1e-6
NEG = -1e30
REL_BUCKETS = 32
REL_MAX = 1024
DIST = 2 * S

DN_H, DN_D, DN_C = 8, 64, 64
DN_QKV = DN_H * 3 * DN_D
CONV_W = 4
NSA_H, NSA_G, NSA_D = 8, 2, 64
CMP_LEN, CMP_STRIDE = 32, 16
N_CMP = (S - CMP_LEN) // CMP_STRIDE + 1
CW = 32
ROPE_THETA = 10000.0
HALF = NSA_D // 2
FFN = 3584
N_EXP = 8
GROUPS = FFN // 512

SLOTS = 7
MIX_SLOTS = 4
SLOT = 4096


def t5_bucket(rel):
    half = REL_BUCKETS // 2
    exact = half // 2
    n = np.abs(rel)
    large = exact + (np.log(np.maximum(n, 1) / exact) / np.log(REL_MAX / exact) * (half - exact)).astype(np.int32)
    large = np.minimum(large, half - 1)
    return np.where(rel > 0, half, 0) + np.where(n < exact, n, large)


C_ID, C_SCAN, C_CAUSAL, C_FREQ, C_CMPM, C_CMPB, C_TRI, C_ROW4, C_EXP, C_BLK = 0, 128, 640, 896, 928, 960, 992, 1120, 1136, 1144
C_FLOATS = C_BLK + P
M_GLA, M_LE, M_LT, M_LEVEL = 0, 512, 640, 768
LEVELS = (1, 2, 4, 8, 16, 32)
M_BYTES = M_LEVEL + P * len(LEVELS)


def constants():
    f = np.zeros((P, C_FLOATS), np.float32)
    m = np.zeros((P, M_BYTES), np.float32)
    p, c = np.arange(P)[:, None], np.arange(P)[None, :]
    t = np.arange(S)
    f[:, C_ID:C_ID + P] = np.eye(P)
    f[:, C_SCAN:C_SCAN + S] = t % CHUNK != 0
    f[:, C_SCAN + S:C_SCAN + 2 * S] = t % CHUNK != CHUNK - 1
    f[:, C_CAUSAL + P:C_CAUSAL + 2 * P] = np.where(c <= p, 0.0, NEG)
    f[:, C_FREQ:C_FREQ + HALF] = 1.0 / (ROPE_THETA ** (np.arange(0, NSA_D, 2, dtype=np.float32) / NSA_D))
    for tile in range(NT):
        q, w = tile * P + p, np.arange(16)[None, :]
        seen = (w * CMP_STRIDE + CMP_LEN - 1 <= q) & (w < N_CMP)
        f[:, C_CMPM + 16 * tile:C_CMPM + 16 * tile + 16] = seen
        f[:, C_CMPB + 16 * tile:C_CMPB + 16 * tile + 16] = np.where(seen, 0.0, NEG)
    f[:, C_TRI:C_TRI + P] = (p <= c) & (p // DN_C == c // DN_C)
    f[:, C_BLK:C_BLK + P] = p // DN_C == c // DN_C
    for j in range(4):
        f[:, C_ROW4 + j] = p[:, 0] // CHUNK == j
    f[:, C_EXP:C_EXP + N_EXP] = np.arange(N_EXP)
    same = p // CHUNK == c // CHUNK
    for tile in range(NT):
        m[:, M_GLA + tile * P:M_GLA + tile * P + P] = same & (p <= c)
        m[:, M_GLA + S + tile * P:M_GLA + S + tile * P + P] = same & (p > c)
    block = p // DN_C == c // DN_C
    m[:, M_LE:M_LE + P] = block & (p <= c)
    m[:, M_LT:M_LT + P] = block & (p < c)
    for n, s in enumerate(LEVELS):
        m[:, M_LEVEL + n * P:M_LEVEL + (n + 1) * P] = (p // (2 * s) == c // (2 * s)) & ((c // s) % 2 == 1) & ((p // s) % 2 == 0)
    d = S - np.arange(DIST)
    hot = (t5_bucket(d)[None, :] == np.arange(REL_BUCKETS)[:, None]).astype(np.float32)
    hits = (np.abs(d) <= 64).astype(np.int32) + (d % 4 == 0) + (d % 16 == 0)
    times = np.where(hits > 0, np.log(np.maximum(hits, 1)), NEG).astype(np.float32)
    return f, m, hot, np.repeat(times[None, :], A_HEADS, 0)


INS = ["x", "w_in_ab", "gla_gate_up", "gla_gate_bias", "gla_norm", "w_out_ab", "w_in_c", "hgrn_lower_bounds",
       "hgrn_norm", "w_out_c", "rel_bias", "ln_gain", "ln_bias", "c_2", "positions_2", "w_ada_2", "b_ada_2",
       "norm_mix_2", "norm_ffn_2", "w_in_2", "conv_w_2", "a_log_2", "dt_bias_2", "dn_norm_2", "cmp_pos_2",
       "w_cmp1_2", "w_cmp2_2", "q_norm_2", "k_norm_2", "w_oa_2", "w_ob_2", "w_out_2", "w1_dense_2", "w3_dense_2",
       "w2_dense_2", "w_router_2", "w1_moe_2", "w3_moe_2", "w2_moe_2"]


def network(nc, I, const_f, const_m, const_hot, const_times, out, upto=9):
    ctx = ExitStack()
    with ctx:
        def sb(name, shape, dt=F32):
            return ctx.enter_context(nc.sbuf_tensor(name, shape, dt))

        sems = {}

        def sem(name):
            if name not in sems:
                sems[name] = ctx.enter_context(nc.semaphore(name))
            return sems[name]

        X = sb("X", [P, NT, D])
        HT = sb("HT", [P, KC, S])
        RING = sb("RING", [P, SLOTS * SLOT])
        PROJ = sb("PROJ", [P, 5120])
        MODB = sb("MODB", [P, 3 * D])
        ROW = sb("ROW", [P, 2 * D])
        CF = sb("CF", [P, C_FLOATS])
        CM = sb("CM", [P, M_BYTES], U8)
        small = sb("small", [P, 1664])
        norm_rows = sb("norm_rows", [P, DEPTH, 5, 64])
        cmp_prm = sb("cmp_prm", [NSA_D, DEPTH, 192])
        ab_w = sb("ab_w", [P, 2, KC, 16])
        router_w = sb("router_w", [P, KC, N_EXP])
        PSA = ctx.enter_context(nc.psum_tensor("PSA", [P, 2, 1024], F32))
        PSB = ctx.enter_context(nc.psum_tensor("PSB", [P, 4, 512], F32))
        SCR = RING[:, MIX_SLOTS * SLOT:SLOTS * SLOT]
        SM = SCR[:, 9728:10240].rearrange("p (d t) -> p d t", d=2)
        lrT = SCR[0:16, 10240:10752].rearrange("p (d t) -> p d t", d=2)
        up_w = SCR[0:16, 10752:11776].rearrange("p (d f) -> p d f", d=2)
        squares = SCR[:, 11776:12032]
        lr_w = SCR[:, 12032:12288].rearrange("p (k n) -> p k n", k=KC)
        bias_dram = nc.dram_tensor("bias_by_distance", [A_HEADS, DIST], F32, kind="Internal")

        ident = CF[:, C_ID:C_ID + P]
        at = [0]

        def keep(n):
            at[0] += n
            assert at[0] <= 1664
            return small[:, at[0] - n:at[0]]

        stat = keep(64)
        stats6 = keep(24)
        gate_bias = keep(8)
        lower = keep(24).rearrange("p (l h) -> p l h", l=2)
        lb = keep(12)
        omlb = keep(12)

        items = []

        def item(src, slot=None):
            n = len(items)
            mixer = [i for i in items if i[1] < MIX_SLOTS]
            if slot is None:
                slot = (mixer[-1][1] + 1) % MIX_SLOTS if mixer else 0
            before = [i for i, x in enumerate(items) if x[1] == slot]
            items.append((src, slot, before[-1] if before else None, len(before)))
            return n

        def columns(w, c0, n, slot=None):
            return item(w[:, c0:c0 + n].rearrange("(k p) n -> p k n", p=P), slot)

        def rows(w, r0, slot=None):
            return item(w[r0:r0 + 512, :].rearrange("(k p) n -> p k n", p=P), slot)

        def view(n):
            src, slot, _, _ = items[n]
            p, a, b = src.shape
            return RING[0:p, slot * SLOT:slot * SLOT + a * b].rearrange("p (a b) -> p a b", a=a)

        w_ab, w_c = I["w_in_ab"][0], I["w_in_c"][0]
        AB_Q, AB_K, AB_V = [columns(w_ab, 512 * j, 512) for j in range(3)]
        AB_GLA = [columns(w_ab, 1536 + 512 * j, 512) for j in range(4)]
        AB_GATE = [columns(w_ab, 3616 + 512 * j, 512) for j in range(3)]
        AB_OUT = [rows(I["w_out_ab"][0], 512 * j) for j in range(3)]
        C_GROUP = [[columns(w_c, 1536 * j + 512 * g, 512) for j in range(5)] for g in range(3)]
        C_OUT = [rows(I["w_out_c"][0], 512 * j) for j in range(3)]

        L2 = []
        for l in range(DEPTH):
            w_in, ada = I["w_in_2"][l], I["w_ada_2"][l]
            L2.append(dict(
                ada=[columns(ada, 512 * j, 512) for j in range(6)],
                qkv=[columns(w_in, 512 * j, 512) for j in range(3)],
                z=columns(w_in, 1536, 512),
                nq=columns(w_in, 2064, 512),
                kv=[columns(w_in, 2576, 512), columns(w_in, 3088, 280)],
                cmp=item(I["w_cmp1_2"][l].rearrange("k (l d) e -> d (k l) e", d=NSA_D)),
                mg=[columns(w_in, 3368 + 512 * j, 512) for j in range(4)],
                oa=rows(I["w_oa_2"][l], 0),
                ob=rows(I["w_ob_2"][l], 0),
                out=[rows(I["w_out_2"][l], 512 * j) for j in range(2)],
                ada_f=[columns(ada, 512 * j, 512) for j in range(6, 12)],
            ))
            if l == 0:
                w1, w3, w2 = I["w1_dense_2"][0], I["w3_dense_2"][0], I["w2_dense_2"][0]
            else:
                w1, w3, w2 = I["w1_moe_2"][0, 0], I["w3_moe_2"][0, 0], I["w2_moe_2"][0, 0]
            L2[l]["ffn"] = [(columns(w1, 512 * g, 512, (3 * g) % SLOTS), columns(w3, 512 * g, 512, (3 * g + 1) % SLOTS),
                             rows(w2, 512 * g, (3 * g + 2) % SLOTS)) for g in range(GROUPS)]
        PER_EXPERT = 3 * GROUPS

        row_list = []

        def row(src):
            row_list.append(src)
            return len(row_list) - 1

        R_GLA = row(I["gla_norm"][0:1, :])
        R_LN = [[row(I["ln_gain"][0:1, :]), row(I["ln_bias"][0:1, :])]]
        R_HGRN = [row(I["hgrn_norm"][0:1, 512 * g:512 * g + 512]) for g in range(3)]
        R_LN.append([row(I["ln_gain"][1:2, :]), row(I["ln_bias"][1:2, :])])

        R_MIX, R_FFN = [], []
        for l in range(DEPTH):
            b_ada = I["b_ada_2"]
            R_MIX.append([row(b_ada[l:l + 1, 0:D]), row(b_ada[l:l + 1, D:2 * D]), row(I["norm_mix_2"][l:l + 1, :]),
                          row(b_ada[l:l + 1, 2 * D:3 * D])])
            R_FFN.append([row(b_ada[l:l + 1, 3 * D:4 * D]), row(b_ada[l:l + 1, 4 * D:5 * D]),
                          row(I["norm_ffn_2"][l:l + 1, :]), row(b_ada[l:l + 1, 5 * D:6 * D])])

        def row_at(n):
            w = row_list[n].shape[1]
            return ROW[:, (n % 2) * D:(n % 2) * D + w]

        phases = {}

        def phase(eng, name):
            k = phases.setdefault(eng, 0) + 1
            phases[eng] = k
            eng.drain().then_inc(sem("phase"), 1)
            eng.wait_ge(sem("phase"), 3 * k)

        def wait_item(pe, n):
            pe.wait_ge(sem(f"slot_loaded{items[n][1]}"), 16 * (items[n][3] + 1))

        pairs = {}

        def pair_of(eng):
            k = pairs.get(eng, 0)
            pairs[eng] = k + 1
            return k

        def project_tokens(pe, n, cols=512):
            k = pair_of("pe")
            wait_item(pe, n)
            if k >= 2:
                pe.wait_ge(sem("pair_taken"), k - 1)
            W = view(n)
            for t in range(NT):
                for c in range(KC):
                    mm = pe.matmul(PSA[:, k % 2, 512 * t:512 * t + cols], HT[:, c, P * t:P * t + P], W[:, c, 0:cols],
                                   start=(c == 0), stop=(c == KC - 1))
            mm.then_inc(sem("item_used"), 1)

        def project_features(pe, n):
            k = pair_of("pe")
            wait_item(pe, n)
            if k >= 2:
                pe.wait_ge(sem("pair_taken"), k - 1)
            W = view(n)
            for j in range(4):
                for c in range(KC):
                    mm = pe.matmul(PSA[:, k % 2, S * j:S * j + S], W[:, c, P * j:P * j + P], HT[:, c, :],
                                   start=(c == 0), stop=(c == KC - 1))
            mm.then_inc(sem("item_used"), 1)

        def take(act, n, dst, func=ACT.Copy, scale=1.0, cols=512, tokens=True):
            k = pair_of("act")
            act.wait_ge(sem("item_used"), n + 1)
            src = PSA[:, k % 2, :].rearrange("p (a b) -> p a b", a=2 if tokens else 4)[:, :, 0:cols]
            act.activation(dst, src, func, scale=scale).then_inc(sem("pair_taken"), 1)

        def skip_pairs(eng, n):
            pairs[eng] = pairs.get(eng, 0) + n

        turns = {}

        def pe_turn(pe, src, n_chunks, name):
            for g in range(n_chunks // 2):
                k = turns.setdefault("pe", 0)
                turns["pe"] = k + 1
                if k >= 4:
                    pe.wait_ge(sem("turned_taken"), k - 3)
                for j in range(2):
                    for t in range(NT):
                        mm = pe.transpose(PSB[:, k % 4, S * j + P * t:S * j + P * t + P],
                                          src[:, t, P * (2 * g + j):P * (2 * g + j) + P], ident)
                mm.then_inc(sem("turned"), 1)

        def take_turned(eng, dst, n_chunks):
            for g in range(n_chunks // 2):
                k = turns.setdefault("take", 0)
                turns["take"] = k + 1
                eng.wait_ge(sem("turned"), k + 1)
                eng.tensor_copy(dst[:, 2 * g:2 * g + 2, :],
                                PSB[:, k % 4, :].rearrange("p (a b) -> p a b", a=2)).then_inc(sem("turned_taken"), 1)

        ATT = SCR[:, 3072:3072 + 2048].rearrange("p (b a) -> p b a", b=4)
        s_buf = [ATT[:, b, :].rearrange("p (t k) -> p t k", t=NT) for b in range(2)]
        p_buf = [ATT[:, 2 + b, :].rearrange("p (c q) -> p c q", c=NT) for b in range(2)]
        att_max, att_sum, att_rs = keep(16), keep(16), keep(16)
        amx = [att_max[:, 2 * b:2 * b + 2] for b in range(8)]

        def pe_attention(pe, base, heads, qT, kT, v, out_at, causal, fresh=True):
            def scores(h):
                i = base + h
                if h >= 2 or not fresh:
                    pe.wait_ge(sem("att_scored"), i - 1)
                q = qT(h)
                for t in range(NT):
                    w = P * (t + 1) if causal else S
                    mm = pe.matmul(PSB[:, i % 2, S * t:S * t + w], q[:, P * t:P * t + P], kT(h)[:, 0:w],
                                   start=True, stop=True)
                mm.then_inc(sem("att_scores"), 1)

            scores(0)
            for h in range(heads):
                i = base + h
                if h + 1 < heads:
                    scores(h + 1)
                pe.wait_ge(sem("att_probs"), i + 1)
                if h >= 2 or not fresh:
                    pe.wait_ge(sem("att_turned_taken"), i - 1)
                for t in range(NT):
                    for c in range(t + 1 if causal else NT):
                        mm = pe.transpose(PSB[:, 2 + i % 2, S * c + P * t:S * c + P * t + P],
                                          s_buf[i % 2][:, t, P * c:P * c + P], ident)
                mm.then_inc(sem("att_turned"), 1)
                pe.wait_ge(sem("att_turned_taken"), i + 1)
                for t in range(NT):
                    n = t + 1 if causal else NT
                    for c in range(n):
                        mm = pe.matmul(out_at(t, h), p_buf[i % 2][:, c, P * t:P * t + P], v(c, h),
                                       start=(c == 0), stop=(c == n - 1))
                mm.then_inc(sem("att_values"), 1)

        def act_attention(act, base, heads, causal, sums, fresh=True):
            for h in range(heads):
                i = base + h
                act.wait_ge(sem("att_scored"), i + 1)
                for t in range(NT):
                    w = P * (t + 1) if causal else S
                    e = act.activation(s_buf[i % 2][:, t, 0:w], s_buf[i % 2][:, t, 0:w], ACT.Exp,
                                       bias=amx[i % 8][:, t:t + 1], accum_out=sums[:, t * heads + h:t * heads + h + 1])
                e.then_inc(sem("att_probs"), 1)
                act.wait_ge(sem("att_turned"), i + 1)
                if h >= 2 or not fresh:
                    act.wait_ge(sem("att_values"), i - 1)
                if causal:
                    act.activation(p_buf[i % 2][:, 0, :], PSB[:, 2 + i % 2, 0:S], ACT.Copy)
                    e = act.activation(p_buf[i % 2][:, 1, P:S], PSB[:, 2 + i % 2, S + P:2 * S], ACT.Copy)
                else:
                    e = act.activation(p_buf[i % 2], PSB[:, 2 + i % 2, :].rearrange("p (c q) -> p c q", c=NT), ACT.Copy)
                e.then_inc(sem("att_turned_taken"), 1)

        def dve_attention(dve, base, heads, causal, bias, fresh=True):
            for h in range(heads):
                i = base + h
                dve.wait_ge(sem("att_scores"), i + 1)
                if h >= 2 or not fresh:
                    dve.wait_ge(sem("att_turned"), i - 1)
                    dve.wait_ge(sem("att_turned_taken"), i - 1)
                for t in range(NT):
                    w = P * (t + 1) if causal else S
                    dve.scalar_tensor_tensor(s_buf[i % 2][:, t, 0:w], PSB[:, i % 2, S * t:S * t + w], A_DIM ** -0.5,
                                             bias(t, h, w), ALU.mult, ALU.add)
                dve.drain()
                for t in range(NT):
                    w = P * (t + 1) if causal else S
                    e = dve.tensor_reduce(amx[i % 8][:, t:t + 1], s_buf[i % 2][:, t, 0:w], AX.X, ALU.max, negate=True)
                e.then_inc(sem("att_scored"), 1)

        gla_at = [0]

        def scratch(n):
            gla_at[0] += n
            assert gla_at[0] <= (SLOTS - MIX_SLOTS) * SLOT
            return SCR[:, gla_at[0] - n:gla_at[0]]

        G_B = [scratch(S) for _ in range(2)]
        G_D = [scratch(2 * S).rearrange("p (a t) -> p a t", a=2) for _ in range(2)]
        G_E = [scratch(4 * S).rearrange("p (a t) -> p a t", a=4) for _ in range(2)]
        G_Q = [scratch(2 * S).rearrange("p (a t) -> p a t", a=2) for _ in range(2)]
        G_K = [scratch(2 * S).rearrange("p (a t) -> p a t", a=2) for _ in range(2)]
        G_KT = [scratch(S).rearrange("p (t f) -> p t f", t=NT) for _ in range(2)]
        G_ST = [scratch(7 * 256) for _ in range(2)]
        G_EB = [keep(NCH) for _ in range(2)]
        VM = MODB[:, 0:2048]
        ms = keep(NT * 12)
        ref_at = (CHUNK // 2 - 1, CHUNK // 2)
        last_at = (CHUNK - 1, 0)

        def chunked(a):
            return a.rearrange("p (c t) -> p c t", t=CHUNK)

        def dve_decay(dve, j, d, g):
            if j >= 2:
                dve.wait_ge(sem("gla_exp"), j - 1)
            m = CF[:, C_SCAN + d * S:C_SCAN + d * S + S]
            if d == 0:
                dve.tensor_tensor_scan(G_B[d], m, g, 0.0, ALU.mult, ALU.add)
            else:
                dve.tensor_tensor_scan(G_B[d][:, ::-1], m[:, ::-1], g[:, ::-1], 0.0, ALU.mult, ALU.add)
            dve.drain()
            b = chunked(G_B[d])
            for k, where in enumerate((ref_at[d], last_at[d])):
                e = dve.tensor_tensor(chunked(G_D[d][:, k, :]), b,
                                      b[:, :, where:where + 1].broadcast_to([P, NCH, CHUNK]), ALU.subtract)
            e.then_inc(sem("gla_decay"), 1)

        def act_exp(act, j, d, scale):
            act.wait_ge(sem("gla_decay"), j + 1)
            if j >= 2:
                act.wait_ge(sem("gla_scaled"), j - 1)
            act.activation(G_E[d][:, 0, :], G_D[d][:, 0, :], ACT.Exp, scale=scale)
            act.activation(G_E[d][:, 1, :], G_B[d], ACT.Exp, scale=scale)
            act.activation(G_E[d][:, 2:4, :], G_D[d], ACT.Exp, scale=-scale).then_inc(sem("gla_exp"), 1)

        def dve_scale(dve, j, d, q, k, q_scale):
            dve.wait_ge(sem("gla_exp"), j + 1)
            if j >= 2:
                dve.wait_ge(sem("gla_done"), j - 1)
            dve.scalar_tensor_tensor(G_Q[d], G_E[d][:, 0:2, :], q_scale, q.unsqueeze(1).broadcast_to([P, 2, S]),
                                     ALU.mult, ALU.mult)
            dve.tensor_copy(G_EB[d], chunked(G_E[d][:, 1, :])[:, :, last_at[d]])
            dve.tensor_tensor(G_K[d], G_E[d][:, 2:4, :], k.unsqueeze(1).broadcast_to([P, 2, S]), ALU.mult)\
                .then_inc(sem("gla_scaled"), 1)

        def dve_mask(dve, j, d):
            dve.wait_ge(sem("gla_scores"), j + 1)
            dve.copy_predicated(SM[:, d, :], CM[:, M_GLA + d * S:M_GLA + d * S + S], PSB[:, 3, 0:S])\
                .then_inc(sem("gla_masked"), 1)

        def dve_states(dve, j, d, V):
            per = 1024 // V
            for s in range(NCH - 1):
                c = s if d == 0 else NCH - 1 - s
                u = (NCH // per) * j + s // per
                if s % per == 0:
                    dve.wait_ge(sem("gla_updates"), u + 1 + (2 * B_HEADS if per == NCH else 0))
                U = PSA[:, (u if per < NCH else d) % 2, V * (c % per):V * (c % per) + V]
                new = G_ST[d][:, V * s:V * s + V]
                if s == 0:
                    e = dve.tensor_copy(new, U)
                else:
                    dve.drain()
                    e = dve.scalar_tensor_tensor(new, G_ST[d][:, V * (s - 1):V * s], G_EB[d][:, c:c + 1], U,
                                                 ALU.mult, ALU.add)
                e.then_inc(sem("gla_state"), 1)

        def pe_gla(pe, n, V, v):
            per = 1024 // V
            O = PSB[:, n % 2, 0:2 * V].rearrange("p (t v) -> p t v", t=NT)
            for d in range(2):
                j = 2 * n + d
                pe.wait_ge(sem("gla_scaled"), j + 1)
                for t in range(NT):
                    pe.transpose(PSB[:, 2, P * t:P * t + P], G_K[d][:, 1, P * t:P * t + P], ident)
                for t in range(NT):
                    mm = pe.matmul(PSB[:, 3, P * t:P * t + P], G_K[d][:, 0, P * t:P * t + P],
                                   G_Q[d][:, 0, P * t:P * t + P], start=True, stop=True)
                mm.then_inc(sem("gla_scores"), 1)
                pe.wait_ge(sem("gla_masked"), j + 1)
                if d == 0 and n >= 2:
                    pe.wait_ge(sem("gla_out_taken"), n - 1)
                for t in range(NT):
                    pe.matmul(O[:, t, :], SM[:, d, P * t:P * t + P], v(t), start=(d == 0 and t == 0), stop=False,
                              skip_group_check=True)
                pe.wait_ge(sem("gla_turned_taken"), j + 1)
                pe.wait_ge(sem("gla_spread"), n + 1)
                for half in range(NCH // per):
                    u = (NCH // per) * j + half
                    if per == NCH:
                        if j >= 2:
                            pe.wait_ge(sem("gla_state"), 7 * (j - 1))
                        for t in range(NT):
                            mm = pe.matmul(PSA[:, d, 512 * t:512 * t + 512], G_KT[d][:, t, :],
                                           VM[:, 512 * t:512 * t + 512], start=True, stop=True)
                    else:
                        t = half if d == 0 else 1 - half
                        if u >= 2:
                            pe.wait_ge(sem("gla_state"), 7 * (j - 1) + (4 if half == 0 else 7))
                        for k in range(2):
                            mm = pe.matmul(PSA[:, u % 2, 512 * k:512 * k + 512], G_KT[d][:, t, :],
                                           VM[:, 1024 * t + 512 * k:1024 * t + 512 * k + 512], start=True, stop=True)
                    mm.then_inc(sem("gla_updates"), 1)
                    if per < NCH:
                        inter(pe, n, d, V, O, range(half * 3, half * 3 + 3) if half == 0 else range(3, 7), d == 1 and half == 1)
                if per == NCH:
                    inter(pe, n, d, V, O, range(0, 7), d == 1)

        def inter(pe, n, d, V, O, steps, last):
            j = 2 * n + d
            for s in steps:
                c = s + 1 if d == 0 else NCH - 2 - s
                pe.wait_ge(sem("gla_state"), 7 * j + s + 1)
                r = CHUNK * (c % 4)
                mm = pe.matmul(O[r:r + CHUNK, c // 4, :], G_Q[d][:, 1, CHUNK * c:CHUNK * c + CHUNK],
                               G_ST[d][:, V * s:V * s + V], start=False, stop=True, skip_group_check=True)
            if steps[-1] == 6:
                mm.then_inc(sem("gla_done"), 1)

        def act_gla(act, n0, heads, V, scale, y):
            total = 2 * (n0 + heads)
            act_exp(act, 2 * n0, 0, scale)
            act_exp(act, 2 * n0 + 1, 1, scale)
            for n in range(n0, n0 + heads):
                for d in range(2):
                    j = 2 * n + d
                    act.wait_ge(sem("gla_scores"), j + 1)
                    act.activation(G_KT[d], PSB[:, 2, 0:S].rearrange("p (t f) -> p t f", t=NT), ACT.Copy)\
                        .then_inc(sem("gla_turned_taken"), 1)
                    if j + 2 < total:
                        act_exp(act, j + 2, d, scale)
                act.wait_ge(sem("gla_out_taken"), n + 1)
                for t in range(NT):
                    e = act.activation(squares[:, 0:V], y(n - n0)[:, t, :], ACT.Square,
                                       accum_out=ms[:, t * heads + n - n0:t * heads + n - n0 + 1])
                    act.drain()
                act.drain().then_inc(sem("gla_squared"), 1)

        def dve_gla(dve, n0, heads, V, q, k, g, v, y, q_scale):
            total = heads * 2

            def decay(i):
                dve_decay(dve, 2 * n0 + i, i % 2, g(i % 2, i // 2))

            decay(0)
            decay(1)
            for h in range(heads):
                n = n0 + h
                if h >= 1:
                    dve.wait_ge(sem("gla_done"), 2 * n)
                vm = VM[:, 0:NCH * V].rearrange("p (t c v) -> p t c v", t=NT, c=4)
                for t in range(NT):
                    for c in range(4):
                        e = dve.tensor_scalar(vm[:, t, c, :], v(t, h), CF[:, C_ROW4 + c:C_ROW4 + c + 1], None, ALU.mult)
                e.then_inc(sem("gla_spread"), 1)
                for d in range(2):
                    j = 2 * n + d
                    dve_scale(dve, j, d, q(h), k(d, h), q_scale)
                    dve_mask(dve, j, d)
                    if 2 * h + d + 2 < total:
                        decay(2 * h + d + 2)
                    dve_states(dve, j, d, V)
                dve.wait_ge(sem("gla_done"), 2 * n + 2)
                dve.tensor_copy(y(h), PSB[:, n % 2, 0:2 * V].rearrange("p (t v) -> p t v", t=NT))\
                    .then_inc(sem("gla_out_taken"), 1)

        counts = {}

        def dve_rs(dve, a, scale, eps):
            k = counts.get("dve_rs", 0) + 1
            counts["dve_rs"] = k
            dve.tensor_scalar(a, a, scale, eps, ALU.mult, ALU.add).then_inc(sem("rs_ready"), 1)
            dve.wait_ge(sem("rs_done"), k)

        def act_rs(act, a):
            k = counts.get("act_rs", 0) + 1
            counts["act_rs"] = k
            act.wait_ge(sem("rs_ready"), k)
            act.activation(a, a, ACT.Ln)
            act.drain()
            act.activation(a, a, ACT.Exp, scale=-0.5).then_inc(sem("rs_done"), 1)

        def pe_out(pe, its, YT):
            for n, it in enumerate(its):
                wait_item(pe, it)
                W = view(it)
                for t in range(NT):
                    for hf in range(2):
                        for c in range(4):
                            mm = pe.matmul(PSA[:, t, 512 * hf:512 * hf + 512], YT[:, 4 * n + c, P * t:P * t + P],
                                           W[:, c, 512 * hf:512 * hf + 512], start=(n == 0 and c == 0),
                                           stop=(n == len(its) - 1 and c == 3))
                mm.then_inc(sem("item_used"), 1)

        def dve_layer_norm(dve, its, layer):
            dve.wait_ge(sem("item_used"), its[-1] + 1)
            for t in range(NT):
                dve.scalar_tensor_tensor(X[:, t, :], X[:, t, :], ALPHA, PSA[:, t, :], ALU.mult, ALU.add)
            dve.drain()
            st = stats6.rearrange("p (t a) -> p t a", t=NT)
            for t in range(NT):
                for hf in range(2):
                    dve.bn_stats(st[:, t, 6 * hf:6 * hf + 6], X[:, t, 512 * hf:512 * hf + 512])
            dve.drain()
            mv = stat[:, 0:4].rearrange("p (t a) -> p t a", t=NT)
            rs = stat[:, 4:6]
            for t in range(NT):
                dve.bn_aggr(mv[:, t, :], st[:, t, :])
            dve.drain()
            dve.tensor_copy(rs, mv[:, :, 1])
            dve.drain()
            dve_rs(dve, rs, 1.0, LN_EPS)
            for t in range(NT):
                dve.tensor_scalar(X[:, t, :], X[:, t, :], mv[:, t, 0:1], rs[:, t:t + 1], ALU.subtract, ALU.mult)
            dve.drain()
            for n, op in zip(R_LN[layer], (ALU.mult, ALU.add)):
                wait_row(dve, n)
                dve.tensor_tensor(X[:, :, :], X[:, :, :], row_at(n).unsqueeze(1).broadcast_to([P, NT, D]), op)
                dve.drain().then_inc(sem("row_used"), 1)

        def wait_row(dve, n):
            dve.wait_ge(sem(f"row_loaded{n % 2}"), 16 * (n // 2 + 1))

        def dve_head_norm(dve, y, heads, V, gain, gate_ready, gate):
            m = ms[:, 0:NT * heads]
            dve_rs(dve, m, 1.0 / V, LN_EPS)
            rs = m.rearrange("p (t h) -> p t h", t=NT)
            for t in range(NT):
                yy = y[:, t, :].rearrange("p (h v) -> p h v", h=heads)
                dve.tensor_tensor(yy, yy, rs[:, t, :].unsqueeze(2).broadcast_to([P, heads, V]), ALU.mult)
            wait_row(dve, gain)
            dve.drain()
            dve.tensor_tensor(y, y, row_at(gain).unsqueeze(1).broadcast_to([P, NT, heads * V]), ALU.mult)
            dve.drain().then_inc(sem("row_used"), 1)
            gate_ready()
            dve.tensor_tensor(y, y, gate, ALU.mult)

        proj = PROJ[:, :]
        ab_q = proj[:, 0:1024].rearrange("p (a t) -> p a t", a=4)
        ab_k = proj[:, 1024:2048].rearrange("p (a t) -> p a t", a=4)
        ab_v = proj[:, 2048:3072].rearrange("p (t f) -> p t f", t=NT)
        bias_t = SCR[:, 0:3072].rearrange("p (h u) -> p h u", h=A_HEADS)
        gla_v = proj[:, 2048:4096].rearrange("p (t f) -> p t f", t=NT)
        gla_g = [g.rearrange("p (h t) -> p h t", h=4) for g in (proj[:, 4096:5120], MODB[:, 2048:3072])]
        ab_gate = proj[:, 0:3072].rearrange("p (t f) -> p t f", t=NT)
        Y3 = sb("Y3", [P, NT, MIX])
        YT = SCR[:, 0:MC * S].rearrange("p (c t) -> p c t", c=MC)
        rel_sb = sb("rel_sb", [REL_BUCKETS, A_HEADS])
        hot_sb = SCR[0:REL_BUCKETS, 8192:8192 + DIST]
        times_sb = SCR[0:A_HEADS, 8192 + DIST:8192 + 2 * DIST]
        tab_sb = SCR[0:A_HEADS, 8192 + 2 * DIST:8192 + 3 * DIST]

        z_raw = [SCR[:, 1024 * d:1024 * d + 1024] for d in range(2)]
        z_log = [Y3[:, d, 512:MIX] for d in range(2)]

        c_q = proj[:, 0:1024].rearrange("p (a t) -> p a t", a=4)
        c_k = [MODB[:, 1024 * (1 + d):1024 * (2 + d)].rearrange("p (a t) -> p a t", a=4) for d in range(2)]
        c_g = [proj[:, 1024 * (1 + d):1024 * (2 + d)].rearrange("p (a t) -> p a t", a=4) for d in range(2)]
        c_v = proj[:, 3072:4096].rearrange("p (t f) -> p t f", t=NT)
        c_gate = proj[:, 4096:5120].rearrange("p (t f) -> p t f", t=NT)

        def pe_first(pe):
            pe.wait_ge(sem("consts"), 16 * N_CONST)
            pe.matmul(PSB[0:A_HEADS, 3, :], rel_sb[:, :], hot_sb, start=True, stop=True).then_inc(sem("bias_row"), 1)
            pe.wait_ge(sem("x_loaded"), 16)
            pe.wait_ge(sem("bias_row_taken"), 1)
            pe_turn(pe, X, KC, "x")
            pe.wait_ge(sem("turned_taken"), KC // 2)
            project_features(pe, AB_Q)
            project_features(pe, AB_K)
            project_tokens(pe, AB_V)
            phase(pe, "attention")
            pe_attention(pe, 0, A_HEADS,
                         lambda h: ab_q[64 * (h % 2):64 * (h % 2) + 64, h // 2, :],
                         lambda h: ab_k[64 * (h % 2):64 * (h % 2) + 64, h // 2, :],
                         lambda c, h: ab_v[:, c, 64 * h:64 * h + 64],
                         lambda t, h: PSA[:, h % 2, 512 * t + 64 * (h // 2):512 * t + 64 * (h // 2) + 64], False)
            phase(pe, "attention done")
            project_features(pe, AB_GLA[0])
            project_features(pe, AB_GLA[1])
            project_tokens(pe, AB_GLA[2])
            project_tokens(pe, AB_GLA[3])
            for d in range(2):
                for c in range(KC):
                    mm = pe.matmul(PSB[0:16, d, 0:S], lr_w[:, c, 16 * d:16 * d + 16], HT[:, c, :],
                                   start=(c == 0), stop=(c == KC - 1))
            mm.then_inc(sem("lr_done"), 1)
            pe.wait_ge(sem("lr_taken"), 1)
            pe.wait_ge(sem("pair_taken"), 7)
            for d in range(2):
                for h in range(B_HEADS):
                    mm = pe.matmul(PSA[:, d, S * h:S * h + S], up_w[:, d, P * h:P * h + P], lrT[:, d, :],
                                   start=True, stop=True)
                mm.then_inc(sem("gate_logits"), 1)
            phase(pe, "scan")
            for n in range(B_HEADS):
                pe_gla(pe, n, B_VAL, lambda t, n=n: gla_v[:, t, B_VAL * n:B_VAL * n + B_VAL])
            phase(pe, "scan done")
            for n in AB_GATE:
                project_tokens(pe, n)
            phase(pe, "y")
            pe_turn(pe, Y3, MC, "y")
            pe.wait_ge(sem("turned_taken"), KC // 2 + MC // 2)
            pe_out(pe, AB_OUT, YT)
            phase(pe, "x1")

        def act_first(act):
            act.wait_ge(sem("consts"), 16 * N_CONST)
            take(act, AB_Q, ab_q, cols=S, tokens=False)
            take(act, AB_K, ab_k, cols=S, tokens=False)
            take(act, AB_V, ab_v)
            phase(act, "attention")
            act_attention(act, 0, A_HEADS, False, att_sum)
            phase(act, "attention done")
            take(act, AB_GLA[0], ab_q, cols=S, tokens=False, scale=P ** -0.5)
            take(act, AB_GLA[1], ab_k, cols=S, tokens=False)
            take(act, AB_GLA[2], gla_v[:, :, 0:512])
            take(act, AB_GLA[3], gla_v[:, :, 512:1024])
            act.wait_ge(sem("lr_done"), 1)
            act.activation(lrT[:, :, :], PSB[0:16, 0:2, 0:S], ACT.Copy).then_inc(sem("lr_taken"), 1)
            for d in range(2):
                z = z_log[d]
                act.wait_ge(sem("gate_abs"), d + 1)
                act.activation(z, z, ACT.Exp)
                act.drain()
                act.activation(z, z, ACT.Ln, bias=1.0).then_inc(sem("gate_log"), 1)
            phase(act, "scan")
            act_gla(act, 0, B_HEADS, B_VAL, 1.0 / GLA_NORM,
                    lambda h: Y3[:, :, 512 + B_VAL * h:512 + B_VAL * h + B_VAL])
            phase(act, "scan done")
            act_rs(act, ms[:, 0:NT * B_HEADS])
            for j, n in enumerate(AB_GATE):
                take(act, n, ab_gate[:, :, 512 * j:512 * j + 512], func=ACT.Silu)
            phase(act, "y")
            act_rs(act, stat[:, 4:6])
            phase(act, "x1")

        def dve_first(dve):
            dve.memset(SM[:, :, :], 0.0)
            dve.wait_ge(sem("consts"), 16 * N_CONST)
            dve.tensor_copy(CM[:, :], PROJ[:, 0:M_BYTES])
            dve.wait_ge(sem("bias_row"), 1)
            dve.tensor_tensor(tab_sb, PSB[0:A_HEADS, 3, :], times_sb, ALU.add).then_inc(sem("bias_row_taken"), 1)
            take_turned(dve, HT, KC)
            phase(dve, "attention")
            dve.wait_ge(sem("bias_spread"), 16)
            dve_attention(dve, 0, A_HEADS, False, lambda t, h, w: bias_t[:, h, P * t:P * t + w][:, ::-1])
            dve.wait_ge(sem("att_values"), A_HEADS)
            dve.reciprocal(att_rs, att_sum)
            dve.drain()
            for t in range(NT):
                for par in range(2):
                    rs = att_rs[:, t * A_HEADS + par:(t + 1) * A_HEADS:2]
                    dst = Y3[:, t, 0:512].rearrange("p (h o e) -> p h o e", o=2, e=64)[:, :, par, :]
                    dve.tensor_tensor(dst, PSA[:, par, 512 * t:512 * t + 256].rearrange("p (h e) -> p h e", e=64),
                                      rs.unsqueeze(2).broadcast_to([P, 4, 64]), ALU.mult)
            phase(dve, "attention done")
            for d in range(2):
                z = z_log[d]
                zr = z_raw[d]
                dve.wait_ge(sem("gate_logits"), d + 1)
                for h in range(B_HEADS):
                    dve.tensor_scalar(zr[:, S * h:S * h + S], PSA[:, d, S * h:S * h + S],
                                      gate_bias[:, 4 * d + h:4 * d + h + 1], None, ALU.add)
                dve.drain()
                dve.scalar_tensor_tensor(z, zr, -1.0, zr, ALU.mult, ALU.min).then_inc(sem("gate_abs"), 1)
            for d in range(2):
                z = z_log[d]
                zr = z_raw[d]
                dve.wait_ge(sem("gate_log"), d + 1)
                dve.scalar_tensor_tensor(gla_g[d].rearrange("p h t -> p (h t)"), zr, 0.0, z, ALU.min, ALU.subtract)
            phase(dve, "scan")
            dve_gla(dve, 0, B_HEADS, B_VAL, lambda h: ab_q[:, h, :], lambda d, h: ab_k[:, h, :],
                    lambda d, h: gla_g[d][:, h, :], lambda t, h: gla_v[:, t, B_VAL * h:B_VAL * h + B_VAL],
                    lambda h: Y3[:, :, 512 + B_VAL * h:512 + B_VAL * h + B_VAL], 1.0)
            phase(dve, "scan done")
            dve_head_norm(dve, Y3[:, :, 512:MIX], B_HEADS, B_VAL, R_GLA,
                          lambda: dve.wait_ge(sem("pair_taken"), 10), ab_gate[:, :, 512:MIX])
            dve.tensor_tensor(Y3[:, :, 0:512], Y3[:, :, 0:512], ab_gate[:, :, 0:512], ALU.mult)
            phase(dve, "y")
            take_turned(dve, YT, MC)
            dve_layer_norm(dve, AB_OUT, 0)
            phase(dve, "x1")

        def pool_first(pool):
            pool.wait_ge(sem("bias_row_taken"), 1)
            pool.dma_start(bias_dram[:, :], tab_sb).then_inc(sem("bias_stored"), 16)
            pool.wait_ge(sem("bias_stored"), 16)
            src = bass.AP(tensor=bias_dram, offset=1, ap=[[1, P], [DIST, A_HEADS], [1, 3 * P]])
            pool.dma_start(bias_t, src).then_inc(sem("bias_spread"), 16)
            for n, src in enumerate(row_list):
                if n >= 2:
                    pool.wait_ge(sem("row_used"), n - 1)
                pool.dma_start(row_at(n), src.broadcast_to([P, src.shape[1]])).then_inc(sem(f"row_loaded{n % 2}"), 16)

        N_C0 = B_HEADS
        C_PAIRS = 10

        NSA_HPG = NSA_H // NSA_G

        def pe_second(pe):
            pe_turn(pe, X, KC, "x")
            pe.wait_ge(sem("turned_taken"), KC + MC // 2)
            for g in range(3):
                for n in C_GROUP[g][0:3]:
                    project_features(pe, n)
                for n in C_GROUP[g][3:5]:
                    project_tokens(pe, n)
                phase(pe, "scan")
                for h in range(4):
                    pe_gla(pe, N_C0 + 4 * g + h, C_VAL, lambda t, h=h: c_v[:, t, P * h:P * h + P])
                phase(pe, "scan done")
            pe_turn(pe, Y3, MC, "y")
            pe.wait_ge(sem("turned_taken"), KC + MC)
            pe_out(pe, C_OUT, YT)
            phase(pe, "x2")

        def act_second(act):
            act.wait_ge(sem("lower_diff"), 1)
            act.activation(lb, lower[:, 0, :], ACT.Exp).then_inc(sem("lower_exp"), 1)
            for g in range(3):
                take(act, C_GROUP[g][0], c_q, func=ACT.Silu, cols=S, tokens=False)
                for d in range(2):
                    take(act, C_GROUP[g][1 + d], c_g[d], func=ACT.Exp, scale=-1.0, cols=S, tokens=False)
                take(act, C_GROUP[g][3], c_v)
                for d in range(2):
                    act.wait_ge(sem("forget"), 2 * g + d + 1)
                    act.activation(c_g[d], c_g[d], ACT.Ln)
                take(act, C_GROUP[g][4], c_gate, func=ACT.Silu)
                phase(act, "scan")
                act_gla(act, N_C0 + 4 * g, 4, C_VAL, 1.0,
                        lambda h: Y3[:, :, 512 * g + P * h:512 * g + P * h + P])
                act_rs(act, ms[:, 0:NT * 4])
                phase(act, "scan done")
            act_rs(act, stat[:, 4:6])
            phase(act, "x2")

        def dve_second(dve):
            take_turned(dve, HT, KC)
            dve.tensor_tensor(lower[:, 0, :], lower[:, 0, :], lower[:, 1, :], ALU.subtract)\
                .then_inc(sem("lower_diff"), 1)
            dve.wait_ge(sem("lower_exp"), 1)
            dve.tensor_scalar(lb, lb, 1.0, None, ALU.add)
            dve.drain()
            dve.reciprocal(lb, lb)
            dve.drain()
            dve.tensor_scalar(omlb, lb, -1.0, 1.0, ALU.mult, ALU.add)
            dve.drain()
            for g in range(3):
                for d in range(2):
                    dve.wait_ge(sem("pair_taken"), C_PAIRS + 5 * g + 2 + d)
                    f = c_g[d]
                    dve.tensor_scalar(f, f, 1.0, None, ALU.add)
                    dve.drain()
                    dve.reciprocal(f, f)
                    dve.drain()
                    dve.tensor_tensor(f, f, omlb[:, 4 * g:4 * g + 4].unsqueeze(2).broadcast_to([P, 4, S]), ALU.mult)
                    dve.drain()
                    dve.tensor_tensor(f, f, lb[:, 4 * g:4 * g + 4].unsqueeze(2).broadcast_to([P, 4, S]), ALU.add)
                    dve.drain()
                    dve.tensor_scalar(c_k[d], f, -1.0, 1.0, ALU.mult, ALU.add).then_inc(sem("forget"), 1)
                phase(dve, "scan")
                y = Y3[:, :, 512 * g:512 * g + 512]
                dve_gla(dve, N_C0 + 4 * g, 4, C_VAL, lambda h: c_q[:, h, :], lambda d, h: c_k[d][:, h, :],
                        lambda d, h: c_g[d][:, h, :], lambda t, h: c_v[:, t, P * h:P * h + P],
                        lambda h: y[:, :, P * h:P * h + P], P ** -0.5)
                dve.wait_ge(sem("gla_squared"), N_C0 + 4 * g + 4)
                dve_head_norm(dve, y, 4, C_VAL, R_HGRN[g], lambda: None, c_gate)
                phase(dve, "scan done")
            take_turned(dve, YT, MC)
            dve_layer_norm(dve, C_OUT, 1)
            phase(dve, "x2")


        asked = {}

        def need(eng, name):
            k = asked.get((eng, name), 0) + 1
            asked[eng, name] = k
            eng.wait_ge(sem(name), k)

        cT = keep(8)
        pos_i = keep(4)
        pos_f = keep(4)
        trig = [keep(96).rearrange("p (g f) -> p g f", g=3) for _ in range(2)]
        conv_w = keep(96).rearrange("p (l c w) -> p l c w", l=DEPTH, w=CONV_W)
        dn_prm = keep(32).rearrange("p (l k h) -> p l k h", l=DEPTH, k=2)
        ab_raw = keep(32).rearrange("p (t k h) -> p t k h", t=NT, k=2)
        beta = keep(16).rearrange("p (t h) -> p t h", t=NT)
        decay_g = keep(16).rearrange("p (t h) -> p t h", t=NT)
        dn_ss = keep(32)
        dn_rs = dn_ss.rearrange("p (t h) -> p t h", t=NT)
        gcol = keep(8)
        grest = keep(8)
        e_gc = keep(8)
        e_rest = keep(8)
        e_last = keep(8).rearrange("p (c m) -> p c m", c=2)
        tmp8 = keep(48)
        o_ss = keep(16)
        nsa_ss = keep(24)
        nsa_rs = nsa_ss.rearrange("p (t h) -> p t h", t=NT)
        nsa_gate = keep(48).rearrange("p (t h k) -> p t h k", t=NT, k=3)
        cmp_m, cmp_s = keep(16), keep(16)
        cmp_pb = keep(2)
        cmp_hid = keep(64)
        kc_ss = keep(1)
        sums2 = [keep(16) for _ in range(2)]
        cw = keep(16)
        logits = keep(16).rearrange("p (t e) -> p t e", t=NT)
        top8 = keep(16).rearrange("p (t e) -> p t e", t=NT)
        top_i = keep(16).rearrange("p (t e) -> p t e", t=NT)
        top_w = keep(4).rearrange("p (t e) -> p t e", t=NT)
        combine = keep(16).rearrange("p (t e) -> p t e", t=NT)
        comb1 = keep(8)
        rms_x = keep(2)
        state_sb = sb("state_sb", [P, 4, DN_D])

        CB = HT[:, :, 0:P]
        H2 = PROJ[:, 0:2 * D].rearrange("p (t f) -> p t f", t=NT)
        RAW = PROJ[:, 0:3072].rearrange("p (c t) -> p c t", c=12)
        CONV = SCR[:, 0:3072].rearrange("p (c t) -> p c t", c=12)
        Z_GATE = PROJ[:, 3072:4096].rearrange("p (t f) -> p t f", t=NT)
        O_A = PROJ[:, 4096:5120].rearrange("p (t f) -> p t f", t=NT)
        OAT = SCR[:, 11264:12288].rearrange("p (c t) -> p c t", c=4)

        def big(k):
            return SCR[:, 1024 * k:1024 * k + 1024].rearrange("p (h t) -> p h t", h=DN_H)

        DM, LT, AT, TI, TT, ZZ, MT = [big(k) for k in range(7)]
        KT = SCR[:, 7168:7680].rearrange("p (m t) -> p m t", m=4)
        BQT = SCR[:, 7680:8704].rearrange("p (m k t) -> p m k t", m=4, k=2)
        QDT = SCR[:, 8704:9216].rearrange("p (m t) -> p m t", m=4)
        WT = SCR[:, 9216:9728].rearrange("p (m t) -> p m t", m=4)
        VNEW = SCR[:, 9728:10240].rearrange("p (h e) -> p h e", h=DN_H)
        DQ, DK, DBK, DQD, DKD, DVB = [PROJ[:, 512 * k:512 * k + 512].rearrange("p (h e) -> p h e", h=DN_H)
                                      for k in range(6)]
        DKBE = SCR[:, 10240:10752].rearrange("p (h e) -> p h e", h=DN_H)

        NQ = PROJ[:, 0:1024].rearrange("p (t f) -> p t f", t=NT)
        KV1 = PROJ[:, 1024:2048].rearrange("p (t f) -> p t f", t=NT)
        KV2 = PROJ[:, 2048:2608].rearrange("p (t f) -> p t f", t=NT)
        NQK = SCR[:, 0:1536].rearrange("p (t h e) -> p t h e", t=NT, h=12)
        ROPE_A = SCR[:, 1536:2304].rearrange("p (h e) -> p h e", h=12)
        ROPE_B = SCR[:, 2304:3072].rearrange("p (h e) -> p h e", h=12)
        QK8 = SCR[:, 3072:5120].rearrange("p (t f) -> p t f", t=NT)
        QKT = SCR[:, 5120:7168].rearrange("p (c t) -> p c t", c=8)
        XT = SCR[0:NSA_D, 7168:8192].rearrange("p (k g t) -> p k g t", k=2, g=NSA_G)
        CMP = SCR[:, 8192:11264]
        VC = CMP[:, 0:512].rearrange("p (g i e) -> p g i e", g=2, i=4)
        PC = CMP[:, 512:1024].rearrange("p (t h c) -> p t h c", t=NT, h=NSA_H)
        PCT = CMP[:, 1024:1536].rearrange("p (t g q) -> p t g q", t=NT, g=NSA_G)
        SCB = CMP[:, 1536:1792].rearrange("p (t h c) -> p t h c", t=NT, h=NSA_H)
        KC_ROWS = CMP[0:30, 1792:1856]
        KC_AB = CMP[0:30, 1856:1984].rearrange("p (k e) -> p k e", k=2)
        KC_DUP = CMP[0:30, 1984:2112].rearrange("p (k e) -> p k e", k=2)
        KCT = CMP[:, 2112:2142]
        OB = SCR[:, 0:1024].rearrange("p (t f) -> p t f", t=NT)
        OBT = SCR[:, 1024:2048].rearrange("p (c t) -> p c t", c=4)
        OB2 = SCR[:, 2048:3072].rearrange("p (t f) -> p t f", t=NT)
        GATES = [Y3.ap().rearrange("p t f -> p (t f)")[:, 1024 * j:1024 * j + 1024] for j in range(3)] + [PROJ[:, 4096:5120]]
        GATES = [g.rearrange("p (t f) -> p t f", t=NT) for g in GATES]
        YM = SCR[:, 3072:5120].rearrange("p (t f) -> p t f", t=NT)
        YM2 = SCR[:, 5120:7168].rearrange("p (t f) -> p t f", t=NT)
        YMT = SCR[:, 7168:9216].rearrange("p (c t) -> p c t", c=8)

        ACC = PROJ[:, 0:2 * D].rearrange("p (t f) -> p t f", t=NT)
        SILU = [PROJ[:, 2048 + S * b:2048 + S * b + S] for b in range(2)]
        HID = [PROJ[:, 2560 + S * b:2560 + S * b + S] for b in range(2)]

        def pe_ada(pe, its):
            need(pe, "c_spread")
            for m in range(3):
                k = pair_of("pe")
                if k >= 2:
                    pe.wait_ge(sem("pair_taken"), k - 1)
                for hf in range(2):
                    n = its[2 * m + hf]
                    wait_item(pe, n)
                    W = view(n)
                    for c in range(KC):
                        mm = pe.matmul(PSA[:, k % 2, 512 * hf:512 * hf + 512], CB[:, c, :], W[:, c, :],
                                       start=(c == 0), stop=(c == KC - 1))
                    mm.then_inc(sem("item_used"), 1)
            need(pe, "h_ready")
            pe_turn(pe, H2, KC, "h")
            pe.wait_ge(sem("turned_taken"), turns["pe"])

        def act_ada(act, its):
            need(act, "x_ready")
            for t in range(NT):
                e = act.activation(H2[:, t, :], X[:, t, :], ACT.Square, accum_out=rms_x[:, t:t + 1])
            act.drain().then_inc(sem("x_squared"), 1)
            act_rs(act, rms_x)
            for m in range(3):
                k = pair_of("act")
                act.wait_ge(sem("item_used"), its[2 * m + 1] + 1)
                act.activation(MODB[:, D * m:D * m + D], PSA[:, k % 2, :], ACT.Copy).then_inc(sem("pair_taken"), 1)

        def dve_ada(dve, rws):
            dve.tensor_copy(CB, cT.unsqueeze(2).broadcast_to([P, KC, P])).then_inc(sem("c_spread"), 1)
            dve.drain().then_inc(sem("x_ready"), 1)
            need(dve, "x_squared")
            dve_rs(dve, rms_x, 1.0 / D, EPS)
            k0 = pairs.get("dve_ada", PAIRS_BEFORE)
            pairs["dve_ada"] = k0 + 3
            m0, m1, m2 = [MODB[:, D * m:D * m + D] for m in range(3)]
            for m, r in ((m0, rws[0]), (m1, rws[1])):
                k0 += 1
                dve.wait_ge(sem("pair_taken"), k0)
                wait_row(dve, r)
                dve.tensor_tensor(m, m, row_at(r), ALU.add)
                dve.drain().then_inc(sem("row_used"), 1)
            wait_row(dve, rws[2])
            dve.scalar_tensor_tensor(m1, m1, 1.0, row_at(rws[2]), ALU.add, ALU.mult)
            dve.drain().then_inc(sem("row_used"), 1)
            for t in range(NT):
                dve.scalar_tensor_tensor(H2[:, t, :], X[:, t, :], rms_x[:, t:t + 1], m1, ALU.mult, ALU.mult)
            dve.drain()
            dve.tensor_tensor(H2, H2, m0.unsqueeze(1).broadcast_to([P, NT, D]), ALU.add).then_inc(sem("h_ready"), 1)
            dve.wait_ge(sem("pair_taken"), k0 + 1)
            wait_row(dve, rws[3])
            dve.tensor_tensor(m2, m2, row_at(rws[3]), ALU.add)
            dve.drain().then_inc(sem("row_used"), 1)
            take_turned(dve, HT, KC)

        def dve_positions(dve):
            dve.tensor_copy(pos_f, pos_i.bitcast(I32))
            dve.drain()
            ang, turn = SCR[:, 0:96].rearrange("p (g f) -> p g f", g=3), SCR[:, 96:288].rearrange("p (k g f) -> p k g f", k=2, g=3)
            for g in range(3):
                dve.tensor_scalar(ang[:, g, :], CF[:, C_FREQ:C_FREQ + HALF], pos_f[:, g:g + 1], None, ALU.mult)
            dve.drain()
            magic = 12582912.0
            two_pi = [6.28125, 0.0019350051879882812, 3.0199159819567e-07]
            for k in range(2):
                dve.tensor_scalar(turn[:, k], ang, float(1.0 / (2.0 * np.pi)), 0.25 * (1 - k), ALU.mult, ALU.add)
                dve.drain()
                dve.tensor_scalar(turn[:, k], turn[:, k], magic, -magic, ALU.add, ALU.add)
                dve.drain()
                src = ang
                for part in two_pi:
                    dve.scalar_tensor_tensor(trig[k], turn[:, k], -part, src, ALU.mult, ALU.add)
                    dve.drain()
                    src = trig[k]
                if k == 0:
                    dve.tensor_scalar(trig[0], trig[0], float(np.pi / 2), None, ALU.add)
                    dve.drain()
                dve.tensor_scalar(trig[k], trig[k], 3.1415925, -3.1415925, ALU.min, ALU.max)
            dve.drain().then_inc(sem("angles"), 1)
            need(dve, "sines")

        def act_positions(act):
            act.activation(cT, cT, ACT.Silu)
            need(act, "angles")
            for k in range(2):
                act.activation(trig[k], trig[k], ACT.Sin)
            act.drain().then_inc(sem("sines"), 1)

        COS, SIN = trig

        def pe_delta(pe, l):
            L = L2[l]
            for n in L["qkv"]:
                project_features(pe, n)
            project_tokens(pe, L["z"])
            for t in range(NT):
                for c in range(KC):
                    mm = pe.matmul(PSB[:, 3, 16 * t:16 * t + 16], HT[:, c, P * t:P * t + P], ab_w[:, l, c, :],
                                   start=(c == 0), stop=(c == KC - 1))
            mm.then_inc(sem("ab_logits"), 1)
            need(pe, "ab_taken")
            need(pe, "conv_done")
            for t in range(NT):
                for g in range(3):
                    k = turns["pe"]
                    turns["pe"] = k + 1
                    pe.wait_ge(sem("turned_taken"), k - 3)
                    for j in range(4):
                        mm = pe.transpose(PSB[:, k % 4, P * j:P * j + P], CONV[:, 4 * g + j, P * t:P * t + P], ident)
                    mm.then_inc(sem("turned"), 1)
            phase(pe, "tokens")
            for t in range(NT):
                need(pe, "g_spread")
                for h in range(DN_H):
                    pe.matmul(PSA[:, 0, P * h:P * h + P], MT[:, h, :], CF[:, C_TRI:C_TRI + P], start=True, stop=True)
                pe.matmul(PSB[:, 0, 0:DN_H], CF[:, C_TRI:C_TRI + P], decay_g[:, t, :], start=True, stop=True)
                pe.matmul(PSB[:, 0, DN_H:2 * DN_H], CF[:, C_BLK:C_BLK + P], decay_g[:, t, :], start=True, stop=True)\
                    .then_inc(sem("gc_sums"), 1)
                need(pe, "dn_rows")
                for k, src in enumerate((DK, DBK, DQ, DQD)):
                    for m in range(4):
                        mm = pe.transpose(PSB[:, k, P * m:P * m + P], src[:, 2 * m:2 * m + 2, :].rearrange("p a e -> p (a e)"), ident)
                mm.then_inc(sem("dn_turned"), 1)
                need(pe, "dn_turned_taken")
                for h in range(DN_H):
                    o, m = h % 2, h // 2
                    mm = pe.matmul(PSA[:, o, S * m:S * m + S], KT[64 * o:64 * o + 64, m, :],
                                   BQT[64 * o:64 * o + 64, m, :, :].rearrange("p k t -> p (k t)"), start=True, stop=True)
                mm.then_inc(sem("dn_scores"), 1)
                need(pe, "inv_first")
                for h in range(DN_H):
                    mm = pe.transpose(PSA[:, 0, P * h:P * h + P], TT[:, h, :], ident)
                mm.then_inc(sem("inv_turned"), 1)
                for _ in LEVELS[1:]:
                    need(pe, "inv_ready")
                    for h in range(DN_H):
                        mm = pe.matmul(PSA[:, 0, P * h:P * h + P], MT[:, h, :], TI[:, h, :], start=True, stop=True)
                    mm.then_inc(sem("inv_z"), 1)
                    need(pe, "inv_z_taken")
                    for h in range(DN_H):
                        pe.matmul(PSA[:, 1, P * h:P * h + P], TT[:, h, :], ZZ[:, h, :], start=True, stop=True)
                    for h in range(DN_H):
                        mm = pe.matmul(PSB[:, h // 4, P * (h % 4):P * (h % 4) + P], ZZ[:, h, :], TT[:, h, :],
                                       start=True, stop=True)
                    mm.then_inc(sem("inv_tz"), 1)
                need(pe, "inv_done")
                for h in range(DN_H):
                    o, m = h % 2, h // 2
                    mm = pe.matmul(PSA[64 * o:64 * o + 64, 0, P * m:P * m + P], DKBE[:, h, :], TT[:, h, :],
                                   start=(m == 0), stop=True, skip_group_check=True)
                mm.then_inc(sem("w_ready"), 1)
                for h in range(DN_H):
                    o, m = h % 2, h // 2
                    mm = pe.matmul(PSB[:, o, 64 * m:64 * m + 64], TT[:, h, :], DVB[:, h, :], start=(m == 0), stop=False,
                                   skip_group_check=True)
                need(pe, "w_taken")
                for c in range(2):
                    r = DN_C * c
                    need(pe, "dn_state")
                    for h in range(DN_H):
                        o, m = h % 2, h // 2
                        mm = pe.matmul(PSB[r:r + 64, o, 64 * m:64 * m + 64], WT[64 * o:64 * o + 64, m, r:r + 64],
                                       state_sb[64 * o:64 * o + 64, m, :], start=False, stop=True, skip_group_check=True)
                    mm.then_inc(sem("v_new"), 1)
                    for h in range(DN_H):
                        o, m = h % 2, h // 2
                        pe.matmul(PSB[r:r + 64, 2 + o, 64 * m:64 * m + 64], QDT[64 * o:64 * o + 64, m, r:r + 64],
                                  state_sb[64 * o:64 * o + 64, m, :], start=(m == 0), stop=False, skip_group_check=True)
                    need(pe, "v_new_taken")
                    for h in range(DN_H):
                        o, m = h % 2, h // 2
                        mm = pe.matmul(PSA[64 * o:64 * o + 64, 1, 64 * m:64 * m + 64], DKD[r:r + 64, h, :],
                                       VNEW[r:r + 64, h, :], start=(m == 0), stop=True, skip_group_check=True)
                    mm.then_inc(sem("dn_update"), 1)
                for h in range(DN_H):
                    o, m = h % 2, h // 2
                    mm = pe.matmul(PSB[:, 2 + o, 64 * m:64 * m + 64], AT[:, h, :], VNEW[:, h, :], start=False, stop=True,
                                   skip_group_check=True)
                mm.then_inc(sem("dn_out"), 1)
                need(pe, "dn_out_taken")
            phase(pe, "delta done")
            pe_turn(pe, O_A, 4, "oa")

        def act_delta(act, l):
            L = L2[l]
            for i, n in enumerate(L["qkv"]):
                take(act, n, RAW[:, 4 * i:4 * i + 4, :], cols=S, tokens=False)
            take(act, L["z"], Z_GATE, func=ACT.Silu)
            need(act, "conv_sum")
            act.activation(CONV, CONV, ACT.Silu).then_inc(sem("conv_done"), 1)
            need(act, "ab_ready")
            act.activation(beta, ab_raw[:, :, 0, :], ACT.Sigmoid)
            act.activation(tmp8[:, 0:16], tmp8[:, 0:16], ACT.Exp)
            act.activation(dn_prm[:, l, 0, :], dn_prm[:, l, 0, :], ACT.Exp)
            act.drain()
            act.activation(tmp8[:, 0:16], tmp8[:, 0:16], ACT.Ln, bias=1.0)
            act.drain().then_inc(sem("softplus"), 1)
            act_rs(act, dn_ss)
            phase(act, "tokens")
            for t in range(NT):
                need(act, "gc_cols")
                act.activation(e_gc, gcol, ACT.Exp)
                act.activation(e_rest, grest, ACT.Exp)
                e = act.activation(DM, DM, ACT.Exp)
                need(act, "last_cols")
                act.activation(e_last, e_last, ACT.Exp)
                act.drain().then_inc(sem("dn_exp"), 1)
                need(act, "dn_turned")
                act.activation(KT, PSB[:, 0, :].rearrange("p (m t) -> p m t", m=4), ACT.Copy)
                act.activation(BQT[:, :, 0, :], PSB[:, 1, :].rearrange("p (m t) -> p m t", m=4), ACT.Copy)
                act.activation(BQT[:, :, 1, :], PSB[:, 2, :].rearrange("p (m t) -> p m t", m=4), ACT.Copy)
                act.activation(QDT, PSB[:, 3, :].rearrange("p (m t) -> p m t", m=4), ACT.Copy)
                act.drain().then_inc(sem("dn_turned_taken"), 1)
                for _ in LEVELS[1:]:
                    need(act, "inv_z")
                    act.activation(ZZ.rearrange("p h t -> p (h t)"), PSA[:, 0, :], ACT.Copy).then_inc(sem("inv_z_taken"), 1)
                need(act, "w_ready")
                act.activation(WT, PSA[:, 0, 0:512].rearrange("p (m t) -> p m t", m=4), ACT.Copy).then_inc(sem("w_taken"), 1)
            need(act, "o_sums")
            act_rs(act, o_ss)
            phase(act, "delta done")

        def dve_delta(dve, l):
            k0 = pairs["dve_ada"]
            for i in range(12):
                if i % 4 == 0:
                    k0 += 1
                    dve.wait_ge(sem("pair_taken"), k0)
                dve.tensor_scalar(CONV[:, i, :], RAW[:, i, :], conv_w[:, l, i, 3:4], None, ALU.mult)
            for back in range(1, CONV_W):
                dve.drain()
                for i in range(12):
                    e = dve.scalar_tensor_tensor(CONV[:, i, back:S], RAW[:, i, 0:S - back],
                                                 conv_w[:, l, i, 3 - back:4 - back], CONV[:, i, back:S], ALU.mult, ALU.add)
            e.then_inc(sem("conv_sum"), 1)
            pairs["dve_ada"] = k0 + 1
            need(dve, "ab_logits")
            dve.tensor_copy(ab_raw.rearrange("p t k h -> p (t k h)"), PSB[:, 3, 0:32]).then_inc(sem("ab_taken"), 1)
            dve.drain()
            a = ab_raw[:, :, 1, :]
            dve.tensor_tensor(a, a, dn_prm[:, l, 1, :].unsqueeze(1).broadcast_to([P, NT, DN_H]), ALU.add)
            dve.drain()
            dve.scalar_tensor_tensor(tmp8[:, 0:16].rearrange("p (t h) -> p t h", t=NT), a, -1.0, a, ALU.mult, ALU.min)
            dve.drain().then_inc(sem("ab_ready"), 1)
            for t in range(NT):
                for g in range(3):
                    k = turns["take"]
                    turns["take"] = k + 1
                    dve.wait_ge(sem("turned"), k + 1)
                    dve.tensor_copy(Y3[:, t, 512 * g:512 * g + 512], PSB[:, k % 4, :]).then_inc(sem("turned_taken"), 1)
            need(dve, "softplus")
            dve.scalar_tensor_tensor(decay_g, a, 0.0, tmp8[:, 0:16].rearrange("p (t h) -> p t h", t=NT), ALU.max, ALU.add)
            dve.drain()
            dve.scalar_tensor_tensor(decay_g, decay_g, -1.0, dn_prm[:, l, 0, :].unsqueeze(1).broadcast_to([P, NT, DN_H]),
                                     ALU.mult, ALU.mult)
            sq = SCR[:, 4096:6144].rearrange("p (t f) -> p t f", t=NT)
            dve.tensor_tensor(sq, Y3[:, :, 0:1024], Y3[:, :, 0:1024], ALU.mult)
            dve.drain()
            dve.tensor_reduce(dn_ss.rearrange("p (t h) -> p t h", t=NT), sq.rearrange("p t (h e) -> p t h e", e=64), AX.X, ALU.add)
            dve.drain()
            dve_rs(dve, dn_ss, 1.0, EPS)
            dve.tensor_scalar(dn_rs[:, :, 0:8], dn_rs[:, :, 0:8], DN_D ** -0.5, None, ALU.mult)
            dve.memset(state_sb[:, :, :], 0.0)
            phase(dve, "tokens")

            def rows8(a):
                return a.unsqueeze(2).broadcast_to([P, DN_H, 64])

            for t in range(NT):
                q, k, v = [Y3[:, t, 512 * j:512 * j + 512].rearrange("p (h e) -> p h e", h=DN_H) for j in range(3)]
                dve.tensor_copy(MT, decay_g[:, t, :].unsqueeze(2).broadcast_to([P, DN_H, P])).then_inc(sem("g_spread"), 1)
                dve.tensor_tensor(DQ, q, rows8(dn_rs[:, t, 0:8]), ALU.mult)
                dve.tensor_tensor(DK, k, rows8(dn_rs[:, t, 8:16]), ALU.mult)
                dve.tensor_tensor(DVB, v, rows8(beta[:, t, :]), ALU.mult)
                need(dve, "gc_sums")
                dve.tensor_copy(gcol, PSB[:, 0, 0:8])
                dve.drain()
                dve.tensor_tensor(grest, PSB[:, 0, 8:16], gcol, ALU.subtract)
                for h in range(DN_H):
                    dve.tensor_scalar(DM[:, h, :], PSA[:, 0, P * h:P * h + P], gcol[:, h:h + 1], 0.0, ALU.subtract, ALU.min)
                dve.drain().then_inc(sem("gc_cols"), 1)
                gl = PSA[:, 0, :].rearrange("p (m o t) -> p m o t", m=4, o=2)
                for o in range(2):
                    for c in range(2):
                        dve.tensor_copy(e_last[64 * o:64 * o + 64, c, :], gl[64 * o:64 * o + 64, :, o, 64 * c + 63])
                dve.drain().then_inc(sem("last_cols"), 1)
                dve.tensor_tensor(DBK, DK, rows8(beta[:, t, :]), ALU.mult)
                need(dve, "dn_exp")
                dve.tensor_tensor(DQD, DQ, rows8(e_gc), ALU.mult)
                dve.tensor_tensor(DKD, DK, rows8(e_rest), ALU.mult)
                dve.drain()
                dve.scalar_tensor_tensor(DKBE, DBK, -1.0, rows8(e_gc), ALU.mult, ALU.mult).then_inc(sem("dn_rows"), 1)
                dve.tensor_tensor(DM, DM, CM[:, M_LE:M_LE + P].unsqueeze(1).broadcast_to([P, DN_H, P]), ALU.mult)
                dve.drain()
                need(dve, "dn_scores")
                for o in range(2):
                    ps = PSA[:, o, :].rearrange("p (m k t) -> p m k t", m=4, k=2)
                    dm, lt, atd = [x.rearrange("p (m o) t -> p m o t", o=2)[:, :, o, :] for x in (DM, LT, AT)]
                    dve.tensor_tensor(lt, ps[:, :, 0, :], dm, ALU.mult)
                    dve.tensor_tensor(atd, ps[:, :, 1, :], dm, ALU.mult)
                dve.drain()
                dve.tensor_tensor(LT, LT, CM[:, M_LT:M_LT + P].unsqueeze(1).broadcast_to([P, DN_H, P]), ALU.mult)
                dve.drain()

                def level(n):
                    return CM[:, M_LEVEL + n * P:M_LEVEL + n * P + P].unsqueeze(1).broadcast_to([P, DN_H, P])

                dve.tensor_tensor(TT, LT, level(0), ALU.mult)
                dve.tensor_tensor(MT, LT, level(1), ALU.mult)
                dve.drain()
                dve.scalar_tensor_tensor(TT, TT, -1.0, ident.unsqueeze(1).broadcast_to([P, DN_H, P]), ALU.mult, ALU.add)\
                    .then_inc(sem("inv_first"), 1)
                need(dve, "inv_turned")
                dve.tensor_copy(TI.rearrange("p h t -> p (h t)"), PSA[:, 0, :]).then_inc(sem("inv_ready"), 1)
                for n in range(1, len(LEVELS)):
                    need(dve, "inv_tz")
                    dve.tensor_tensor(TI.rearrange("p h t -> p (h t)"), TI.rearrange("p h t -> p (h t)"), PSA[:, 1, :], ALU.subtract)
                    dve.tensor_tensor(TT.rearrange("p h t -> p (h t)"), TT.rearrange("p h t -> p (h t)"), PSB[:, 0:2, :].rearrange("p a b -> p (a b)"), ALU.subtract)
                    if n + 1 < len(LEVELS):
                        dve.tensor_tensor(MT, LT, level(n + 1), ALU.mult)
                    dve.drain().then_inc(sem("inv_ready" if n + 1 < len(LEVELS) else "inv_done"), 1)
                for c in range(2):
                    r = DN_C * c
                    dve.drain().then_inc(sem("dn_state"), 1)
                    need(dve, "v_new")
                    vn = VNEW[r:r + 64].rearrange("p (m o) e -> p m o e", o=2)
                    for o in range(2):
                        e = dve.tensor_copy(vn[:, :, o, :], PSB[r:r + 64, o, 0:256].rearrange("p (m e) -> p m e", m=4))
                    e.then_inc(sem("v_new_taken"), 1)
                    need(dve, "dn_update")
                    dve.tensor_tensor(state_sb[:, :, :], state_sb[:, :, :], e_last[:, c, :].unsqueeze(2).broadcast_to([P, 4, 64]), ALU.mult)
                    dve.drain()
                    dve.tensor_tensor(state_sb[:, :, :], state_sb[:, :, :], PSA[:, 1, 0:256].rearrange("p (m e) -> p m e", m=4), ALU.add)
                need(dve, "dn_out")
                oa = O_A[:, t, :].rearrange("p (m o e) -> p m o e", m=4, o=2)
                for o in range(2):
                    e = dve.tensor_copy(oa[:, :, o, :], PSB[:, 2 + o, 0:256].rearrange("p (m e) -> p m e", m=4))
                e.then_inc(sem("dn_out_taken"), 1)
            dve.drain()
            sq = SCR[:, 0:1024].rearrange("p (t f) -> p t f", t=NT)
            dve.tensor_tensor(sq, O_A, O_A, ALU.mult)
            dve.drain()
            dve.tensor_reduce(o_ss, sq.rearrange("p t (h e) -> p (t h) e", e=64), AX.X, ALU.add)
            dve.drain().then_inc(sem("o_sums"), 1)
            dve_rs(dve, o_ss, 1.0 / DN_D, EPS)
            oh = O_A.rearrange("p t (h e) -> p (t h) e", e=64)
            dve.tensor_tensor(oh, oh, o_ss.unsqueeze(2).broadcast_to([P, 16, 64]), ALU.mult)
            dve.drain()
            dve.tensor_tensor(oh, oh, norm_rows[:, l, 4:5, :].broadcast_to([P, 16, 64]), ALU.mult)
            dve.drain()
            dve.tensor_tensor(O_A, O_A, Z_GATE, ALU.mult)
            phase(dve, "delta done")
            take_turned(dve, OAT, 4)

        assert S // 64 <= 16 and S <= 512

        def pe_nsa(pe, l):
            L = L2[l]
            pe.wait_ge(sem("turned_taken"), turns["pe"])
            project_tokens(pe, L["nq"])
            project_tokens(pe, L["kv"][0])
            project_tokens(pe, L["kv"][1], 280)
            pe.wait_ge(sem("pair_taken"), pairs["pe"])
            for kind in range(2):
                for g in range(NSA_G):
                    for t in range(NT):
                        mm = pe.transpose(PSB[0:NSA_D, kind, S * g + P * t:S * g + P * t + P],
                                          KV1[:, t, 64 * (2 * kind + g):64 * (2 * kind + g) + 64], ident)
            mm.then_inc(sem("cmp_turned"), 1)
            need(pe, "cmp_turned_taken")
            wait_item(pe, L["cmp"])
            W = view(L["cmp"])
            pos = cmp_prm[:, l, 0:64].rearrange("p (k l) -> p k l", k=2)
            for kind in range(2):
                for i in range(CMP_LEN):
                    x = XT[:, kind, :, i:i + CMP_STRIDE * (N_CMP - 1) + 1:CMP_STRIDE]
                    mm = pe.matmul(PSB[0:64, 2, 32 * kind:32 * kind + 30].rearrange("p (g j) -> p g j", g=2), W[:, CMP_LEN * kind + i, :], x,
                                   start=(i == 0), stop=(i == CMP_LEN - 1))
                for i in range(CMP_LEN):
                    mm = pe.matmul(PSB[0:64, 2, 64 + kind:65 + kind], W[:, CMP_LEN * kind + i, :], pos[:, kind, i:i + 1],
                                   start=(i == 0), stop=(i == CMP_LEN - 1))
            mm.then_inc(sem("item_used"), 1)
            need(pe, "cmp_hidden")
            w2 = cmp_prm[:, l, 64:192].rearrange("p (k e) -> p k e", k=2)
            hid = cmp_hid[0:64, :]
            pe.matmul(PSB[0:30, 0, 0:64], hid[:, 0:30], w2[:, 0, :], start=True, stop=True)
            for g in range(NSA_G):
                for i in range(4):
                    mm = pe.matmul(PSB[32 * i:32 * i + N_CMP, 1, 64 * g:64 * g + 64], hid[:, 32 + 15 * g:47 + 15 * g], w2[:, 1, :],
                                   start=(g == 0), stop=True, skip_group_check=True)
            mm.then_inc(sem("cmp_kv"), 1)
            for n in L["mg"]:
                project_tokens(pe, n)
            need(pe, "qk_ready")
            need(pe, "kc_rows")
            pe_turn(pe, QK8, 8, "qk")
            pe.wait_ge(sem("turned_taken"), turns["pe"])
            need(pe, "kc_ready")
            pe.transpose(PSB[:, 0, 0:30], KC_DUP.rearrange("p k e -> p (k e)"), ident[0:30, 0:30]).then_inc(sem("kc_turned"), 1)
            need(pe, "kc_taken")
            phase(pe, "compressed")
            for o in range(2):
                for t in range(NT):
                    for m in range(4):
                        g = (2 * m + o) // NSA_HPG
                        mm = pe.matmul(PSB[:, o, 64 * t + 16 * m:64 * t + 16 * m + 15], QKT[64 * o:64 * o + 64, m, P * t:P * t + P],
                                       KCT[64 * o:64 * o + 64, 15 * g:15 * g + 15], start=True, stop=True)
            mm.then_inc(sem("cmp_scores"), 1)
            need(pe, "cmp_probs")
            for t in range(NT):
                for g in range(NSA_G):
                    mm = pe.transpose(PSB[:, 2, S * t + P * g:S * t + P * g + P],
                                      PC[:, t, 4 * g:4 * g + 4, :].rearrange("p h c -> p (h c)"), ident)
            mm.then_inc(sem("cmp_pturned"), 1)
            need(pe, "cmp_ptaken")
            for t in range(NT):
                for g in range(NSA_G):
                    mm = pe.matmul(PSA[:, 0, 512 * t + 256 * g:512 * t + 256 * g + 256], PCT[:, t, g, :],
                                   VC[:, g, :, :].rearrange("p i e -> p (i e)"), start=True, stop=True)
            mm.then_inc(sem("cmp_out"), 1)
            phase(pe, "attention")
            for kind in range(2):
                v = KV1 if kind == 0 else KV2
                c0 = 384 if kind == 0 else 128
                pe_attention(pe, att_base(l, kind), NSA_H,
                             lambda h: QKT[64 * (h % 2):64 * (h % 2) + 64, h // 2, :],
                             lambda h: QKT[64 * (h % 2):64 * (h % 2) + 64, 4 + 2 * kind + h // NSA_HPG, :],
                             lambda c, h: v[:, c, c0 + 64 * (h // NSA_HPG):c0 + 64 * (h // NSA_HPG) + 64],
                             lambda t, h: PSA[:, kind, 512 * t + 64 * h:512 * t + 64 * h + 64], True, kind == 0)
            phase(pe, "attention done")

        def att_base(l, kind):
            return A_HEADS + NSA_H * (2 * l + kind)

        def act_nsa(act, l):
            L = L2[l]
            take(act, L["nq"], NQ)
            take(act, L["kv"][0], KV1)
            take(act, L["kv"][1], KV2, cols=280)
            act.drain()
            act.activation(nsa_gate, KV2[:, :, 256:280].rearrange("p t (h k) -> p t h k", k=3), ACT.Sigmoid)
            need(act, "cmp_turned")
            act.activation(XT.rearrange("p k g t -> p (k g t)"), PSB[0:64, 0:2, :].rearrange("p a b -> p (a b)"), ACT.Copy)\
                .then_inc(sem("cmp_turned_taken"), 1)
            act.wait_ge(sem("item_used"), L["cmp"] + 1)
            act.activation(cmp_pb[0:64, :], PSB[0:64, 2, 64:66], ACT.Copy)
            act.drain()
            for kind in range(2):
                e = act.activation(cmp_hid[0:64, 32 * kind:32 * kind + 30], PSB[0:64, 2, 32 * kind:32 * kind + 30], ACT.Silu,
                                   bias=cmp_pb[0:64, kind:kind + 1])
            e.then_inc(sem("cmp_hidden"), 1)
            for j, n in enumerate(L["mg"]):
                take(act, n, GATES[j], func=ACT.Sigmoid)
            need(act, "nsa_sums")
            act_rs(act, nsa_ss)
            need(act, "kc_sums")
            act_rs(act, kc_ss[0:30])
            need(act, "kc_turned")
            act.activation(KCT, PSB[:, 0, 0:30], ACT.Copy).then_inc(sem("kc_taken"), 1)
            phase(act, "compressed")
            need(act, "cmp_scored")
            act.activation(SCB[:, :, :, 0:15], SCB[:, :, :, 0:15], ACT.Exp).then_inc(sem("cmp_exp"), 1)
            need(act, "cmp_pturned")
            act.activation(PCT.rearrange("p t g q -> p (t g q)"), PSB[:, 2, :], ACT.Copy).then_inc(sem("cmp_ptaken"), 1)
            phase(act, "attention")
            for kind in range(2):
                act_attention(act, att_base(l, kind), NSA_H, True, sums2[kind], kind == 0)
            phase(act, "attention done")


        def dve_nsa(dve, l):
            dve.memset(VC, 0.0)
            dve.memset(PC, 0.0)
            pairs["dve_ada"] += 3
            dve.wait_ge(sem("pair_taken"), pairs["dve_ada"])
            pairs["dve_ada"] += 4
            parts = [(NQ, 0, 0, 8), (KV1, 256, 8, 2), (KV2, 0, 10, 2)]
            q3 = [(src[:, :, c0:c0 + 64 * n].rearrange("p t (h e) -> p t h e", e=64), h0, n) for src, c0, h0, n in parts]
            for src, h0, n in q3:
                dve.tensor_tensor(NQK[:, :, h0:h0 + n, :], src, src, ALU.mult)
            dve.drain()
            dve.tensor_reduce(nsa_rs, NQK, AX.X, ALU.add)
            dve.drain().then_inc(sem("nsa_sums"), 1)
            dve_rs(dve, nsa_ss, 1.0 / NSA_D, EPS)
            for t in range(NT):
                for src, h0, n in q3:
                    dve.tensor_tensor(NQK[:, t, h0:h0 + n, :], src[:, t], nsa_rs[:, t, h0:h0 + n].unsqueeze(2).broadcast_to([P, n, 64]), ALU.mult)
            dve.drain()
            for t in range(NT):
                for r, h0, n in ((0, 0, 8), (2, 8, 2), (3, 10, 2)):
                    dve.tensor_tensor(NQK[:, t, h0:h0 + n, :], NQK[:, t, h0:h0 + n, :], norm_rows[:, l, r:r + 1, :].broadcast_to([P, n, 64]), ALU.mult)
            for t in range(NT):
                dve.drain()
                for dst, tr in ((ROPE_A, COS), (ROPE_B, SIN)):
                    for hf in range(2):
                        dve.tensor_tensor(dst[:, :, HALF * hf:HALF * hf + HALF], NQK[:, t, :, HALF * hf:HALF * hf + HALF],
                                          tr[:, t:t + 1, :].broadcast_to([P, 12, HALF]), ALU.mult)
                dve.drain()
                for hf, op in ((0, ALU.subtract), (1, ALU.add)):
                    a, b = ROPE_A[:, :, HALF * hf:HALF * hf + HALF], ROPE_B[:, :, HALF * (1 - hf):HALF * (1 - hf) + HALF]
                    q = QK8[:, t, 0:512].rearrange("p (h e) -> p h e", e=64)
                    dve.tensor_tensor(q[:, :, HALF * hf:HALF * hf + HALF], a[:, 0:8], b[:, 0:8], op)
                    kd = QK8[:, t, 512:1024].rearrange("p (k c e) -> p k c e", k=4, c=2)
                    for twice in range(2):
                        e = dve.tensor_tensor(kd[:, :, twice, HALF * hf:HALF * hf + HALF], a[:, 8:12], b[:, 8:12], op)
            e.then_inc(sem("qk_ready"), 1)
            need(dve, "cmp_kv")
            dve.tensor_copy(KC_ROWS, PSB[0:30, 0, 0:64])
            for g in range(NSA_G):
                for i in range(4):
                    dve.tensor_copy(VC[32 * i:32 * i + N_CMP, g, i, :], PSB[32 * i:32 * i + N_CMP, 1, 64 * g:64 * g + 64])
            dve.drain().then_inc(sem("kc_rows"), 1)
            dve.tensor_tensor(KC_AB[:, 0, :], KC_ROWS, KC_ROWS, ALU.mult)
            dve.drain()
            dve.tensor_reduce(kc_ss[0:30], KC_AB[:, 0, :], AX.X, ALU.add)
            dve.drain().then_inc(sem("kc_sums"), 1)
            dve_rs(dve, kc_ss[0:30], 1.0 / NSA_D, EPS)
            dve.scalar_tensor_tensor(KC_ROWS, KC_ROWS, kc_ss[0:30], norm_rows[0:30, l, 1, :], ALU.mult, ALU.mult)
            dve.drain()
            for k, tr in enumerate((COS, SIN)):
                dve.tensor_tensor(KC_AB[:, k, :].rearrange("p (a e) -> p a e", a=2), KC_ROWS.rearrange("p (a e) -> p a e", a=2),
                                  tr[0:30, 2:3, :].broadcast_to([30, 2, HALF]), ALU.mult)
            dve.drain()
            for hf, op in ((0, ALU.subtract), (1, ALU.add)):
                dve.tensor_tensor(KC_DUP[:, :, HALF * hf:HALF * hf + HALF],
                                  KC_AB[:, 0:1, HALF * hf:HALF * hf + HALF].broadcast_to([30, 2, HALF]),
                                  KC_AB[:, 1:2, HALF * (1 - hf):HALF * (1 - hf) + HALF].broadcast_to([30, 2, HALF]), op)
            dve.drain().then_inc(sem("kc_ready"), 1)
            take_turned(dve, QKT, 8)
            phase(dve, "compressed")
            need(dve, "cmp_scores")
            for o in range(2):
                for t in range(NT):
                    dve.scalar_tensor_tensor(SCB.rearrange("p t (m o) c -> p t m o c", o=2)[:, t, :, o, 0:15],
                                             PSB[:, o, 64 * t:64 * t + 64].rearrange("p (m c) -> p m c", m=4)[:, :, 0:15], NSA_D ** -0.5,
                                             CF[:, C_CMPB + 16 * t:C_CMPB + 16 * t + 15].unsqueeze(1).broadcast_to([P, 4, 15]),
                                             ALU.mult, ALU.add)
            dve.drain()
            s3 = SCB.rearrange("p t h c -> p (t h) c")[:, :, 0:15]
            dve.tensor_reduce(cmp_m, s3, AX.X, ALU.max)
            dve.drain()
            dve.tensor_tensor(s3, s3, cmp_m.unsqueeze(2).broadcast_to([P, 16, 15]), ALU.subtract).then_inc(sem("cmp_scored"), 1)
            need(dve, "cmp_exp")
            for t in range(NT):
                dve.tensor_tensor(PC[:, t, :, 0:15], SCB[:, t, :, 0:15],
                                  CF[:, C_CMPM + 16 * t:C_CMPM + 16 * t + 15].unsqueeze(1).broadcast_to([P, NSA_H, 15]), ALU.mult)
            dve.drain().then_inc(sem("cmp_probs"), 1)
            dve.tensor_reduce(cmp_s, PC.rearrange("p t h c -> p (t h) c"), AX.X, ALU.add)
            dve.drain()
            dve.tensor_scalar(cmp_s, cmp_s, 1e-30, None, ALU.max)
            dve.drain()
            dve.reciprocal(cmp_s, cmp_s)
            dve.drain()
            gate = nsa_gate.rearrange("p t h k -> p (t h) k")
            dve.tensor_tensor(cw, cmp_s, gate[:, :, 0], ALU.mult)
            dve.drain()
            need(dve, "cmp_out")
            ob = OB.rearrange("p t (h e) -> p (t h) e", e=64)
            ob2 = OB2.rearrange("p t (h e) -> p (t h) e", e=64)
            dve.tensor_tensor(ob, PSA[:, 0, :].rearrange("p (h e) -> p h e", e=64), cw.unsqueeze(2).broadcast_to([P, 16, 64]), ALU.mult)
            phase(dve, "attention")
            for kind in range(2):
                dve_attention(dve, att_base(l, kind), NSA_H, True,
                              lambda t, h, w: CF[:, C_CAUSAL + P * (1 - t):C_CAUSAL + P * (1 - t) + w], kind == 0)
            dve.wait_ge(sem("att_values"), att_base(l, 2))
            for kind in range(2):
                dve.reciprocal(sums2[kind], sums2[kind])
                dve.drain()
                dve.tensor_tensor(cw, sums2[kind], gate[:, :, 1 + kind], ALU.mult)
                dve.drain()
                dve.tensor_tensor(ob2, PSA[:, kind, :].rearrange("p (h e) -> p h e", e=64), cw.unsqueeze(2).broadcast_to([P, 16, 64]), ALU.mult)
                dve.drain()
                dve.tensor_tensor(ob, ob, ob2, ALU.add)
                dve.drain()
            phase(dve, "attention done")

        def pe_join(pe, l):
            L = L2[l]
            pe_turn(pe, OB, 4, "ob")
            for n, src in ((L["oa"], OAT), (L["ob"], OBT)):
                if src is OBT:
                    pe.wait_ge(sem("turned_taken"), turns["pe"])
                    need(pe, "ya_taken")
                pe_out(pe, [n], src)
            need(pe, "ym_ready")
            pe_turn(pe, YM, 8, "ym")
            pe.wait_ge(sem("turned_taken"), turns["pe"])
            pe_out(pe, L["out"], YMT)
            phase(pe, "mixed")

        def act_join(act, l):
            phase(act, "mixed")

        def dve_join(dve, l):
            L = L2[l]
            take_turned(dve, OBT, 4)
            ps = PSA[:, :, :]
            dve.wait_ge(sem("item_used"), L["oa"] + 1)
            for hf in range(2):
                e = dve.tensor_tensor(YM[:, :, 512 * hf:512 * hf + 512], ps[:, :, 512 * hf:512 * hf + 512], GATES[hf], ALU.mult)
            e.then_inc(sem("ya_taken"), 1)
            dve.wait_ge(sem("item_used"), L["ob"] + 1)
            for hf in range(2):
                dve.tensor_tensor(YM2[:, :, 512 * hf:512 * hf + 512], ps[:, :, 512 * hf:512 * hf + 512], GATES[2 + hf], ALU.mult)
            dve.drain()
            dve.tensor_tensor(YM, YM, YM2, ALU.add).then_inc(sem("ym_ready"), 1)
            take_turned(dve, YMT, 8)
            dve.wait_ge(sem("item_used"), L["out"][1] + 1)
            dve.tensor_tensor(YM2, ps, MODB[:, 2 * D:3 * D].unsqueeze(1).broadcast_to([P, NT, D]), ALU.mult)
            dve.drain()
            dve.tensor_tensor(X[:, :, :], X[:, :, :], YM2, ALU.add)
            dve.drain().then_inc(sem("scratch_free"), 1)
            phase(dve, "mixed")

        def pe_router(pe):
            for t in range(NT):
                for c in range(KC):
                    mm = pe.matmul(PSB[:, 0, N_EXP * t:N_EXP * t + N_EXP], HT[:, c, P * t:P * t + P], router_w[:, c, :],
                                   start=(c == 0), stop=(c == KC - 1))
            mm.then_inc(sem("logits"), 1)
            need(pe, "logits_taken")

        def act_router(act):
            need(act, "top_diff")
            act.activation(top_w[:, :, 1], top_w[:, :, 1], ACT.Exp)
            act.drain().then_inc(sem("top_exp"), 1)

        def dve_router(dve):
            need(dve, "logits")
            dve.tensor_copy(logits, PSB[:, 0, 0:16].rearrange("p (t e) -> p t e", t=NT)).then_inc(sem("logits_taken"), 1)
            dve.drain()
            for t in range(NT):
                dve.max(top8[:, t, :], logits[:, t, :])
            dve.drain()
            for t in range(NT):
                dve.max_index(top_i[:, t, :].bitcast(U32), top8[:, t, :], logits[:, t, :])
            dve.tensor_tensor(top_w[:, :, 1], top8[:, :, 1], top8[:, :, 0], ALU.subtract)
            dve.drain().then_inc(sem("top_diff"), 1)
            dve.tensor_copy(top8, top_i.bitcast(U32))
            need(dve, "top_exp")
            dve.tensor_scalar(top_w[:, :, 0], top_w[:, :, 1], 1.0, None, ALU.add)
            dve.drain()
            dve.reciprocal(top_w[:, :, 0], top_w[:, :, 0])
            dve.drain()
            dve.tensor_tensor(top_w[:, :, 1], top_w[:, :, 1], top_w[:, :, 0], ALU.mult)
            dve.drain()
            for t in range(NT):
                place = CF[:, C_EXP:C_EXP + N_EXP]
                dve.tensor_scalar(combine[:, t, :], place, top8[:, t, 0:1], top_w[:, t, 0:1], ALU.is_equal, ALU.mult)
                dve.tensor_scalar(comb1, place, top8[:, t, 1:2], top_w[:, t, 1:2], ALU.is_equal, ALU.mult)
                dve.drain()
                dve.tensor_tensor(combine[:, t, :], combine[:, t, :], comb1, ALU.add)
                dve.drain()

        CHUNKS = FFN // P

        def pe_expert(pe, l, e, turn):
            fs = L2[l]["ffn"]

            def down(k):
                g, q = k // 4, k % 4
                if q == 0:
                    load(fs[g][2])
                W = view(fs[g][2])
                pe.wait_ge(sem("hidden"), e * CHUNKS + k + 1)
                if k == 0 and not (isinstance(e, int) and e == 0):
                    pe.wait_ge(sem("expert_added"), e)
                for n in range(4):
                    t, hf = n // 2, n % 2
                    mm = pe.matmul(PSA[:, t, 512 * hf:512 * hf + 512], HID[k % 2][:, P * t:P * t + P],
                                   W[:, q, 512 * hf:512 * hf + 512], start=(k == 0), stop=(k == CHUNKS - 1))
                    if q == 2 and n < 2:
                        mm.then_inc(sem("item_used"), 1)
                    if q == 3 and n == 3:
                        mm.then_inc(sem("item_used"), 1)

            def load(n):
                pe.wait_ge(sem(f"slot_loaded{items[n][1]}"), 16 * (items[n][3] + 1) + 48 * turn)

            for k in range(CHUNKS):
                g, q = k // 4, k % 4
                for which, name, free in ((0, "ffn_gate", "ffn_silu"), (1, "ffn_up", "hidden")):
                    if q == 0:
                        load(fs[g][which])
                    W = view(fs[g][which])
                    if not (isinstance(e, int) and e == 0 and k < 2):
                        pe.wait_ge(sem(free), e * CHUNKS + k - 1)
                    for c in range(KC):
                        mm = pe.matmul(PSB[:, 2 * which + k % 2, 0:S], W[:, c, P * q:P * q + P], HT[:, c, :],
                                       start=(c == 0), stop=(c == KC - 1))
                    mm.then_inc(sem(name), 1)
                if k >= 1:
                    down(k - 1)
            down(CHUNKS - 1)

        def act_expert(act, e):
            for k in range(CHUNKS):
                act.wait_ge(sem("ffn_gate"), e * CHUNKS + k + 1)
                if not (isinstance(e, int) and e == 0 and k < 2):
                    act.wait_ge(sem("hidden"), e * CHUNKS + k - 1)
                act.activation(SILU[k % 2], PSB[:, k % 2, 0:S], ACT.Silu).then_inc(sem("ffn_silu"), 1)

        def dve_expert(dve, l, e, weight):
            for k in range(CHUNKS):
                dve.wait_ge(sem("ffn_silu"), e * CHUNKS + k + 1)
                dve.wait_ge(sem("ffn_up"), e * CHUNKS + k + 1)
                dve.tensor_tensor(HID[k % 2], SILU[k % 2], PSB[:, 2 + k % 2, 0:S], ALU.mult).then_inc(sem("hidden"), 1)
            dve.wait_ge(sem("item_used"), weight[1])
            for t in range(NT):
                if weight[0] is None:
                    x = dve.tensor_copy(ACC[:, t, :], PSA[:, t, :])
                else:
                    x = dve.scalar_tensor_tensor(ACC[:, t, :], PSA[:, t, :], weight[0](t), ACC[:, t, :], ALU.mult, ALU.add)
            x.then_inc(sem("expert_added"), 1)
            dve.drain()

        def dve_ffn_end(dve):
            for t in range(NT):
                dve.tensor_tensor(ACC[:, t, :], ACC[:, t, :], MODB[:, 2 * D:3 * D], ALU.mult)
            dve.drain()
            dve.tensor_tensor(X[:, :, :], X[:, :, :], ACC, ALU.add)
            phase(dve, "ffn done")


        PAIRS_BEFORE = 10 + 15

        def pe_block2(pe):
            for l in range(DEPTH):
                pe_ada(pe, L2[l]["ada"])
                pe_delta(pe, l)
                pe_nsa(pe, l)
                pe_join(pe, l)
                pe_ada(pe, L2[l]["ada_f"])
                if l == 0:
                    phase(pe, "ffn")
                    pe_expert(pe, 0, 0, 0)
                else:
                    pe_router(pe)
                    phase(pe, "ffn")
                    with pe.Fori(0, N_EXP) as e:
                        pe_expert(pe, 1, e + 1, e)
                phase(pe, "ffn done")

        def act_block2(act):
            act_positions(act)
            for l in range(DEPTH):
                act_ada(act, L2[l]["ada"])
                act_delta(act, l)
                act_nsa(act, l)
                act_join(act, l)
                act_ada(act, L2[l]["ada_f"])
                if l == 0:
                    phase(act, "ffn")
                    act_expert(act, 0)
                else:
                    act_router(act)
                    phase(act, "ffn")
                    with act.Fori(0, N_EXP) as e:
                        act_expert(act, e + 1)
                phase(act, "ffn done")

        def dve_block2(dve):
            dve_positions(dve)
            for l in range(DEPTH):
                dve_ada(dve, R_MIX[l])
                dve_delta(dve, l)
                dve_nsa(dve, l)
                dve_join(dve, l)
                dve_ada(dve, R_FFN[l])
                last = L2[l]["ffn"][-1][2] + 1
                if l == 0:
                    phase(dve, "ffn")
                    dve_expert(dve, 0, 0, (None, last))
                else:
                    dve_router(dve)
                    dve.memset(ACC, 0.0)
                    phase(dve, "ffn")
                    with dve.Fori(0, N_EXP) as e:
                        dve_expert(dve, 1, e + 1, (lambda t: combine[:, t, bass.ds(e, 1)], e * PER_EXPERT + last))
                dve_ffn_end(dve)

        consts = [(CF[:, :], const_f), (PROJ[:, 0:M_BYTES], const_m), (hot_sb, const_hot), (times_sb, const_times),
                  (rel_sb[:, :], I["rel_bias"]),
                  (lr_w[:, :, :], w_ab[:, 3584:3616].rearrange("(k p) n -> p k n", p=P)),
                  (up_w[:, :, :], I["gla_gate_up"][0].rearrange("d r n -> r d n"))]
        for d in range(2):
            consts.append((gate_bias[:, 4 * d:4 * d + 4], I["gla_gate_bias"][0, d].rearrange("(h p) -> p h", p=P)))
            consts.append((lower[:, d, :], I["hgrn_lower_bounds"][d].rearrange("(h p) -> p h", p=P)))
        N_CONST = len(consts)
        later = [(cT, I["c_2"][0].rearrange("(k p) -> p k", p=P)),
                 (pos_i[:, 0:2].bitcast(I32), I["positions_2"][0].rearrange("(t p) -> p t", p=P)),
                 (router_w[:, :, :], I["w_router_2"][0].rearrange("(k p) e -> p k e", p=P))]
        ends = I["positions_2"][0:1, CMP_LEN - 1:CMP_LEN + CMP_STRIDE * (N_CMP - 1):CMP_STRIDE].rearrange("a j -> j a")
        for g in range(NSA_G):
            later.append((pos_i[N_CMP * g:N_CMP * g + N_CMP, 2:3].bitcast(I32), ends))
        for l in range(DEPTH):
            later.append((ab_w[:, l, :, :], I["w_in_2"][l, :, 2048:2064].rearrange("(k p) n -> p k n", p=P)))
            for w in range(CONV_W):
                later.append((conv_w[:, l, :, w], I["conv_w_2"][l, w].rearrange("(c p) -> p c", p=P)))
            for k, name in enumerate(("a_log_2", "dt_bias_2")):
                later.append((dn_prm[:, l, k, :], I[name][l:l + 1, :].broadcast_to([P, DN_H])))
            for r, src in enumerate([I["q_norm_2"][l:l + 1, :]] + [I["k_norm_2"][l, j:j + 1, :] for j in range(3)]
                                    + [I["dn_norm_2"][l:l + 1, :]]):
                later.append((norm_rows[:, l, r, :], src.broadcast_to([P, 64])))
            for k in range(2):
                later.append((cmp_prm[:, l, 32 * k:32 * k + 32], I["cmp_pos_2"][l, k].rearrange("l d -> d l")))
                later.append((cmp_prm[:, l, 64 + 64 * k:128 + 64 * k], I["w_cmp2_2"][l, k]))

        block = ctx.enter_context(nc.Block())

        @block.sync
        def _(sp):
            sp.dma_start(X[:, :, :], I["x"][0].rearrange("(t p) f -> p t f", p=P)).then_inc(sem("x_loaded"), 16)
            free = 0
            for n, (src, slot, before, _) in enumerate(items):
                if before is not None:
                    sp.wait_ge(sem("item_used"), before + 1)
                for l in range(DEPTH):
                    if n == L2[l]["ffn"][0][0]:
                        free = l + 1
                if slot >= MIX_SLOTS:
                    sp.wait_ge(sem("scratch_free"), free)
                sp.dma_start(view(n), src).then_inc(sem(f"slot_loaded{slot}"), 16)
            first = L2[1]["ffn"][0][0]
            moe = [I[name][0] for name in ("w1_moe_2", "w3_moe_2", "w2_moe_2")]
            with sp.Fori(1, N_EXP) as e:
                for j in range(PER_EXPERT):
                    g, which = j // 3, j % 3
                    w = moe[which][bass.ds(e, 1)]
                    if which < 2:
                        src = w[:, :, 512 * g:512 * g + 512].rearrange("a (k p) n -> p (a k) n", p=P)
                    else:
                        src = w[:, 512 * g:512 * g + 512, :].rearrange("a (k p) n -> p (a k) n", p=P)
                    sp.wait_ge(sem("item_used"), e * PER_EXPERT + (first + j - SLOTS + 1))
                    sp.dma_start(view(first + j), src).then_inc(sem(f"slot_loaded{j % SLOTS}"), 16)
            sp.wait_ge(sem("result"), 1)
            sp.dma_start(out[0].rearrange("(t p) f -> p t f", p=P), X[:, :, :]).then_inc(sem("out_stored"), 16)
            sp.wait_ge(sem("out_stored"), 16)

        @block.gpsimd
        def _(pool):
            for dst, src in consts:
                pool.dma_start(dst, src, allow_slow_non_contiguous=True).then_inc(sem("consts"), 16)
            pool.memset(pos_i.bitcast(I32), 0)
            pool.drain()
            for dst, src in later:
                pool.dma_start(dst, src, allow_slow_non_contiguous=True).then_inc(sem("later"), 16)
            pool_first(pool)

        @block.scalar
        def _(act):
            act_first(act)
            act_second(act)
            act.wait_ge(sem("later"), 16 * len(later))
            act_block2(act)

        @block.vector
        def _(dve):
            dve_first(dve)
            dve_second(dve)
            dve.wait_ge(sem("later"), 16 * len(later))
            dve_block2(dve)
            dve.drain().then_inc(sem("result"), 1)

        @block.tensor
        def _(pe):
            pe_first(pe)
            pe_second(pe)
            pe.wait_ge(sem("later"), 16 * len(later))
            pe_block2(pe)


def kernel(**inputs):
    from concourse import bacc
    from concourse.bass_utils import run_bass_kernel_spmd

    nc = bacc.Bacc("TRN2", target_bir_lowering=False, num_devices=1)
    arrays = {f"in_{name}": np.ascontiguousarray(inputs[name]) for name in INS}
    arrays.update(zip(("const_f", "const_m", "const_hot", "const_times"), constants()))
    aps = {n: nc.dram_tensor(n, a.shape, mybir.dt.from_np(a.dtype), kind="ExternalInput").ap() for n, a in arrays.items()}
    result = nc.dram_tensor("result", (1, S, D), F32, kind="ExternalOutput").ap()
    network(nc, {name: aps[f"in_{name}"] for name in INS}, aps["const_f"], aps["const_m"], aps["const_hot"],
            aps["const_times"], result)
    ran = run_bass_kernel_spmd(nc, [arrays], core_ids=[0])
    return ran.results[0]["result"]
```

```python
from contextlib import ExitStack

import numpy as np

import concourse.bass as bass
from concourse import mybir

F32 = mybir.dt.float32
I32 = mybir.dt.int32
U8 = mybir.dt.uint8
U32 = mybir.dt.uint32
ALU = mybir.AluOpType
ACT = mybir.ActivationFunctionType
AX = mybir.AxisListType

P = 128
S = 256
NT = S // P
D = 1024
KC = D // P
DEPTH = 2

A_HEADS, A_DIM = 8, 64
B_HEADS, B_VAL = 4, 256
C_HEADS, C_VAL = 12, 128
CHUNK = 32
NCH = S // CHUNK
MIX = 1536
MC = MIX // P
GLA_NORM = 16.0
ALPHA = (2 * DEPTH) ** 0.25
LN_EPS = 1e-5
EPS = 1e-6
NEG = -1e30
REL_BUCKETS = 32
REL_MAX = 1024
DIST = 2 * S

DN_H, DN_D, DN_C = 8, 64, 64
DN_QKV = DN_H * 3 * DN_D
CONV_W = 4
NSA_H, NSA_G, NSA_D = 8, 2, 64
CMP_LEN, CMP_STRIDE = 32, 16
N_CMP = (S - CMP_LEN) // CMP_STRIDE + 1
CW = 32
ROPE_THETA = 10000.0
HALF = NSA_D // 2
FFN = 3584
N_EXP = 8
GROUPS = FFN // 512

SLOTS = 7
MIX_SLOTS = 4
SLOT = 4096


def t5_bucket(rel):
    half = REL_BUCKETS // 2
    exact = half // 2
    n = np.abs(rel)
    large = exact + (np.log(np.maximum(n, 1) / exact) / np.log(REL_MAX / exact) * (half - exact)).astype(np.int32)
    large = np.minimum(large, half - 1)
    return np.where(rel > 0, half, 0) + np.where(n < exact, n, large)


C_ID, C_SCAN, C_CAUSAL, C_FREQ, C_CMPM, C_CMPB, C_TRI, C_ROW4, C_EXP, C_BLK = 0, 128, 640, 896, 928, 960, 992, 1120, 1136, 1144
C_BEFORE, C_ONE, C_SLOT = C_BLK + P, C_BLK + 2 * P, C_BLK + 3 * P
C_FLOATS = C_SLOT + P
M_GLA, M_LE, M_LT, M_LEVEL = 0, 512, 640, 768
LEVELS = (1, 2, 4, 8, 16, 32)
M_BYTES = M_LEVEL + P * len(LEVELS)


def constants():
    f = np.zeros((P, C_FLOATS), np.float32)
    m = np.zeros((P, M_BYTES), np.float32)
    p, c = np.arange(P)[:, None], np.arange(P)[None, :]
    t = np.arange(S)
    f[:, C_ID:C_ID + P] = np.eye(P)
    f[:, C_SCAN:C_SCAN + S] = t % CHUNK != 0
    f[:, C_SCAN + S:C_SCAN + 2 * S] = t % CHUNK != CHUNK - 1
    f[:, C_CAUSAL + P:C_CAUSAL + 2 * P] = np.where(c <= p, 0.0, NEG)
    f[:, C_FREQ:C_FREQ + HALF] = 1.0 / (ROPE_THETA ** (np.arange(0, NSA_D, 2, dtype=np.float32) / NSA_D))
    for tile in range(NT):
        q, w = tile * P + p, np.arange(16)[None, :]
        seen = (w * CMP_STRIDE + CMP_LEN - 1 <= q) & (w < N_CMP)
        f[:, C_CMPM + 16 * tile:C_CMPM + 16 * tile + 16] = seen
        f[:, C_CMPB + 16 * tile:C_CMPB + 16 * tile + 16] = np.where(seen, 0.0, NEG)
    f[:, C_TRI:C_TRI + P] = (p <= c) & (p // DN_C == c // DN_C)
    f[:, C_BLK:C_BLK + P] = p // DN_C == c // DN_C
    f[:, C_BEFORE:C_BEFORE + P] = p < c
    f[:, C_ONE:C_ONE + P] = 1.0
    f[:, C_SLOT:C_SLOT + P] = c
    for j in range(4):
        f[:, C_ROW4 + j] = p[:, 0] // CHUNK == j
    f[:, C_EXP:C_EXP + N_EXP] = np.arange(N_EXP)
    same = p // CHUNK == c // CHUNK
    for tile in range(NT):
        m[:, M_GLA + tile * P:M_GLA + tile * P + P] = same & (p <= c)
        m[:, M_GLA + S + tile * P:M_GLA + S + tile * P + P] = same & (p > c)
    block = p // DN_C == c // DN_C
    m[:, M_LE:M_LE + P] = block & (p <= c)
    m[:, M_LT:M_LT + P] = block & (p < c)
    for n, s in enumerate(LEVELS):
        m[:, M_LEVEL + n * P:M_LEVEL + (n + 1) * P] = (p // (2 * s) == c // (2 * s)) & ((c // s) % 2 == 1) & ((p // s) % 2 == 0)
    d = S - np.arange(DIST)
    hot = (t5_bucket(d)[None, :] == np.arange(REL_BUCKETS)[:, None]).astype(np.float32)
    hits = (np.abs(d) <= 64).astype(np.int32) + (d % 4 == 0) + (d % 16 == 0)
    times = np.where(hits > 0, np.log(np.maximum(hits, 1)), NEG).astype(np.float32)
    return f, m, hot, np.repeat(times[None, :], A_HEADS, 0)


INS = ["x", "w_in_ab", "gla_gate_up", "gla_gate_bias", "gla_norm", "w_out_ab", "w_in_c", "hgrn_lower_bounds",
       "hgrn_norm", "w_out_c", "rel_bias", "ln_gain", "ln_bias", "c_2", "positions_2", "w_ada_2", "b_ada_2",
       "norm_mix_2", "norm_ffn_2", "w_in_2", "conv_w_2", "a_log_2", "dt_bias_2", "dn_norm_2", "cmp_pos_2",
       "w_cmp1_2", "w_cmp2_2", "q_norm_2", "k_norm_2", "w_oa_2", "w_ob_2", "w_out_2", "w1_dense_2", "w3_dense_2",
       "w2_dense_2", "w_router_2", "w1_moe_2", "w3_moe_2", "w2_moe_2"]


def network(nc, I, const_f, const_m, const_hot, const_times, out, upto=9):
    ctx = ExitStack()
    with ctx:
        def sb(name, shape, dt=F32):
            return ctx.enter_context(nc.sbuf_tensor(name, shape, dt))

        sems = {}

        def sem(name):
            if name not in sems:
                sems[name] = ctx.enter_context(nc.semaphore(name))
            return sems[name]

        X = sb("X", [P, NT, D])
        HT = sb("HT", [P, KC, S])
        RING = sb("RING", [P, SLOTS * SLOT])
        PROJ = sb("PROJ", [P, 5120])
        MODB = sb("MODB", [P, 3 * D])
        ROW = sb("ROW", [P, 2 * D])
        CF = sb("CF", [P, C_FLOATS])
        CM = sb("CM", [P, M_BYTES], U8)
        small = sb("small", [P, 1664])
        norm_rows = sb("norm_rows", [P, DEPTH, 5, 64])
        cmp_prm = sb("cmp_prm", [NSA_D, DEPTH, 192])
        ab_w = sb("ab_w", [P, 2, KC, 16])
        router_w = sb("router_w", [P, KC, N_EXP])
        PSA = ctx.enter_context(nc.psum_tensor("PSA", [P, 2, 1024], F32))
        PSB = ctx.enter_context(nc.psum_tensor("PSB", [P, 4, 512], F32))
        SCR = RING[:, MIX_SLOTS * SLOT:SLOTS * SLOT]
        SM = SCR[:, 9728:10240].rearrange("p (d t) -> p d t", d=2)
        lrT = SCR[0:16, 10240:10752].rearrange("p (d t) -> p d t", d=2)
        up_w = SCR[0:16, 10752:11776].rearrange("p (d f) -> p d f", d=2)
        squares = SCR[:, 11776:12032]
        lr_w = SCR[:, 12032:12288].rearrange("p (k n) -> p k n", k=KC)
        bias_dram = nc.dram_tensor("bias_by_distance", [A_HEADS, DIST], F32, kind="Internal")

        ident = CF[:, C_ID:C_ID + P]
        at = [0]

        def keep(n):
            at[0] += n
            assert at[0] <= 1664
            return small[:, at[0] - n:at[0]]

        stat = keep(64)
        stats6 = keep(24)
        gate_bias = keep(8)
        lower = keep(24).rearrange("p (l h) -> p l h", l=2)
        lb = keep(12)
        omlb = keep(12)

        items = []

        def item(src, slot=None):
            n = len(items)
            mixer = [i for i in items if i[1] < MIX_SLOTS]
            if slot is None:
                slot = (mixer[-1][1] + 1) % MIX_SLOTS if mixer else 0
            before = [i for i, x in enumerate(items) if x[1] == slot]
            items.append((src, slot, before[-1] if before else None, len(before)))
            return n

        def columns(w, c0, n, slot=None):
            return item(w[:, c0:c0 + n].rearrange("(k p) n -> p k n", p=P), slot)

        def rows(w, r0, slot=None):
            return item(w[r0:r0 + 512, :].rearrange("(k p) n -> p k n", p=P), slot)

        def view(n):
            src, slot, _, _ = items[n]
            p, a, b = src.shape
            return RING[0:p, slot * SLOT:slot * SLOT + a * b].rearrange("p (a b) -> p a b", a=a)

        w_ab, w_c = I["w_in_ab"][0], I["w_in_c"][0]
        AB_Q, AB_K, AB_V = [columns(w_ab, 512 * j, 512) for j in range(3)]
        AB_GLA = [columns(w_ab, 1536 + 512 * j, 512) for j in range(4)]
        AB_GATE = [columns(w_ab, 3616 + 512 * j, 512) for j in range(3)]
        AB_OUT = [rows(I["w_out_ab"][0], 512 * j) for j in range(3)]
        C_GROUP = [[columns(w_c, 1536 * j + 512 * g, 512) for j in range(5)] for g in range(3)]
        C_OUT = [rows(I["w_out_c"][0], 512 * j) for j in range(3)]

        L2 = []
        for l in range(DEPTH):
            w_in, ada = I["w_in_2"][l], I["w_ada_2"][l]
            L2.append(dict(
                ada=[columns(ada, 512 * j, 512) for j in range(6)],
                qkv=[columns(w_in, 512 * j, 512) for j in range(3)],
                z=columns(w_in, 1536, 512),
                nq=columns(w_in, 2064, 512),
                kv=[columns(w_in, 2576, 512), columns(w_in, 3088, 280)],
                cmp=item(I["w_cmp1_2"][l].rearrange("k (l d) e -> d (k l) e", d=NSA_D)),
                mg=[columns(w_in, 3368 + 512 * j, 512) for j in range(4)],
                oa=rows(I["w_oa_2"][l], 0),
                ob=rows(I["w_ob_2"][l], 0),
                out=[rows(I["w_out_2"][l], 512 * j) for j in range(2)],
                ada_f=[columns(ada, 512 * j, 512) for j in range(6, 12)],
            ))
            if l == 0:
                w1, w3, w2 = I["w1_dense_2"][0], I["w3_dense_2"][0], I["w2_dense_2"][0]
            else:
                w1, w3, w2 = I["w1_moe_2"][0, 0], I["w3_moe_2"][0, 0], I["w2_moe_2"][0, 0]
            L2[l]["ffn"] = [(columns(w1, 512 * g, 512, (3 * g) % SLOTS), columns(w3, 512 * g, 512, (3 * g + 1) % SLOTS),
                             rows(w2, 512 * g, (3 * g + 2) % SLOTS)) for g in range(GROUPS)]
        PER_EXPERT = 3 * GROUPS

        row_list = []

        def row(src):
            row_list.append(src)
            return len(row_list) - 1

        R_GLA = row(I["gla_norm"][0:1, :])
        R_LN = [[row(I["ln_gain"][0:1, :]), row(I["ln_bias"][0:1, :])]]
        R_HGRN = [row(I["hgrn_norm"][0:1, 512 * g:512 * g + 512]) for g in range(3)]
        R_LN.append([row(I["ln_gain"][1:2, :]), row(I["ln_bias"][1:2, :])])

        R_MIX, R_FFN = [], []
        for l in range(DEPTH):
            b_ada = I["b_ada_2"]
            R_MIX.append([row(b_ada[l:l + 1, 0:D]), row(b_ada[l:l + 1, D:2 * D]), row(I["norm_mix_2"][l:l + 1, :]),
                          row(b_ada[l:l + 1, 2 * D:3 * D])])
            R_FFN.append([row(b_ada[l:l + 1, 3 * D:4 * D]), row(b_ada[l:l + 1, 4 * D:5 * D]),
                          row(I["norm_ffn_2"][l:l + 1, :]), row(b_ada[l:l + 1, 5 * D:6 * D])])

        def row_at(n):
            w = row_list[n].shape[1]
            return ROW[:, (n % 2) * D:(n % 2) * D + w]

        phases = {}

        def phase(eng, name):
            k = phases.setdefault(eng, 0) + 1
            phases[eng] = k
            eng.drain().then_inc(sem("phase"), 1)
            eng.wait_ge(sem("phase"), 3 * k)

        def wait_item(pe, n):
            pe.wait_ge(sem(f"slot_loaded{items[n][1]}"), 16 * (items[n][3] + 1))

        pairs = {}

        def pair_of(eng):
            k = pairs.get(eng, 0)
            pairs[eng] = k + 1
            return k

        def project_tokens(pe, n, cols=512):
            k = pair_of("pe")
            wait_item(pe, n)
            if k >= 2:
                pe.wait_ge(sem("pair_taken"), k - 1)
            W = view(n)
            for t in range(NT):
                for c in range(KC):
                    mm = pe.matmul(PSA[:, k % 2, 512 * t:512 * t + cols], HT[:, c, P * t:P * t + P], W[:, c, 0:cols],
                                   start=(c == 0), stop=(c == KC - 1))
            mm.then_inc(sem("item_used"), 1)

        def project_features(pe, n):
            k = pair_of("pe")
            wait_item(pe, n)
            if k >= 2:
                pe.wait_ge(sem("pair_taken"), k - 1)
            W = view(n)
            for j in range(4):
                for c in range(KC):
                    mm = pe.matmul(PSA[:, k % 2, S * j:S * j + S], W[:, c, P * j:P * j + P], HT[:, c, :],
                                   start=(c == 0), stop=(c == KC - 1))
            mm.then_inc(sem("item_used"), 1)

        def take(act, n, dst, func=ACT.Copy, scale=1.0, cols=512, tokens=True):
            k = pair_of("act")
            act.wait_ge(sem("item_used"), n + 1)
            src = PSA[:, k % 2, :].rearrange("p (a b) -> p a b", a=2 if tokens else 4)[:, :, 0:cols]
            act.activation(dst, src, func, scale=scale).then_inc(sem("pair_taken"), 1)

        def skip_pairs(eng, n):
            pairs[eng] = pairs.get(eng, 0) + n

        turns = {}

        def pe_turn(pe, src, n_chunks, name):
            for g in range(n_chunks // 2):
                k = turns.setdefault("pe", 0)
                turns["pe"] = k + 1
                if k >= 4:
                    pe.wait_ge(sem("turned_taken"), k - 3)
                for j in range(2):
                    for t in range(NT):
                        mm = pe.transpose(PSB[:, k % 4, S * j + P * t:S * j + P * t + P],
                                          src[:, t, P * (2 * g + j):P * (2 * g + j) + P], ident)
                mm.then_inc(sem("turned"), 1)

        def take_turned(eng, dst, n_chunks):
            for g in range(n_chunks // 2):
                k = turns.setdefault("take", 0)
                turns["take"] = k + 1
                eng.wait_ge(sem("turned"), k + 1)
                eng.tensor_copy(dst[:, 2 * g:2 * g + 2, :],
                                PSB[:, k % 4, :].rearrange("p (a b) -> p a b", a=2)).then_inc(sem("turned_taken"), 1)

        ATT = SCR[:, 3072:3072 + 2048].rearrange("p (b a) -> p b a", b=4)
        s_buf = [ATT[:, b, :].rearrange("p (t k) -> p t k", t=NT) for b in range(2)]
        p_buf = [ATT[:, 2 + b, :].rearrange("p (c q) -> p c q", c=NT) for b in range(2)]
        att_max, att_sum, att_rs = keep(16), keep(16), keep(16)
        amx = [att_max[:, 2 * b:2 * b + 2] for b in range(8)]

        def pe_attention(pe, base, heads, qT, kT, v, out_at, causal, fresh=True):
            def scores(h):
                i = base + h
                if h >= 2 or not fresh:
                    pe.wait_ge(sem("att_scored"), i - 1)
                q = qT(h)
                for t in range(NT):
                    w = P * (t + 1) if causal else S
                    mm = pe.matmul(PSB[:, i % 2, S * t:S * t + w], q[:, P * t:P * t + P], kT(h)[:, 0:w],
                                   start=True, stop=True)
                mm.then_inc(sem("att_scores"), 1)

            def values(h):
                i = base + h
                pe.wait_ge(sem("att_turned_taken"), i + 1)
                for t in range(NT):
                    n = t + 1 if causal else NT
                    for c in range(n):
                        mm = pe.matmul(out_at(t, h), p_buf[i % 2][:, c, P * t:P * t + P], v(c, h),
                                       start=(c == 0), stop=(c == n - 1))
                mm.then_inc(sem("att_values"), 1)

            scores(0)
            for h in range(heads):
                i = base + h
                if h + 1 < heads:
                    scores(h + 1)
                pe.wait_ge(sem("att_probs"), i + 1)
                if h >= 2 or not fresh:
                    pe.wait_ge(sem("att_turned_taken"), i - 1)
                for t in range(NT):
                    for c in range(t + 1 if causal else NT):
                        mm = pe.transpose(PSB[:, 2 + i % 2, S * c + P * t:S * c + P * t + P],
                                          s_buf[i % 2][:, t, P * c:P * c + P], ident)
                mm.then_inc(sem("att_turned"), 1)
                if h >= 1:
                    values(h - 1)
            values(heads - 1)

        def act_attention(act, base, heads, causal, sums, fresh=True):
            for h in range(heads):
                i = base + h
                act.wait_ge(sem("att_scored"), i + 1)
                for t in range(NT):
                    w = P * (t + 1) if causal else S
                    e = act.activation(s_buf[i % 2][:, t, 0:w], s_buf[i % 2][:, t, 0:w], ACT.Exp,
                                       bias=amx[i % 8][:, t:t + 1], accum_out=sums[:, t * heads + h:t * heads + h + 1])
                e.then_inc(sem("att_probs"), 1)
                act.wait_ge(sem("att_turned"), i + 1)
                if h >= 2 or not fresh:
                    act.wait_ge(sem("att_values"), i - 1)
                if causal:
                    act.activation(p_buf[i % 2][:, 0, :], PSB[:, 2 + i % 2, 0:S], ACT.Copy)
                    e = act.activation(p_buf[i % 2][:, 1, P:S], PSB[:, 2 + i % 2, S + P:2 * S], ACT.Copy)
                else:
                    e = act.activation(p_buf[i % 2], PSB[:, 2 + i % 2, :].rearrange("p (c q) -> p c q", c=NT), ACT.Copy)
                e.then_inc(sem("att_turned_taken"), 1)

        def dve_attention(dve, base, heads, causal, bias, fresh=True):
            for h in range(heads):
                i = base + h
                dve.wait_ge(sem("att_scores"), i + 1)
                if h >= 2 or not fresh:
                    dve.wait_ge(sem("att_turned"), i - 1)
                    dve.wait_ge(sem("att_turned_taken"), i - 1)
                for t in range(NT):
                    w = P * (t + 1) if causal else S
                    dve.scalar_tensor_tensor(s_buf[i % 2][:, t, 0:w], PSB[:, i % 2, S * t:S * t + w], A_DIM ** -0.5,
                                             bias(t, h, w), ALU.mult, ALU.add)
                dve.drain()
                for t in range(NT):
                    w = P * (t + 1) if causal else S
                    e = dve.tensor_reduce(amx[i % 8][:, t:t + 1], s_buf[i % 2][:, t, 0:w], AX.X, ALU.max, negate=True)
                e.then_inc(sem("att_scored"), 1)

        gla_at = [0]

        def scratch(n):
            gla_at[0] += n
            assert gla_at[0] <= (SLOTS - MIX_SLOTS) * SLOT
            return SCR[:, gla_at[0] - n:gla_at[0]]

        G_B = [scratch(S) for _ in range(2)]
        G_D = [scratch(2 * S).rearrange("p (a t) -> p a t", a=2) for _ in range(2)]
        G_E = [scratch(4 * S).rearrange("p (a t) -> p a t", a=4) for _ in range(2)]
        G_Q = [scratch(2 * S).rearrange("p (a t) -> p a t", a=2) for _ in range(2)]
        G_K = [scratch(2 * S).rearrange("p (a t) -> p a t", a=2) for _ in range(2)]
        G_KT = [scratch(S).rearrange("p (t f) -> p t f", t=NT) for _ in range(2)]
        G_ST = [scratch(7 * 256) for _ in range(2)]
        G_EB = [keep(NCH) for _ in range(2)]
        ms = keep(NT * 12)
        ref_at = (CHUNK // 2 - 1, CHUNK // 2)
        last_at = (CHUNK - 1, 0)

        def chunked(a):
            return a.rearrange("p (c t) -> p c t", t=CHUNK)

        def dve_decay(dve, j, d, g):
            if j >= 2:
                dve.wait_ge(sem("gla_exp"), j - 1)
            m = CF[:, C_SCAN + d * S:C_SCAN + d * S + S]
            if d == 0:
                dve.tensor_tensor_scan(G_B[d], m, g, 0.0, ALU.mult, ALU.add)
            else:
                dve.tensor_tensor_scan(G_B[d][:, ::-1], m[:, ::-1], g[:, ::-1], 0.0, ALU.mult, ALU.add)
            dve.drain()
            b = chunked(G_B[d])
            for k, where in enumerate((ref_at[d], last_at[d])):
                e = dve.tensor_tensor(chunked(G_D[d][:, k, :]), b,
                                      b[:, :, where:where + 1].broadcast_to([P, NCH, CHUNK]), ALU.subtract)
            e.then_inc(sem("gla_decay"), 1)

        def act_exp(act, j, d, scale):
            act.wait_ge(sem("gla_decay"), j + 1)
            if j >= 2:
                act.wait_ge(sem("gla_scaled"), j - 1)
            act.activation(G_E[d][:, 0, :], G_D[d][:, 0, :], ACT.Exp, scale=scale)
            act.activation(G_E[d][:, 1, :], G_B[d], ACT.Exp, scale=scale)
            act.activation(G_E[d][:, 2:4, :], G_D[d], ACT.Exp, scale=-scale).then_inc(sem("gla_exp"), 1)

        def dve_scale(dve, j, d, q, k, q_scale):
            dve.wait_ge(sem("gla_exp"), j + 1)
            if j >= 2:
                dve.wait_ge(sem("gla_done"), j - 1)
            dve.scalar_tensor_tensor(G_Q[d], G_E[d][:, 0:2, :], q_scale, q.unsqueeze(1).broadcast_to([P, 2, S]),
                                     ALU.mult, ALU.mult)
            dve.tensor_copy(G_EB[d], chunked(G_E[d][:, 1, :])[:, :, last_at[d]])
            dve.tensor_tensor(G_K[d], G_E[d][:, 2:4, :], k.unsqueeze(1).broadcast_to([P, 2, S]), ALU.mult)\
                .then_inc(sem("gla_scaled"), 1)

        def dve_mask(dve, j, d):
            dve.wait_ge(sem("gla_scores"), j + 1)
            dve.copy_predicated(SM[:, d, :], CM[:, M_GLA + d * S:M_GLA + d * S + S], PSB[:, 3, 0:S])\
                .then_inc(sem("gla_masked"), 1)

        def dve_states(dve, j, d, V):
            dve.wait_ge(sem("gla_updates"), j + 1)
            for s in range(NCH - 1):
                c = s if d == 0 else NCH - 1 - s
                U = update(c, V)
                new = G_ST[d][:, V * s:V * s + V]
                if s == 0:
                    e = dve.tensor_copy(new, U)
                else:
                    dve.drain()
                    e = dve.scalar_tensor_tensor(new, G_ST[d][:, V * (s - 1):V * s], G_EB[d][:, c:c + 1], U,
                                                 ALU.mult, ALU.add)
                e.then_inc(sem("gla_state"), 1)

        def pe_gla(pe, n0, heads, V, v):
            gla_scores(pe, 2 * n0)
            for j in range(2 * n0, 2 * (n0 + heads)):
                n, d = j // 2, j % 2
                O = PSB[:, n % 2, 0:2 * V].rearrange("p (t v) -> p t v", t=NT)
                values = [v(t, n - n0) for t in range(NT)]
                pe.wait_ge(sem("gla_masked"), j + 1)
                if d == 0 and n >= 2:
                    pe.wait_ge(sem("gla_out_taken"), n - 1)
                for t in range(NT):
                    pe.matmul(O[:, t, :], SM[:, d, P * t:P * t + P], values[t], start=(d == 0 and t == 0), stop=False,
                              skip_group_check=True)
                pe.wait_ge(sem("gla_turned_taken"), j + 1)
                if j >= 1:
                    pe.wait_ge(sem("gla_state"), (NCH - 1) * j)
                for s in range(NCH):
                    c = s if d == 0 else NCH - 1 - s
                    r = CHUNK * (c % 4)
                    if s < NCH - 1:
                        mm = pe.matmul(update(c, V), G_KT[d][r:r + CHUNK, c // 4, :], values[c // 4][r:r + CHUNK, :],
                                       start=True, stop=True)
                mm.then_inc(sem("gla_updates"), 1)
                if j + 1 < 2 * (n0 + heads):
                    gla_scores(pe, j + 1)
                for s in range(NCH - 1):
                    c = s + 1 if d == 0 else NCH - 2 - s
                    pe.wait_ge(sem("gla_state"), 7 * j + s + 1)
                    r = CHUNK * (c % 4)
                    mm = pe.matmul(O[r:r + CHUNK, c // 4, :], G_Q[d][:, 1, CHUNK * c:CHUNK * c + CHUNK],
                                   G_ST[d][:, V * s:V * s + V], start=False, stop=True, skip_group_check=True)
                mm.then_inc(sem("gla_done"), 1)

        def update(c, V):
            at = 512 * (c % 2) + V * (c // 4)
            return PSA[:, c % 4 // 2, at:at + V]

        def gla_scores(pe, j):
            d = j % 2
            pe.wait_ge(sem("gla_scaled"), j + 1)
            if j >= 1:
                pe.wait_ge(sem("gla_turned_taken"), j)
                pe.wait_ge(sem("gla_masked"), j)
            for t in range(NT):
                pe.transpose(PSB[:, 2, P * t:P * t + P], G_K[d][:, 1, P * t:P * t + P], ident)
            for t in range(NT):
                mm = pe.matmul(PSB[:, 3, P * t:P * t + P], G_K[d][:, 0, P * t:P * t + P],
                               G_Q[d][:, 0, P * t:P * t + P], start=True, stop=True)
            mm.then_inc(sem("gla_scores"), 1)

        def act_gla(act, n0, heads, V, scale, y):
            end = 2 * (n0 + heads)

            def square(n):
                act.wait_ge(sem("gla_out_taken"), n + 1)
                for t in range(NT):
                    act.activation(squares[:, 0:V], y(n - n0)[:, t, :], ACT.Square,
                                   accum_out=ms[:, t * heads + n - n0:t * heads + n - n0 + 1])
                    act.drain()

            act_exp(act, 2 * n0, 0, scale)
            act_exp(act, 2 * n0 + 1, 1, scale)
            for j in range(2 * n0, end):
                act.wait_ge(sem("gla_scores"), j + 1)
                act.activation(G_KT[j % 2], PSB[:, 2, 0:S].rearrange("p (t f) -> p t f", t=NT), ACT.Copy)\
                    .then_inc(sem("gla_turned_taken"), 1)
                if j + 2 < end:
                    act_exp(act, j + 2, j % 2, scale)
                if j % 2 == 0 and j > 2 * n0:
                    square(j // 2 - 1)
            square(n0 + heads - 1)
            act.drain().then_inc(sem("gla_squared"), 1)

        def dve_gla(dve, n0, heads, V, q, k, g, y, q_scale):
            total = heads * 2

            def decay(i):
                dve_decay(dve, 2 * n0 + i, i % 2, g(i % 2, i // 2))

            def scaled(i):
                dve_scale(dve, 2 * n0 + i, i % 2, q(i // 2), k(i % 2, i // 2), q_scale)

            def take_out(h):
                dve.wait_ge(sem("gla_done"), 2 * (n0 + h) + 2)
                dve.tensor_copy(y(h), PSB[:, (n0 + h) % 2, 0:2 * V].rearrange("p (t v) -> p t v", t=NT))\
                    .then_inc(sem("gla_out_taken"), 1)

            decay(0)
            decay(1)
            scaled(0)
            for i in range(total):
                dve_mask(dve, 2 * n0 + i, i % 2)
                if i + 1 < total:
                    scaled(i + 1)
                if i + 2 < total:
                    decay(i + 2)
                if i % 2 == 0 and i > 0:
                    take_out(i // 2 - 1)
                dve_states(dve, 2 * n0 + i, i % 2, V)
            take_out(heads - 1)

        counts = {}

        def dve_rs(dve, a, scale, eps):
            k = counts.get("dve_rs", 0) + 1
            counts["dve_rs"] = k
            dve.tensor_scalar(a, a, scale, eps, ALU.mult, ALU.add).then_inc(sem("rs_ready"), 1)
            dve.wait_ge(sem("rs_done"), k)

        def act_rs(act, a):
            k = counts.get("act_rs", 0) + 1
            counts["act_rs"] = k
            act.wait_ge(sem("rs_ready"), k)
            act.activation(a, a, ACT.Ln)
            act.drain()
            act.activation(a, a, ACT.Exp, scale=-0.5).then_inc(sem("rs_done"), 1)

        def pe_out(pe, its, YT):
            for n, it in enumerate(its):
                wait_item(pe, it)
                W = view(it)
                for t in range(NT):
                    for hf in range(2):
                        for c in range(4):
                            mm = pe.matmul(PSA[:, t, 512 * hf:512 * hf + 512], YT[:, 4 * n + c, P * t:P * t + P],
                                           W[:, c, 512 * hf:512 * hf + 512], start=(n == 0 and c == 0),
                                           stop=(n == len(its) - 1 and c == 3))
                mm.then_inc(sem("item_used"), 1)

        def dve_layer_norm(dve, its, layer):
            dve.wait_ge(sem("item_used"), its[-1] + 1)
            for t in range(NT):
                dve.scalar_tensor_tensor(X[:, t, :], X[:, t, :], ALPHA, PSA[:, t, :], ALU.mult, ALU.add)
            dve.drain()
            st = stats6.rearrange("p (t a) -> p t a", t=NT)
            for t in range(NT):
                for hf in range(2):
                    dve.bn_stats(st[:, t, 6 * hf:6 * hf + 6], X[:, t, 512 * hf:512 * hf + 512])
            dve.drain()
            mv = stat[:, 0:4].rearrange("p (t a) -> p t a", t=NT)
            rs = stat[:, 4:6]
            for t in range(NT):
                dve.bn_aggr(mv[:, t, :], st[:, t, :])
            dve.drain()
            dve.tensor_copy(rs, mv[:, :, 1])
            dve.drain()
            dve_rs(dve, rs, 1.0, LN_EPS)
            for t in range(NT):
                dve.tensor_scalar(X[:, t, :], X[:, t, :], mv[:, t, 0:1], rs[:, t:t + 1], ALU.subtract, ALU.mult)
            dve.drain()
            for n, op in zip(R_LN[layer], (ALU.mult, ALU.add)):
                wait_row(dve, n)
                dve.tensor_tensor(X[:, :, :], X[:, :, :], row_at(n).unsqueeze(1).broadcast_to([P, NT, D]), op)
                dve.drain().then_inc(sem("row_used"), 1)

        def wait_row(dve, n):
            dve.wait_ge(sem(f"row_loaded{n % 2}"), 16 * (n // 2 + 1))

        def dve_head_norm(dve, y, heads, V, gain, gate_ready, gate):
            m = ms[:, 0:NT * heads]
            dve_rs(dve, m, 1.0 / V, LN_EPS)
            rs = m.rearrange("p (t h) -> p t h", t=NT)
            for t in range(NT):
                yy = y[:, t, :].rearrange("p (h v) -> p h v", h=heads)
                dve.tensor_tensor(yy, yy, rs[:, t, :].unsqueeze(2).broadcast_to([P, heads, V]), ALU.mult)
            wait_row(dve, gain)
            dve.drain()
            dve.tensor_tensor(y, y, row_at(gain).unsqueeze(1).broadcast_to([P, NT, heads * V]), ALU.mult)
            dve.drain().then_inc(sem("row_used"), 1)
            gate_ready()
            dve.tensor_tensor(y, y, gate, ALU.mult)

        proj = PROJ[:, :]
        ab_q = proj[:, 0:1024].rearrange("p (a t) -> p a t", a=4)
        ab_k = proj[:, 1024:2048].rearrange("p (a t) -> p a t", a=4)
        ab_v = proj[:, 2048:3072].rearrange("p (t f) -> p t f", t=NT)
        bias_t = SCR[:, 0:3072].rearrange("p (h u) -> p h u", h=A_HEADS)
        gla_v = proj[:, 2048:4096].rearrange("p (t f) -> p t f", t=NT)
        gla_g = [g.rearrange("p (h t) -> p h t", h=4) for g in (proj[:, 4096:5120], MODB[:, 2048:3072])]
        ab_gate = proj[:, 0:3072].rearrange("p (t f) -> p t f", t=NT)
        Y3 = sb("Y3", [P, NT, MIX])
        YT = SCR[:, 0:MC * S].rearrange("p (c t) -> p c t", c=MC)
        rel_sb = sb("rel_sb", [REL_BUCKETS, A_HEADS])
        hot_sb = SCR[0:REL_BUCKETS, 8192:8192 + DIST]
        times_sb = SCR[0:A_HEADS, 8192 + DIST:8192 + 2 * DIST]
        tab_sb = SCR[0:A_HEADS, 8192 + 2 * DIST:8192 + 3 * DIST]

        z_raw = [SCR[:, 1024 * d:1024 * d + 1024] for d in range(2)]
        z_log = [Y3[:, d, 512:MIX] for d in range(2)]

        c_q = proj[:, 0:1024].rearrange("p (a t) -> p a t", a=4)
        c_k = [MODB[:, 1024 * (1 + d):1024 * (2 + d)].rearrange("p (a t) -> p a t", a=4) for d in range(2)]
        c_g = [proj[:, 1024 * (1 + d):1024 * (2 + d)].rearrange("p (a t) -> p a t", a=4) for d in range(2)]
        c_v = proj[:, 3072:4096].rearrange("p (t f) -> p t f", t=NT)
        c_gate = proj[:, 4096:5120].rearrange("p (t f) -> p t f", t=NT)

        def pe_first(pe):
            pe.wait_ge(sem("tables"), 16)
            pe.wait_ge(sem("x_loaded"), 16)
            pe_turn(pe, X, KC, "x")
            pe.wait_ge(sem("turned_taken"), KC // 2)
            project_features(pe, AB_Q)
            pe.wait_ge(sem("bias_tables"), 48)
            pe.matmul(PSB[0:A_HEADS, 3, :], rel_sb[:, :], hot_sb, start=True, stop=True).then_inc(sem("bias_row"), 1)
            project_features(pe, AB_K)
            project_tokens(pe, AB_V)
            phase(pe, "attention")
            pe_attention(pe, 0, A_HEADS,
                         lambda h: ab_q[64 * (h % 2):64 * (h % 2) + 64, h // 2, :],
                         lambda h: ab_k[64 * (h % 2):64 * (h % 2) + 64, h // 2, :],
                         lambda c, h: ab_v[:, c, 64 * h:64 * h + 64],
                         lambda t, h: PSA[:, h % 2, 512 * t + 64 * (h // 2):512 * t + 64 * (h // 2) + 64], False)
            phase(pe, "attention done")
            pe.wait_ge(sem("consts"), 16 * N_CONST)
            project_features(pe, AB_GLA[0])
            project_features(pe, AB_GLA[1])
            project_tokens(pe, AB_GLA[2])
            project_tokens(pe, AB_GLA[3])
            for d in range(2):
                for c in range(KC):
                    mm = pe.matmul(PSB[0:16, d, 0:S], lr_w[:, c, 16 * d:16 * d + 16], HT[:, c, :],
                                   start=(c == 0), stop=(c == KC - 1))
            mm.then_inc(sem("lr_done"), 1)
            pe.wait_ge(sem("lr_taken"), 1)
            pe.wait_ge(sem("pair_taken"), 7)
            for d in range(2):
                for h in range(B_HEADS):
                    mm = pe.matmul(PSA[:, d, S * h:S * h + S], up_w[:, d, P * h:P * h + P], lrT[:, d, :],
                                   start=True, stop=True)
                mm.then_inc(sem("gate_logits"), 1)
            phase(pe, "scan")
            pe_gla(pe, 0, B_HEADS, B_VAL, lambda t, h: gla_v[:, t, B_VAL * h:B_VAL * h + B_VAL])
            phase(pe, "scan done")
            for n in AB_GATE:
                project_tokens(pe, n)
            phase(pe, "y")
            pe_turn(pe, Y3, MC, "y")
            pe.wait_ge(sem("turned_taken"), KC // 2 + MC // 2)
            pe_out(pe, AB_OUT, YT)
            phase(pe, "x1")

        def act_first(act):
            act.dma_start(CF[:, :], const_f).then_inc(sem("tables"), 16)
            act.dma_start(PROJ[:, 0:M_BYTES], const_m).then_inc(sem("masks_loaded"), 16)
            for dst, src in ((hot_sb, const_hot), (rel_sb[:, :], I["rel_bias"]), (times_sb, const_times)):
                act.dma_start(dst, src).then_inc(sem("bias_tables"), 16)
            act.wait_ge(sem("masks_kept"), 1)
            take(act, AB_Q, ab_q, cols=S, tokens=False)
            take(act, AB_K, ab_k, cols=S, tokens=False)
            take(act, AB_V, ab_v)
            phase(act, "attention")
            act_attention(act, 0, A_HEADS, False, att_sum)
            phase(act, "attention done")
            take(act, AB_GLA[0], ab_q, cols=S, tokens=False, scale=P ** -0.5)
            take(act, AB_GLA[1], ab_k, cols=S, tokens=False)
            take(act, AB_GLA[2], gla_v[:, :, 0:512])
            take(act, AB_GLA[3], gla_v[:, :, 512:1024])
            act.wait_ge(sem("lr_done"), 1)
            act.activation(lrT[:, :, :], PSB[0:16, 0:2, 0:S], ACT.Copy).then_inc(sem("lr_taken"), 1)
            for d in range(2):
                z = z_log[d]
                act.wait_ge(sem("gate_abs"), d + 1)
                act.activation(z, z, ACT.Exp)
                act.drain()
                act.activation(z, z, ACT.Ln, bias=1.0).then_inc(sem("gate_log"), 1)
            phase(act, "scan")
            act_gla(act, 0, B_HEADS, B_VAL, 1.0 / GLA_NORM,
                    lambda h: Y3[:, :, 512 + B_VAL * h:512 + B_VAL * h + B_VAL])
            phase(act, "scan done")
            act_rs(act, ms[:, 0:NT * B_HEADS])
            for j, n in enumerate(AB_GATE):
                take(act, n, ab_gate[:, :, 512 * j:512 * j + 512], func=ACT.Silu)
            phase(act, "y")
            act_rs(act, stat[:, 4:6])
            phase(act, "x1")

        def dve_first(dve):
            dve.memset(SM[:, :, :], 0.0)
            take_turned(dve, HT, KC)
            dve.wait_ge(sem("masks_loaded"), 16)
            dve.tensor_copy(CM[:, :], PROJ[:, 0:M_BYTES]).then_inc(sem("masks_kept"), 1)
            dve.wait_ge(sem("bias_tables"), 48)
            dve.wait_ge(sem("bias_row"), 1)
            dve.tensor_tensor(tab_sb, PSB[0:A_HEADS, 3, :], times_sb, ALU.add).then_inc(sem("bias_row_taken"), 1)
            phase(dve, "attention")
            dve.wait_ge(sem("bias_spread"), 16)
            dve_attention(dve, 0, A_HEADS, False, lambda t, h, w: bias_t[:, h, P * t:P * t + w][:, ::-1])
            dve.wait_ge(sem("att_values"), A_HEADS)
            dve.reciprocal(att_rs, att_sum)
            dve.drain()
            for t in range(NT):
                for par in range(2):
                    rs = att_rs[:, t * A_HEADS + par:(t + 1) * A_HEADS:2]
                    dst = Y3[:, t, 0:512].rearrange("p (h o e) -> p h o e", o=2, e=64)[:, :, par, :]
                    dve.tensor_tensor(dst, PSA[:, par, 512 * t:512 * t + 256].rearrange("p (h e) -> p h e", e=64),
                                      rs.unsqueeze(2).broadcast_to([P, 4, 64]), ALU.mult)
            phase(dve, "attention done")
            dve.wait_ge(sem("consts"), 16 * N_CONST)
            for d in range(2):
                z = z_log[d]
                zr = z_raw[d]
                dve.wait_ge(sem("gate_logits"), d + 1)
                for h in range(B_HEADS):
                    dve.tensor_scalar(zr[:, S * h:S * h + S], PSA[:, d, S * h:S * h + S],
                                      gate_bias[:, 4 * d + h:4 * d + h + 1], None, ALU.add)
                dve.drain()
                dve.scalar_tensor_tensor(z, zr, -1.0, zr, ALU.mult, ALU.min).then_inc(sem("gate_abs"), 1)
            for d in range(2):
                z = z_log[d]
                zr = z_raw[d]
                dve.wait_ge(sem("gate_log"), d + 1)
                dve.scalar_tensor_tensor(gla_g[d].rearrange("p h t -> p (h t)"), zr, 0.0, z, ALU.min, ALU.subtract)
            phase(dve, "scan")
            dve_gla(dve, 0, B_HEADS, B_VAL, lambda h: ab_q[:, h, :], lambda d, h: ab_k[:, h, :],
                    lambda d, h: gla_g[d][:, h, :],
                    lambda h: Y3[:, :, 512 + B_VAL * h:512 + B_VAL * h + B_VAL], 1.0)
            phase(dve, "scan done")
            dve_head_norm(dve, Y3[:, :, 512:MIX], B_HEADS, B_VAL, R_GLA,
                          lambda: dve.wait_ge(sem("pair_taken"), 10), ab_gate[:, :, 512:MIX])
            dve.tensor_tensor(Y3[:, :, 0:512], Y3[:, :, 0:512], ab_gate[:, :, 0:512], ALU.mult)
            phase(dve, "y")
            take_turned(dve, YT, MC)
            dve_layer_norm(dve, AB_OUT, 0)
            phase(dve, "x1")

        def pool_first(pool):
            for n, src in enumerate(row_list):
                if n >= 2:
                    pool.wait_ge(sem("row_used"), n - 1)
                pool.dma_start(row_at(n), src.broadcast_to([P, src.shape[1]])).then_inc(sem(f"row_loaded{n % 2}"), 16)

        N_C0 = B_HEADS
        C_PAIRS = 10

        NSA_HPG = NSA_H // NSA_G

        def pe_second(pe):
            pe_turn(pe, X, KC, "x")
            pe.wait_ge(sem("turned_taken"), KC + MC // 2)
            for g in range(3):
                for n in C_GROUP[g][0:3]:
                    project_features(pe, n)
                for n in C_GROUP[g][3:5]:
                    project_tokens(pe, n)
                phase(pe, "scan")
                pe_gla(pe, N_C0 + 4 * g, 4, C_VAL, lambda t, h: c_v[:, t, P * h:P * h + P])
                phase(pe, "scan done")
            pe.wait_ge(sem("y_ready"), 1)
            pe_turn(pe, Y3, MC, "y")
            pe.wait_ge(sem("turned_taken"), KC + MC)
            pe_out(pe, C_OUT, YT)
            phase(pe, "x2")

        def act_second(act):
            act.wait_ge(sem("lower_diff"), 1)
            act.activation(lb, lower[:, 0, :], ACT.Exp).then_inc(sem("lower_exp"), 1)
            for g in range(3):
                take(act, C_GROUP[g][0], c_q, func=ACT.Silu, cols=S, tokens=False)
                for d in range(2):
                    take(act, C_GROUP[g][1 + d], c_g[d], func=ACT.Exp, scale=-1.0, cols=S, tokens=False)
                take(act, C_GROUP[g][3], c_v)
                for d in range(2):
                    act.wait_ge(sem("forget"), 2 * g + d + 1)
                    act.activation(c_g[d], c_g[d], ACT.Ln)
                take(act, C_GROUP[g][4], c_gate, func=ACT.Silu)
                phase(act, "scan")
                act_gla(act, N_C0 + 4 * g, 4, C_VAL, 1.0,
                        lambda h: Y3[:, :, 512 * g + P * h:512 * g + P * h + P])
                phase(act, "scan done")
                act_rs(act, ms[:, 0:NT * 4])
            act.wait_ge(sem("later"), 16 * len(later))
            act_positions(act)
            act_rs(act, stat[:, 4:6])
            phase(act, "x2")

        def dve_second(dve):
            take_turned(dve, HT, KC)
            dve.tensor_tensor(lower[:, 0, :], lower[:, 0, :], lower[:, 1, :], ALU.subtract)\
                .then_inc(sem("lower_diff"), 1)
            dve.wait_ge(sem("lower_exp"), 1)
            dve.tensor_scalar(lb, lb, 1.0, None, ALU.add)
            dve.drain()
            dve.reciprocal(lb, lb)
            dve.drain()
            dve.tensor_scalar(omlb, lb, -1.0, 1.0, ALU.mult, ALU.add)
            dve.drain()
            for g in range(3):
                for d in range(2):
                    dve.wait_ge(sem("pair_taken"), C_PAIRS + 5 * g + 2 + d)
                    f = c_g[d]
                    dve.tensor_scalar(f, f, 1.0, None, ALU.add)
                    dve.drain()
                    dve.reciprocal(f, f)
                    dve.drain()
                    dve.tensor_tensor(f, f, omlb[:, 4 * g:4 * g + 4].unsqueeze(2).broadcast_to([P, 4, S]), ALU.mult)
                    dve.drain()
                    dve.tensor_tensor(f, f, lb[:, 4 * g:4 * g + 4].unsqueeze(2).broadcast_to([P, 4, S]), ALU.add)
                    dve.drain()
                    dve.tensor_scalar(c_k[d], f, -1.0, 1.0, ALU.mult, ALU.add).then_inc(sem("forget"), 1)
                phase(dve, "scan")
                y = Y3[:, :, 512 * g:512 * g + 512]
                dve_gla(dve, N_C0 + 4 * g, 4, C_VAL, lambda h: c_q[:, h, :], lambda d, h: c_k[d][:, h, :],
                        lambda d, h: c_g[d][:, h, :], lambda h: y[:, :, P * h:P * h + P], P ** -0.5)
                dve.wait_ge(sem("gla_squared"), g + 2)
                phase(dve, "scan done")
                dve_head_norm(dve, y, 4, C_VAL, R_HGRN[g], lambda: None, c_gate)
                if g == 2:
                    dve.drain().then_inc(sem("y_ready"), 1)
            take_turned(dve, YT, MC)
            dve.wait_ge(sem("later"), 16 * len(later))
            dve_positions(dve)
            dve_layer_norm(dve, C_OUT, 1)
            phase(dve, "x2")


        asked = {}

        def need(eng, name):
            k = asked.get((eng, name), 0) + 1
            asked[eng, name] = k
            eng.wait_ge(sem(name), k)

        cT = keep(8)
        pos_i = keep(4)
        pos_f = keep(4)
        trig = [keep(96).rearrange("p (g f) -> p g f", g=3) for _ in range(2)]
        conv_w = keep(96).rearrange("p (l c w) -> p l c w", l=DEPTH, w=CONV_W)
        dn_prm = keep(32).rearrange("p (l k h) -> p l k h", l=DEPTH, k=2)
        ab_raw = keep(32).rearrange("p (t k h) -> p t k h", t=NT, k=2)
        beta = keep(16).rearrange("p (t h) -> p t h", t=NT)
        decay_g = keep(16).rearrange("p (t h) -> p t h", t=NT)
        dn_ss = keep(32)
        dn_rs = dn_ss.rearrange("p (t h) -> p t h", t=NT)
        gcol = keep(8)
        grest = keep(8)
        e_gc = keep(8)
        e_rest = keep(8)
        e_last = keep(8).rearrange("p (c m) -> p c m", c=2)
        tmp8 = keep(48)
        o_ss = keep(16)
        nsa_ss = keep(24)
        nsa_rs = nsa_ss.rearrange("p (t h) -> p t h", t=NT)
        nsa_gate = keep(48).rearrange("p (t h k) -> p t h k", t=NT, k=3)
        cmp_m, cmp_s = keep(16), keep(16)
        cmp_pb = keep(2)
        cmp_hid = keep(64)
        kc_ss = keep(1)
        sums2 = [keep(16) for _ in range(2)]
        cw = keep(16)
        logits = keep(16).rearrange("p (t e) -> p t e", t=NT)
        top8 = keep(16).rearrange("p (t e) -> p t e", t=NT)
        top_i = keep(16).rearrange("p (t e) -> p t e", t=NT)
        top_w = keep(4).rearrange("p (t e) -> p t e", t=NT)
        chosen = keep(2 * N_EXP).rearrange("p (t e) -> p t e", t=NT)
        chosen1 = keep(N_EXP)
        TURN_COLS = 2 * N_EXP + 1
        t_weight = keep(NT * TURN_COLS).rearrange("p (t n) -> p t n", t=NT)
        t_place = keep(NT * TURN_COLS).rearrange("p (t n) -> p t n", t=NT)
        turns_f = keep(1)
        turns_i = keep(1)
        rms_x = keep(2)
        state_sb = sb("state_sb", [P, 4, DN_D])

        CB = HT[:, :, 0:P]
        H2 = PROJ[:, 0:2 * D].rearrange("p (t f) -> p t f", t=NT)
        RAW = PROJ[:, 0:3072].rearrange("p (c t) -> p c t", c=12)
        CONV = SCR[:, 0:3072].rearrange("p (c t) -> p c t", c=12)
        Z_GATE = PROJ[:, 3072:4096].rearrange("p (t f) -> p t f", t=NT)
        O_A = PROJ[:, 4096:5120].rearrange("p (t f) -> p t f", t=NT)
        OAT = SCR[:, 11264:12288].rearrange("p (c t) -> p c t", c=4)

        def big(k):
            return SCR[:, 1024 * k:1024 * k + 1024].rearrange("p (h t) -> p h t", h=DN_H)

        DM, LT, AT, TI, TT, ZZ, MT = [big(k) for k in range(7)]
        HALVES = (range(0, DN_H // 2), range(DN_H // 2, DN_H))

        def half(a, n):
            return a[:, HALVES[n][0]:HALVES[n][-1] + 1, :].rearrange("p h t -> p (h t)")

        KT = SCR[:, 7168:7680].rearrange("p (m t) -> p m t", m=4)
        BQT = SCR[:, 7680:8704].rearrange("p (m k t) -> p m k t", m=4, k=2)
        QDT = SCR[:, 8704:9216].rearrange("p (m t) -> p m t", m=4)
        WT = SCR[:, 9216:9728].rearrange("p (m t) -> p m t", m=4)
        VNEW = SCR[:, 9728:10240].rearrange("p (h e) -> p h e", h=DN_H)
        DQ, DK, DBK, DQD, DKD, DVB = [PROJ[:, 512 * k:512 * k + 512].rearrange("p (h e) -> p h e", h=DN_H)
                                      for k in range(6)]
        DKBE = SCR[:, 10240:10752].rearrange("p (h e) -> p h e", h=DN_H)

        NQ = PROJ[:, 0:1024].rearrange("p (t f) -> p t f", t=NT)
        KV1 = PROJ[:, 1024:2048].rearrange("p (t f) -> p t f", t=NT)
        KV2 = PROJ[:, 2048:2608].rearrange("p (t f) -> p t f", t=NT)
        NQK = SCR[:, 0:1536].rearrange("p (t h e) -> p t h e", t=NT, h=12)
        ROPE_A = SCR[:, 1536:2304].rearrange("p (h e) -> p h e", h=12)
        ROPE_B = SCR[:, 2304:3072].rearrange("p (h e) -> p h e", h=12)
        QK8 = SCR[:, 3072:5120].rearrange("p (t f) -> p t f", t=NT)
        QKT = SCR[:, 5120:7168].rearrange("p (c t) -> p c t", c=8)
        XT = SCR[0:NSA_D, 7168:8192].rearrange("p (k g t) -> p k g t", k=2, g=NSA_G)
        CMP = SCR[:, 8192:11264]
        VC = CMP[:, 0:512].rearrange("p (g i e) -> p g i e", g=2, i=4)
        PC = CMP[:, 512:1024].rearrange("p (t h c) -> p t h c", t=NT, h=NSA_H)
        PCT = CMP[:, 1024:1536].rearrange("p (t g q) -> p t g q", t=NT, g=NSA_G)
        SCB = CMP[:, 1536:1792].rearrange("p (t h c) -> p t h c", t=NT, h=NSA_H)
        KC_ROWS = CMP[0:30, 1792:1856]
        KC_AB = CMP[0:30, 1856:1984].rearrange("p (k e) -> p k e", k=2)
        KC_DUP = CMP[0:30, 1984:2112].rearrange("p (k e) -> p k e", k=2)
        KCT = CMP[:, 2112:2142]
        OB = SCR[:, 0:1024].rearrange("p (t f) -> p t f", t=NT)
        OBT = SCR[:, 1024:2048].rearrange("p (c t) -> p c t", c=4)
        OB2 = SCR[:, 2048:3072].rearrange("p (t f) -> p t f", t=NT)
        GATES = [Y3.ap().rearrange("p t f -> p (t f)")[:, 1024 * j:1024 * j + 1024] for j in range(3)] + [PROJ[:, 4096:5120]]
        GATES = [g.rearrange("p (t f) -> p t f", t=NT) for g in GATES]
        YM = SCR[:, 3072:5120].rearrange("p (t f) -> p t f", t=NT)
        YM2 = SCR[:, 5120:7168].rearrange("p (t f) -> p t f", t=NT)
        YMT = SCR[:, 7168:9216].rearrange("p (c t) -> p c t", c=8)

        ACC = PROJ[:, 2 * D:4 * D].rearrange("p (t f) -> p t f", t=NT)
        SILU = [PROJ[:, 4096 + S * b:4096 + S * b + S] for b in range(2)]
        HID = [PROJ[:, 4608 + S * b:4608 + S * b + S] for b in range(2)]
        EX = Y3.ap().rearrange("p t f -> p (t f)")
        HTG = EX[:, 0:1024].rearrange("p (k s) -> p k s", k=KC)
        YG = EX[:, 1024:2048]
        SELT = EX[:, 2048:2304].rearrange("p (t q) -> p t q", t=NT)
        SEL = EX[:, 2304:2560].rearrange("p (t q) -> p t q", t=NT)
        SELW = EX[:, 2560:2816].rearrange("p (t q) -> p t q", t=NT)

        ADA_SUMMED = 5
        ONES = HT[:, 0, P:2 * P]

        def dve_ada_sums(dve, its):
            for n in its:
                wait_item(dve, n)
                W = view(n)
                dve.tensor_scalar(W[:, 0, :], W[:, 0, :], cT[:, 0:1], None, ALU.mult)
                for c in range(1, ADA_SUMMED):
                    dve.drain()
                    dve.scalar_tensor_tensor(W[:, 0, :], W[:, c, :], cT[:, c:c + 1], W[:, 0, :], ALU.mult, ALU.add)
                dve.drain().then_inc(sem("ada_summed"), 1)

        def pe_ada(pe, its):
            need(pe, "c_spread")
            for m in range(3):
                k = pair_of("pe")
                if k >= 2:
                    pe.wait_ge(sem("pair_taken"), k - 1)
                for hf in range(2):
                    n = its[2 * m + hf]
                    wait_item(pe, n)
                    W = view(n)
                    for c in range(ADA_SUMMED, KC):
                        pe.matmul(PSA[:, k % 2, 512 * hf:512 * hf + 512], CB[:, c, :], W[:, c, :],
                                  start=(c == ADA_SUMMED), stop=False)
                    need(pe, "ada_summed")
                    pe.matmul(PSA[:, k % 2, 512 * hf:512 * hf + 512], ONES, W[:, 0, :], start=False, stop=True)\
                        .then_inc(sem("item_used"), 1)
            need(pe, "h_ready")
            pe_turn(pe, H2, KC, "h")
            pe.wait_ge(sem("turned_taken"), turns["pe"])

        def act_ada(act, its):
            need(act, "x_ready")
            for t in range(NT):
                e = act.activation(H2[:, t, :], X[:, t, :], ACT.Square, accum_out=rms_x[:, t:t + 1])
            act.drain().then_inc(sem("x_squared"), 1)
            act_rs(act, rms_x)
            for m in range(3):
                k = pair_of("act")
                act.wait_ge(sem("item_used"), its[2 * m + 1] + 1)
                act.activation(MODB[:, D * m:D * m + D], PSA[:, k % 2, :], ACT.Copy).then_inc(sem("pair_taken"), 1)

        def dve_ada(dve, its, rws):
            dve.memset(ONES, 1.0)
            dve.tensor_copy(CB, cT.unsqueeze(2).broadcast_to([P, KC, P])).then_inc(sem("c_spread"), 1)
            dve.drain().then_inc(sem("x_ready"), 1)
            dve_ada_sums(dve, its)
            need(dve, "x_squared")
            dve_rs(dve, rms_x, 1.0 / D, EPS)
            k0 = pairs.get("dve_ada", PAIRS_BEFORE)
            pairs["dve_ada"] = k0 + 3
            m0, m1, m2 = [MODB[:, D * m:D * m + D] for m in range(3)]
            for m, r in ((m0, rws[0]), (m1, rws[1])):
                k0 += 1
                dve.wait_ge(sem("pair_taken"), k0)
                wait_row(dve, r)
                dve.tensor_tensor(m, m, row_at(r), ALU.add)
                dve.drain().then_inc(sem("row_used"), 1)
            wait_row(dve, rws[2])
            dve.scalar_tensor_tensor(m1, m1, 1.0, row_at(rws[2]), ALU.add, ALU.mult)
            dve.drain().then_inc(sem("row_used"), 1)
            for t in range(NT):
                dve.scalar_tensor_tensor(H2[:, t, :], X[:, t, :], rms_x[:, t:t + 1], m1, ALU.mult, ALU.mult)
            dve.drain()
            dve.tensor_tensor(H2, H2, m0.unsqueeze(1).broadcast_to([P, NT, D]), ALU.add).then_inc(sem("h_ready"), 1)
            dve.wait_ge(sem("pair_taken"), k0 + 1)
            wait_row(dve, rws[3])
            dve.tensor_tensor(m2, m2, row_at(rws[3]), ALU.add)
            dve.drain().then_inc(sem("row_used"), 1)
            take_turned(dve, HT, KC)

        def dve_positions(dve):
            dve.tensor_copy(pos_f, pos_i.bitcast(I32))
            dve.drain()
            ang, turn = SCR[:, 4096:4192].rearrange("p (g f) -> p g f", g=3), SCR[:, 4192:4384].rearrange("p (k g f) -> p k g f", k=2, g=3)
            for g in range(3):
                dve.tensor_scalar(ang[:, g, :], CF[:, C_FREQ:C_FREQ + HALF], pos_f[:, g:g + 1], None, ALU.mult)
            dve.drain()
            magic = 12582912.0
            two_pi = [6.28125, 0.0019350051879882812, 3.0199159819567e-07]
            for k in range(2):
                dve.tensor_scalar(turn[:, k], ang, float(1.0 / (2.0 * np.pi)), 0.25 * (1 - k), ALU.mult, ALU.add)
                dve.drain()
                dve.tensor_scalar(turn[:, k], turn[:, k], magic, -magic, ALU.add, ALU.add)
                dve.drain()
                src = ang
                for part in two_pi:
                    dve.scalar_tensor_tensor(trig[k], turn[:, k], -part, src, ALU.mult, ALU.add)
                    dve.drain()
                    src = trig[k]
                if k == 0:
                    dve.tensor_scalar(trig[0], trig[0], float(np.pi / 2), None, ALU.add)
                    dve.drain()
                dve.tensor_scalar(trig[k], trig[k], 3.1415925, -3.1415925, ALU.min, ALU.max)
            dve.drain().then_inc(sem("angles"), 1)
            need(dve, "sines")

        def act_positions(act):
            act.activation(cT, cT, ACT.Silu)
            need(act, "angles")
            for k in range(2):
                act.activation(trig[k], trig[k], ACT.Sin)
            act.drain().then_inc(sem("sines"), 1)

        COS, SIN = trig

        def pe_delta(pe, l):
            L = L2[l]
            for n in L["qkv"]:
                project_features(pe, n)
            project_tokens(pe, L["z"])
            for t in range(NT):
                for c in range(KC):
                    mm = pe.matmul(PSB[:, 3, 16 * t:16 * t + 16], HT[:, c, P * t:P * t + P], ab_w[:, l, c, :],
                                   start=(c == 0), stop=(c == KC - 1))
            mm.then_inc(sem("ab_logits"), 1)
            need(pe, "ab_taken")
            need(pe, "conv_done")
            for t in range(NT):
                for g in range(3):
                    k = turns["pe"]
                    turns["pe"] = k + 1
                    pe.wait_ge(sem("turned_taken"), k - 3)
                    for j in range(4):
                        mm = pe.transpose(PSB[:, k % 4, P * j:P * j + P], CONV[:, 4 * g + j, P * t:P * t + P], ident)
                    mm.then_inc(sem("turned"), 1)
            phase(pe, "tokens")
            for t in range(NT):
                need(pe, "g_spread")
                for h in range(DN_H):
                    pe.matmul(PSA[:, 0, P * h:P * h + P], MT[:, h, :], CF[:, C_TRI:C_TRI + P], start=True, stop=True)
                pe.matmul(PSB[:, 0, 0:DN_H], CF[:, C_TRI:C_TRI + P], decay_g[:, t, :], start=True, stop=True)
                pe.matmul(PSB[:, 0, DN_H:2 * DN_H], CF[:, C_BLK:C_BLK + P], decay_g[:, t, :], start=True, stop=True)\
                    .then_inc(sem("gc_sums"), 1)
                need(pe, "dn_rows")
                for k, src in enumerate((DK, DBK, DQ, DQD)):
                    for m in range(4):
                        mm = pe.transpose(PSB[:, k, P * m:P * m + P], src[:, 2 * m:2 * m + 2, :].rearrange("p a e -> p (a e)"), ident)
                mm.then_inc(sem("dn_turned"), 1)
                need(pe, "dn_turned_taken")
                for h in range(DN_H):
                    o, m = h % 2, h // 2
                    mm = pe.matmul(PSA[:, o, S * m:S * m + S], KT[64 * o:64 * o + 64, m, :],
                                   BQT[64 * o:64 * o + 64, m, :, :].rearrange("p k t -> p (k t)"), start=True, stop=True)
                mm.then_inc(sem("dn_scores"), 1)
                for heads in HALVES:
                    need(pe, "inv_first")
                    for h in heads:
                        mm = pe.transpose(PSA[:, 0, P * h:P * h + P], TT[:, h, :], ident)
                    mm.then_inc(sem("inv_turned"), 1)
                for n in range(1, len(LEVELS)):
                    for heads in HALVES:
                        need(pe, "inv_ready")
                        for h in heads:
                            mm = pe.matmul(PSA[:, 0, P * h:P * h + P], MT[:, h, :], TI[:, h, :], start=True, stop=True)
                        mm.then_inc(sem("inv_z"), 1)
                    for heads in HALVES:
                        need(pe, "inv_z_taken")
                        if n + 1 < len(LEVELS):
                            for h in heads:
                                pe.matmul(PSA[:, 1, P * h:P * h + P], TT[:, h, :], ZZ[:, h, :], start=True, stop=True)
                        for h in heads:
                            mm = pe.matmul(PSB[:, h // 4, P * (h % 4):P * (h % 4) + P], ZZ[:, h, :], TT[:, h, :],
                                           start=True, stop=True)
                        mm.then_inc(sem("inv_tz"), 1)
                for _ in HALVES:
                    need(pe, "inv_done")
                for h in range(DN_H):
                    o, m = h % 2, h // 2
                    mm = pe.matmul(PSA[64 * o:64 * o + 64, 0, P * m:P * m + P], DKBE[:, h, :], TT[:, h, :],
                                   start=(m == 0), stop=True, skip_group_check=True)
                mm.then_inc(sem("w_ready"), 1)
                for h in range(DN_H):
                    o, m = h % 2, h // 2
                    mm = pe.matmul(PSB[:, o, 64 * m:64 * m + 64], TT[:, h, :], DVB[:, h, :], start=(m == 0), stop=False,
                                   skip_group_check=True)
                need(pe, "w_taken")
                for c in range(2):
                    r = DN_C * c
                    need(pe, "dn_state")
                    for h in range(DN_H):
                        o, m = h % 2, h // 2
                        mm = pe.matmul(PSB[r:r + 64, o, 64 * m:64 * m + 64], WT[64 * o:64 * o + 64, m, r:r + 64],
                                       state_sb[64 * o:64 * o + 64, m, :], start=False, stop=True, skip_group_check=True)
                    mm.then_inc(sem("v_new"), 1)
                    for h in range(DN_H):
                        o, m = h % 2, h // 2
                        pe.matmul(PSB[r:r + 64, 2 + o, 64 * m:64 * m + 64], QDT[64 * o:64 * o + 64, m, r:r + 64],
                                  state_sb[64 * o:64 * o + 64, m, :], start=(m == 0), stop=False, skip_group_check=True)
                    need(pe, "v_new_taken")
                    for h in range(DN_H):
                        o, m = h % 2, h // 2
                        mm = pe.matmul(PSA[64 * o:64 * o + 64, 1, 64 * m:64 * m + 64], DKD[r:r + 64, h, :],
                                       VNEW[r:r + 64, h, :], start=(m == 0), stop=True, skip_group_check=True)
                    mm.then_inc(sem("dn_update"), 1)
                for h in range(DN_H):
                    o, m = h % 2, h // 2
                    mm = pe.matmul(PSB[:, 2 + o, 64 * m:64 * m + 64], AT[:, h, :], VNEW[:, h, :], start=False, stop=True,
                                   skip_group_check=True)
                mm.then_inc(sem("dn_out"), 1)
                need(pe, "dn_out_taken")
            phase(pe, "delta done")
            pe_turn(pe, O_A, 4, "oa")

        def act_delta(act, l):
            L = L2[l]
            def conv_silu(j):
                need(act, "conv_sum")
                return act.activation(CONV[:, 4 * j:4 * j + 4, :], CONV[:, 4 * j:4 * j + 4, :], ACT.Silu)

            for i, n in enumerate(L["qkv"]):
                take(act, n, RAW[:, 4 * i:4 * i + 4, :], cols=S, tokens=False)
                if i >= 1:
                    conv_silu(i - 1)
            conv_silu(2).then_inc(sem("conv_done"), 1)
            take(act, L["z"], Z_GATE, func=ACT.Silu)
            need(act, "ab_ready")
            act.activation(beta, ab_raw[:, :, 0, :], ACT.Sigmoid)
            act.activation(tmp8[:, 0:16], tmp8[:, 0:16], ACT.Exp)
            act.activation(dn_prm[:, l, 0, :], dn_prm[:, l, 0, :], ACT.Exp)
            act.drain()
            act.activation(tmp8[:, 0:16], tmp8[:, 0:16], ACT.Ln, bias=1.0)
            act.drain().then_inc(sem("softplus"), 1)
            act_rs(act, dn_ss)
            phase(act, "tokens")
            for t in range(NT):
                need(act, "gc_cols")
                act.activation(e_gc, gcol, ACT.Exp)
                act.activation(e_rest, grest, ACT.Exp)
                e = act.activation(DM, DM, ACT.Exp)
                need(act, "last_cols")
                act.activation(e_last, e_last, ACT.Exp)
                act.drain().then_inc(sem("dn_exp"), 1)
                need(act, "dn_turned")
                act.activation(KT, PSB[:, 0, :].rearrange("p (m t) -> p m t", m=4), ACT.Copy)
                act.activation(BQT[:, :, 0, :], PSB[:, 1, :].rearrange("p (m t) -> p m t", m=4), ACT.Copy)
                act.activation(BQT[:, :, 1, :], PSB[:, 2, :].rearrange("p (m t) -> p m t", m=4), ACT.Copy)
                act.activation(QDT, PSB[:, 3, :].rearrange("p (m t) -> p m t", m=4), ACT.Copy)
                act.drain().then_inc(sem("dn_turned_taken"), 1)
                for _ in LEVELS[1:]:
                    for a in range(len(HALVES)):
                        need(act, "inv_z")
                        act.activation(half(ZZ, a), PSA[:, 0, 512 * a:512 * a + 512], ACT.Copy)\
                            .then_inc(sem("inv_z_taken"), 1)
                need(act, "w_ready")
                act.activation(WT, PSA[:, 0, 0:512].rearrange("p (m t) -> p m t", m=4), ACT.Copy).then_inc(sem("w_taken"), 1)
            need(act, "o_sums")
            act_rs(act, o_ss)
            phase(act, "delta done")

        def dve_delta(dve, l):
            k0 = pairs["dve_ada"]
            for j in range(3):
                k0 += 1
                dve.wait_ge(sem("pair_taken"), k0)
                for i in range(4 * j, 4 * j + 4):
                    dve.tensor_scalar(CONV[:, i, :], RAW[:, i, :], conv_w[:, l, i, 3:4], None, ALU.mult)
                for back in range(1, CONV_W):
                    dve.drain()
                    for i in range(4 * j, 4 * j + 4):
                        e = dve.scalar_tensor_tensor(CONV[:, i, back:S], RAW[:, i, 0:S - back], conv_w[:, l, i, 3 - back:4 - back],
                                                     CONV[:, i, back:S], ALU.mult, ALU.add)
                e.then_inc(sem("conv_sum"), 1)
            pairs["dve_ada"] = k0 + 1
            need(dve, "ab_logits")
            dve.tensor_copy(ab_raw.rearrange("p t k h -> p (t k h)"), PSB[:, 3, 0:32]).then_inc(sem("ab_taken"), 1)
            dve.drain()
            a = ab_raw[:, :, 1, :]
            dve.tensor_tensor(a, a, dn_prm[:, l, 1, :].unsqueeze(1).broadcast_to([P, NT, DN_H]), ALU.add)
            dve.drain()
            dve.scalar_tensor_tensor(tmp8[:, 0:16].rearrange("p (t h) -> p t h", t=NT), a, -1.0, a, ALU.mult, ALU.min)
            dve.drain().then_inc(sem("ab_ready"), 1)
            for t in range(NT):
                for g in range(3):
                    k = turns["take"]
                    turns["take"] = k + 1
                    dve.wait_ge(sem("turned"), k + 1)
                    dve.tensor_copy(Y3[:, t, 512 * g:512 * g + 512], PSB[:, k % 4, :]).then_inc(sem("turned_taken"), 1)
            need(dve, "softplus")
            dve.scalar_tensor_tensor(decay_g, a, 0.0, tmp8[:, 0:16].rearrange("p (t h) -> p t h", t=NT), ALU.max, ALU.add)
            dve.drain()
            dve.scalar_tensor_tensor(decay_g, decay_g, -1.0, dn_prm[:, l, 0, :].unsqueeze(1).broadcast_to([P, NT, DN_H]),
                                     ALU.mult, ALU.mult)
            sq = SCR[:, 4096:6144].rearrange("p (t f) -> p t f", t=NT)
            dve.tensor_tensor(sq, Y3[:, :, 0:1024], Y3[:, :, 0:1024], ALU.mult)
            dve.drain()
            dve.tensor_reduce(dn_ss.rearrange("p (t h) -> p t h", t=NT), sq.rearrange("p t (h e) -> p t h e", e=64), AX.X, ALU.add)
            dve.drain()
            dve_rs(dve, dn_ss, 1.0, EPS)
            dve.tensor_scalar(dn_rs[:, :, 0:8], dn_rs[:, :, 0:8], DN_D ** -0.5, None, ALU.mult)
            dve.memset(state_sb[:, :, :], 0.0)
            phase(dve, "tokens")

            def rows8(a):
                return a.unsqueeze(2).broadcast_to([P, DN_H, 64])

            for t in range(NT):
                q, k, v = [Y3[:, t, 512 * j:512 * j + 512].rearrange("p (h e) -> p h e", h=DN_H) for j in range(3)]
                dve.tensor_copy(MT, decay_g[:, t, :].unsqueeze(2).broadcast_to([P, DN_H, P])).then_inc(sem("g_spread"), 1)
                dve.tensor_tensor(DQ, q, rows8(dn_rs[:, t, 0:8]), ALU.mult)
                dve.tensor_tensor(DK, k, rows8(dn_rs[:, t, 8:16]), ALU.mult)
                dve.tensor_tensor(DVB, v, rows8(beta[:, t, :]), ALU.mult)
                need(dve, "gc_sums")
                dve.tensor_copy(gcol, PSB[:, 0, 0:8])
                dve.drain()
                dve.tensor_tensor(grest, PSB[:, 0, 8:16], gcol, ALU.subtract)
                for h in range(DN_H):
                    dve.tensor_scalar(DM[:, h, :], PSA[:, 0, P * h:P * h + P], gcol[:, h:h + 1], 0.0, ALU.subtract, ALU.min)
                dve.drain().then_inc(sem("gc_cols"), 1)
                gl = PSA[:, 0, :].rearrange("p (m o t) -> p m o t", m=4, o=2)
                for o in range(2):
                    for c in range(2):
                        dve.tensor_copy(e_last[64 * o:64 * o + 64, c, :], gl[64 * o:64 * o + 64, :, o, 64 * c + 63])
                dve.drain().then_inc(sem("last_cols"), 1)
                dve.tensor_tensor(DBK, DK, rows8(beta[:, t, :]), ALU.mult)
                need(dve, "dn_exp")
                dve.tensor_tensor(DQD, DQ, rows8(e_gc), ALU.mult)
                dve.tensor_tensor(DKD, DK, rows8(e_rest), ALU.mult)
                dve.drain()
                dve.scalar_tensor_tensor(DKBE, DBK, -1.0, rows8(e_gc), ALU.mult, ALU.mult).then_inc(sem("dn_rows"), 1)
                dve.tensor_tensor(DM, DM, CM[:, M_LE:M_LE + P].unsqueeze(1).broadcast_to([P, DN_H, P]), ALU.mult)
                dve.drain()
                need(dve, "dn_scores")
                for o in range(2):
                    ps = PSA[:, o, :].rearrange("p (m k t) -> p m k t", m=4, k=2)
                    dm, lt, atd = [x.rearrange("p (m o) t -> p m o t", o=2)[:, :, o, :] for x in (DM, LT, AT)]
                    dve.tensor_tensor(lt, ps[:, :, 0, :], dm, ALU.mult)
                    dve.tensor_tensor(atd, ps[:, :, 1, :], dm, ALU.mult)
                dve.drain()
                dve.tensor_tensor(LT, LT, CM[:, M_LT:M_LT + P].unsqueeze(1).broadcast_to([P, DN_H, P]), ALU.mult)
                dve.drain()

                def level(n, heads):
                    mask = CM[:, M_LEVEL + n * P:M_LEVEL + n * P + P].unsqueeze(1)
                    return mask.broadcast_to([P, len(heads), P])

                for heads in HALVES:
                    hs = slice(heads[0], heads[-1] + 1)
                    dve.tensor_tensor(TT[:, hs, :], LT[:, hs, :], level(0, heads), ALU.mult)
                    dve.tensor_tensor(MT[:, hs, :], LT[:, hs, :], level(1, heads), ALU.mult)
                    dve.drain()
                    dve.scalar_tensor_tensor(TT[:, hs, :], TT[:, hs, :], -1.0,
                                             ident.unsqueeze(1).broadcast_to([P, len(heads), P]), ALU.mult, ALU.add)\
                        .then_inc(sem("inv_first"), 1)
                for a in range(len(HALVES)):
                    need(dve, "inv_turned")
                    dve.tensor_copy(half(TI, a), PSA[:, 0, 512 * a:512 * a + 512]).then_inc(sem("inv_ready"), 1)
                for n in range(1, len(LEVELS)):
                    for a, heads in enumerate(HALVES):
                        hs = slice(heads[0], heads[-1] + 1)
                        need(dve, "inv_tz")
                        if n + 1 < len(LEVELS):
                            dve.tensor_tensor(half(TI, a), half(TI, a), PSA[:, 1, 512 * a:512 * a + 512], ALU.subtract)
                            dve.tensor_tensor(MT[:, hs, :], LT[:, hs, :], level(n + 1, heads), ALU.mult)
                        dve.tensor_tensor(half(TT, a), half(TT, a), PSB[:, a, :], ALU.subtract)
                        dve.drain().then_inc(sem("inv_ready" if n + 1 < len(LEVELS) else "inv_done"), 1)
                for c in range(2):
                    r = DN_C * c
                    dve.drain().then_inc(sem("dn_state"), 1)
                    need(dve, "v_new")
                    vn = VNEW[r:r + 64].rearrange("p (m o) e -> p m o e", o=2)
                    for o in range(2):
                        e = dve.tensor_copy(vn[:, :, o, :], PSB[r:r + 64, o, 0:256].rearrange("p (m e) -> p m e", m=4))
                    e.then_inc(sem("v_new_taken"), 1)
                    need(dve, "dn_update")
                    dve.tensor_tensor(state_sb[:, :, :], state_sb[:, :, :], e_last[:, c, :].unsqueeze(2).broadcast_to([P, 4, 64]), ALU.mult)
                    dve.drain()
                    dve.tensor_tensor(state_sb[:, :, :], state_sb[:, :, :], PSA[:, 1, 0:256].rearrange("p (m e) -> p m e", m=4), ALU.add)
                need(dve, "dn_out")
                oa = O_A[:, t, :].rearrange("p (m o e) -> p m o e", m=4, o=2)
                for o in range(2):
                    e = dve.tensor_copy(oa[:, :, o, :], PSB[:, 2 + o, 0:256].rearrange("p (m e) -> p m e", m=4))
                e.then_inc(sem("dn_out_taken"), 1)
            dve.drain()
            sq = SCR[:, 0:1024].rearrange("p (t f) -> p t f", t=NT)
            dve.tensor_tensor(sq, O_A, O_A, ALU.mult)
            dve.drain()
            dve.tensor_reduce(o_ss, sq.rearrange("p t (h e) -> p (t h) e", e=64), AX.X, ALU.add)
            dve.drain().then_inc(sem("o_sums"), 1)
            dve_rs(dve, o_ss, 1.0 / DN_D, EPS)
            oh = O_A.rearrange("p t (h e) -> p (t h) e", e=64)
            dve.tensor_tensor(oh, oh, o_ss.unsqueeze(2).broadcast_to([P, 16, 64]), ALU.mult)
            dve.drain()
            dve.tensor_tensor(oh, oh, norm_rows[:, l, 4:5, :].broadcast_to([P, 16, 64]), ALU.mult)
            dve.drain()
            dve.tensor_tensor(O_A, O_A, Z_GATE, ALU.mult)
            phase(dve, "delta done")
            take_turned(dve, OAT, 4)

        assert S // 64 <= 16 and S <= 512

        def pe_nsa(pe, l):
            L = L2[l]
            pe.wait_ge(sem("turned_taken"), turns["pe"])
            project_tokens(pe, L["nq"])
            project_tokens(pe, L["kv"][0])
            project_tokens(pe, L["kv"][1], 280)
            pe.wait_ge(sem("pair_taken"), pairs["pe"])
            for kind in range(2):
                for g in range(NSA_G):
                    for t in range(NT):
                        mm = pe.transpose(PSB[0:NSA_D, kind, S * g + P * t:S * g + P * t + P],
                                          KV1[:, t, 64 * (2 * kind + g):64 * (2 * kind + g) + 64], ident)
            mm.then_inc(sem("cmp_turned"), 1)
            need(pe, "cmp_turned_taken")
            wait_item(pe, L["cmp"])
            W = view(L["cmp"])
            pos = cmp_prm[:, l, 0:64].rearrange("p (k l) -> p k l", k=2)
            for kind in range(2):
                for i in range(CMP_LEN):
                    x = XT[:, kind, :, i:i + CMP_STRIDE * (N_CMP - 1) + 1:CMP_STRIDE]
                    mm = pe.matmul(PSB[0:64, 2, 32 * kind:32 * kind + 30].rearrange("p (g j) -> p g j", g=2), W[:, CMP_LEN * kind + i, :], x,
                                   start=(i == 0), stop=(i == CMP_LEN - 1))
                for i in range(CMP_LEN):
                    mm = pe.matmul(PSB[0:64, 2, 64 + kind:65 + kind], W[:, CMP_LEN * kind + i, :], pos[:, kind, i:i + 1],
                                   start=(i == 0), stop=(i == CMP_LEN - 1))
            mm.then_inc(sem("item_used"), 1)
            need(pe, "cmp_hidden")
            w2 = cmp_prm[:, l, 64:192].rearrange("p (k e) -> p k e", k=2)
            hid = cmp_hid[0:64, :]
            pe.matmul(PSB[0:30, 0, 0:64], hid[:, 0:30], w2[:, 0, :], start=True, stop=True)
            for g in range(NSA_G):
                for i in range(4):
                    mm = pe.matmul(PSB[32 * i:32 * i + N_CMP, 1, 64 * g:64 * g + 64], hid[:, 32 + 15 * g:47 + 15 * g], w2[:, 1, :],
                                   start=(g == 0), stop=True, skip_group_check=True)
            mm.then_inc(sem("cmp_kv"), 1)
            for n in L["mg"]:
                project_tokens(pe, n)
            need(pe, "qk_ready")
            need(pe, "kc_rows")
            pe_turn(pe, QK8, 8, "qk")
            pe.wait_ge(sem("turned_taken"), turns["pe"])
            need(pe, "kc_ready")
            pe.transpose(PSB[:, 0, 0:30], KC_DUP.rearrange("p k e -> p (k e)"), ident[0:30, 0:30]).then_inc(sem("kc_turned"), 1)
            need(pe, "kc_taken")
            phase(pe, "compressed")
            for o in range(2):
                for t in range(NT):
                    for m in range(4):
                        g = (2 * m + o) // NSA_HPG
                        mm = pe.matmul(PSB[:, o, 64 * t + 16 * m:64 * t + 16 * m + 15], QKT[64 * o:64 * o + 64, m, P * t:P * t + P],
                                       KCT[64 * o:64 * o + 64, 15 * g:15 * g + 15], start=True, stop=True)
            mm.then_inc(sem("cmp_scores"), 1)
            need(pe, "cmp_probs")
            for t in range(NT):
                for g in range(NSA_G):
                    mm = pe.transpose(PSB[:, 2, S * t + P * g:S * t + P * g + P],
                                      PC[:, t, 4 * g:4 * g + 4, :].rearrange("p h c -> p (h c)"), ident)
            mm.then_inc(sem("cmp_pturned"), 1)
            need(pe, "cmp_ptaken")
            for t in range(NT):
                for g in range(NSA_G):
                    mm = pe.matmul(PSA[:, 0, 512 * t + 256 * g:512 * t + 256 * g + 256], PCT[:, t, g, :],
                                   VC[:, g, :, :].rearrange("p i e -> p (i e)"), start=True, stop=True)
            mm.then_inc(sem("cmp_out"), 1)
            phase(pe, "attention")
            for kind in range(2):
                v = KV1 if kind == 0 else KV2
                c0 = 384 if kind == 0 else 128
                pe_attention(pe, att_base(l, kind), NSA_H,
                             lambda h: QKT[64 * (h % 2):64 * (h % 2) + 64, h // 2, :],
                             lambda h: QKT[64 * (h % 2):64 * (h % 2) + 64, 4 + 2 * kind + h // NSA_HPG, :],
                             lambda c, h: v[:, c, c0 + 64 * (h // NSA_HPG):c0 + 64 * (h // NSA_HPG) + 64],
                             lambda t, h: PSA[:, kind, 512 * t + 64 * h:512 * t + 64 * h + 64], True, kind == 0)
            phase(pe, "attention done")

        def att_base(l, kind):
            return A_HEADS + NSA_H * (2 * l + kind)

        def act_nsa(act, l):
            L = L2[l]
            take(act, L["nq"], NQ)
            take(act, L["kv"][0], KV1)
            take(act, L["kv"][1], KV2, cols=280)
            act.drain()
            act.activation(nsa_gate, KV2[:, :, 256:280].rearrange("p t (h k) -> p t h k", k=3), ACT.Sigmoid)
            need(act, "cmp_turned")
            act.activation(XT.rearrange("p k g t -> p (k g t)"), PSB[0:64, 0:2, :].rearrange("p a b -> p (a b)"), ACT.Copy)\
                .then_inc(sem("cmp_turned_taken"), 1)
            act.wait_ge(sem("item_used"), L["cmp"] + 1)
            act.activation(cmp_pb[0:64, :], PSB[0:64, 2, 64:66], ACT.Copy)
            act.drain()
            for kind in range(2):
                e = act.activation(cmp_hid[0:64, 32 * kind:32 * kind + 30], PSB[0:64, 2, 32 * kind:32 * kind + 30], ACT.Silu,
                                   bias=cmp_pb[0:64, kind:kind + 1])
            e.then_inc(sem("cmp_hidden"), 1)
            need(act, "nsa_sums")
            act_rs(act, nsa_ss)
            need(act, "kc_sums")
            act_rs(act, kc_ss[0:30])
            for j, n in enumerate(L["mg"]):
                take(act, n, GATES[j], func=ACT.Sigmoid)
            need(act, "kc_turned")
            act.activation(KCT, PSB[:, 0, 0:30], ACT.Copy).then_inc(sem("kc_taken"), 1)
            phase(act, "compressed")
            need(act, "cmp_scored")
            act.activation(SCB[:, :, :, 0:15], SCB[:, :, :, 0:15], ACT.Exp).then_inc(sem("cmp_exp"), 1)
            need(act, "cmp_pturned")
            act.activation(PCT.rearrange("p t g q -> p (t g q)"), PSB[:, 2, :], ACT.Copy).then_inc(sem("cmp_ptaken"), 1)
            phase(act, "attention")
            for kind in range(2):
                act_attention(act, att_base(l, kind), NSA_H, True, sums2[kind], kind == 0)
            phase(act, "attention done")


        def dve_nsa(dve, l):
            dve.memset(VC, 0.0)
            dve.memset(PC, 0.0)
            pairs["dve_ada"] += 3
            dve.wait_ge(sem("pair_taken"), pairs["dve_ada"])
            pairs["dve_ada"] += 4
            parts = [(NQ, 0, 0, 8), (KV1, 256, 8, 2), (KV2, 0, 10, 2)]
            q3 = [(src[:, :, c0:c0 + 64 * n].rearrange("p t (h e) -> p t h e", e=64), h0, n) for src, c0, h0, n in parts]
            for src, h0, n in q3:
                dve.tensor_tensor(NQK[:, :, h0:h0 + n, :], src, src, ALU.mult)
            dve.drain()
            dve.tensor_reduce(nsa_rs, NQK, AX.X, ALU.add)
            dve.drain().then_inc(sem("nsa_sums"), 1)
            dve_rs(dve, nsa_ss, 1.0 / NSA_D, EPS)
            for t in range(NT):
                for src, h0, n in q3:
                    dve.tensor_tensor(NQK[:, t, h0:h0 + n, :], src[:, t], nsa_rs[:, t, h0:h0 + n].unsqueeze(2).broadcast_to([P, n, 64]), ALU.mult)
            dve.drain()
            for t in range(NT):
                for r, h0, n in ((0, 0, 8), (2, 8, 2), (3, 10, 2)):
                    dve.tensor_tensor(NQK[:, t, h0:h0 + n, :], NQK[:, t, h0:h0 + n, :], norm_rows[:, l, r:r + 1, :].broadcast_to([P, n, 64]), ALU.mult)
            for t in range(NT):
                dve.drain()
                for dst, tr in ((ROPE_A, COS), (ROPE_B, SIN)):
                    for hf in range(2):
                        dve.tensor_tensor(dst[:, :, HALF * hf:HALF * hf + HALF], NQK[:, t, :, HALF * hf:HALF * hf + HALF],
                                          tr[:, t:t + 1, :].broadcast_to([P, 12, HALF]), ALU.mult)
                dve.drain()
                for hf, op in ((0, ALU.subtract), (1, ALU.add)):
                    a, b = ROPE_A[:, :, HALF * hf:HALF * hf + HALF], ROPE_B[:, :, HALF * (1 - hf):HALF * (1 - hf) + HALF]
                    q = QK8[:, t, 0:512].rearrange("p (h e) -> p h e", e=64)
                    dve.tensor_tensor(q[:, :, HALF * hf:HALF * hf + HALF], a[:, 0:8], b[:, 0:8], op)
                    kd = QK8[:, t, 512:1024].rearrange("p (k c e) -> p k c e", k=4, c=2)
                    for twice in range(2):
                        e = dve.tensor_tensor(kd[:, :, twice, HALF * hf:HALF * hf + HALF], a[:, 8:12], b[:, 8:12], op)
            e.then_inc(sem("qk_ready"), 1)
            need(dve, "cmp_kv")
            dve.tensor_copy(KC_ROWS, PSB[0:30, 0, 0:64])
            for g in range(NSA_G):
                for i in range(4):
                    dve.tensor_copy(VC[32 * i:32 * i + N_CMP, g, i, :], PSB[32 * i:32 * i + N_CMP, 1, 64 * g:64 * g + 64])
            dve.drain().then_inc(sem("kc_rows"), 1)
            dve.tensor_tensor(KC_AB[:, 0, :], KC_ROWS, KC_ROWS, ALU.mult)
            dve.drain()
            dve.tensor_reduce(kc_ss[0:30], KC_AB[:, 0, :], AX.X, ALU.add)
            dve.drain().then_inc(sem("kc_sums"), 1)
            dve_rs(dve, kc_ss[0:30], 1.0 / NSA_D, EPS)
            dve.scalar_tensor_tensor(KC_ROWS, KC_ROWS, kc_ss[0:30], norm_rows[0:30, l, 1, :], ALU.mult, ALU.mult)
            dve.drain()
            for k, tr in enumerate((COS, SIN)):
                dve.tensor_tensor(KC_AB[:, k, :].rearrange("p (a e) -> p a e", a=2), KC_ROWS.rearrange("p (a e) -> p a e", a=2),
                                  tr[0:30, 2:3, :].broadcast_to([30, 2, HALF]), ALU.mult)
            dve.drain()
            for hf, op in ((0, ALU.subtract), (1, ALU.add)):
                dve.tensor_tensor(KC_DUP[:, :, HALF * hf:HALF * hf + HALF],
                                  KC_AB[:, 0:1, HALF * hf:HALF * hf + HALF].broadcast_to([30, 2, HALF]),
                                  KC_AB[:, 1:2, HALF * (1 - hf):HALF * (1 - hf) + HALF].broadcast_to([30, 2, HALF]), op)
            dve.drain().then_inc(sem("kc_ready"), 1)
            take_turned(dve, QKT, 8)
            phase(dve, "compressed")
            need(dve, "cmp_scores")
            for o in range(2):
                for t in range(NT):
                    dve.scalar_tensor_tensor(SCB.rearrange("p t (m o) c -> p t m o c", o=2)[:, t, :, o, 0:15],
                                             PSB[:, o, 64 * t:64 * t + 64].rearrange("p (m c) -> p m c", m=4)[:, :, 0:15], NSA_D ** -0.5,
                                             CF[:, C_CMPB + 16 * t:C_CMPB + 16 * t + 15].unsqueeze(1).broadcast_to([P, 4, 15]),
                                             ALU.mult, ALU.add)
            dve.drain()
            s3 = SCB.rearrange("p t h c -> p (t h) c")[:, :, 0:15]
            dve.tensor_reduce(cmp_m, s3, AX.X, ALU.max)
            dve.drain()
            dve.tensor_tensor(s3, s3, cmp_m.unsqueeze(2).broadcast_to([P, 16, 15]), ALU.subtract).then_inc(sem("cmp_scored"), 1)
            need(dve, "cmp_exp")
            for t in range(NT):
                dve.tensor_tensor(PC[:, t, :, 0:15], SCB[:, t, :, 0:15],
                                  CF[:, C_CMPM + 16 * t:C_CMPM + 16 * t + 15].unsqueeze(1).broadcast_to([P, NSA_H, 15]), ALU.mult)
            dve.drain().then_inc(sem("cmp_probs"), 1)
            dve.tensor_reduce(cmp_s, PC.rearrange("p t h c -> p (t h) c"), AX.X, ALU.add)
            dve.drain()
            dve.tensor_scalar(cmp_s, cmp_s, 1e-30, None, ALU.max)
            dve.drain()
            dve.reciprocal(cmp_s, cmp_s)
            dve.drain()
            gate = nsa_gate.rearrange("p t h k -> p (t h) k")
            dve.tensor_tensor(cw, cmp_s, gate[:, :, 0], ALU.mult)
            dve.drain()
            need(dve, "cmp_out")
            ob = OB.rearrange("p t (h e) -> p (t h) e", e=64)
            ob2 = OB2.rearrange("p t (h e) -> p (t h) e", e=64)
            dve.tensor_tensor(ob, PSA[:, 0, :].rearrange("p (h e) -> p h e", e=64), cw.unsqueeze(2).broadcast_to([P, 16, 64]), ALU.mult)
            phase(dve, "attention")
            for kind in range(2):
                dve_attention(dve, att_base(l, kind), NSA_H, True,
                              lambda t, h, w: CF[:, C_CAUSAL + P * (1 - t):C_CAUSAL + P * (1 - t) + w], kind == 0)
            dve.wait_ge(sem("att_values"), att_base(l, 2))
            for kind in range(2):
                dve.reciprocal(sums2[kind], sums2[kind])
                dve.drain()
                dve.tensor_tensor(cw, sums2[kind], gate[:, :, 1 + kind], ALU.mult)
                dve.drain()
                dve.tensor_tensor(ob2, PSA[:, kind, :].rearrange("p (h e) -> p h e", e=64), cw.unsqueeze(2).broadcast_to([P, 16, 64]), ALU.mult)
                dve.drain()
                dve.tensor_tensor(ob, ob, ob2, ALU.add)
                dve.drain()
            phase(dve, "attention done")

        def pe_join(pe, l):
            L = L2[l]
            pe_turn(pe, OB, 4, "ob")
            for n, src in ((L["oa"], OAT), (L["ob"], OBT)):
                if src is OBT:
                    pe.wait_ge(sem("turned_taken"), turns["pe"])
                    need(pe, "ya_taken")
                pe_out(pe, [n], src)
            need(pe, "ym_ready")
            pe_turn(pe, YM, 8, "ym")
            pe.wait_ge(sem("turned_taken"), turns["pe"])
            pe_out(pe, L["out"], YMT)
            phase(pe, "mixed")

        def act_join(act, l):
            phase(act, "mixed")

        def dve_join(dve, l):
            L = L2[l]
            take_turned(dve, OBT, 4)
            ps = PSA[:, :, :]
            dve.wait_ge(sem("item_used"), L["oa"] + 1)
            for hf in range(2):
                e = dve.tensor_tensor(YM[:, :, 512 * hf:512 * hf + 512], ps[:, :, 512 * hf:512 * hf + 512], GATES[hf], ALU.mult)
            e.then_inc(sem("ya_taken"), 1)
            dve.wait_ge(sem("item_used"), L["ob"] + 1)
            for hf in range(2):
                dve.tensor_tensor(YM2[:, :, 512 * hf:512 * hf + 512], ps[:, :, 512 * hf:512 * hf + 512], GATES[2 + hf], ALU.mult)
            dve.drain()
            dve.tensor_tensor(YM, YM, YM2, ALU.add).then_inc(sem("ym_ready"), 1)
            take_turned(dve, YMT, 8)
            dve_ada_sums(dve, L["ada_f"][0:2])
            dve.wait_ge(sem("item_used"), L["out"][1] + 1)
            dve.tensor_tensor(YM2, ps, MODB[:, 2 * D:3 * D].unsqueeze(1).broadcast_to([P, NT, D]), ALU.mult)
            dve.drain()
            dve.tensor_tensor(X[:, :, :], X[:, :, :], YM2, ALU.add)
            dve.drain().then_inc(sem("scratch_free"), 1)
            phase(dve, "mixed")

        def pe_router(pe):
            for t in range(NT):
                for c in range(KC):
                    mm = pe.matmul(PSB[:, 0, N_EXP * t:N_EXP * t + N_EXP], HT[:, c, P * t:P * t + P], router_w[:, c, :],
                                   start=(c == 0), stop=(c == KC - 1))
            mm.then_inc(sem("logits"), 1)
            need(pe, "chosen")
            pe.matmul(PSB[:, 1, 0:8], CF[:, C_BEFORE:C_BEFORE + P], chosen[:, 0, :], start=True, stop=True)
            pe.matmul(PSB[:, 1, 8:16], CF[:, C_BEFORE:C_BEFORE + P], chosen[:, 1, :], start=True, stop=False)
            pe.matmul(PSB[:, 1, 8:16], CF[:, C_ONE:C_ONE + P], chosen[:, 0, :], start=False, stop=True)
            for t in range(NT):
                mm = pe.matmul(PSB[:, 1, 16:24], CF[:, C_ONE:C_ONE + P], chosen[:, t, :], start=(t == 0), stop=(t == NT - 1))
            mm.then_inc(sem("places"), 1)
            need(pe, "places_taken")

        def act_router(act):
            need(act, "top_diff")
            act.activation(top_w[:, :, 1], top_w[:, :, 1], ACT.Exp)
            act.drain().then_inc(sem("top_exp"), 1)

        def dve_router(dve):
            need(dve, "logits")
            dve.tensor_copy(logits, PSB[:, 0, 0:16].rearrange("p (t e) -> p t e", t=NT))
            dve.drain()
            for t in range(NT):
                dve.max(top8[:, t, :], logits[:, t, :])
            dve.drain()
            for t in range(NT):
                dve.max_index(top_i[:, t, :].bitcast(U32), top8[:, t, :], logits[:, t, :])
            dve.tensor_tensor(top_w[:, :, 1], top8[:, :, 1], top8[:, :, 0], ALU.subtract)
            dve.drain().then_inc(sem("top_diff"), 1)
            dve.tensor_copy(top8, top_i.bitcast(U32))
            place = CF[:, C_EXP:C_EXP + N_EXP]
            dve.drain()
            for t in range(NT):
                dve.tensor_scalar(chosen1, place, top8[:, t, 0:1], None, ALU.is_equal)
                dve.drain()
                dve.scalar_tensor_tensor(chosen[:, t, :], place, top8[:, t, 1:2], chosen1, ALU.is_equal, ALU.add)
                dve.drain()
            dve.drain().then_inc(sem("chosen"), 1)
            need(dve, "top_exp")
            dve.tensor_scalar(top_w[:, :, 0], top_w[:, :, 1], 1.0, None, ALU.add)
            dve.drain()
            dve.reciprocal(top_w[:, :, 0], top_w[:, :, 0])
            dve.drain()
            dve.tensor_tensor(top_w[:, :, 1], top_w[:, :, 1], top_w[:, :, 0], ALU.mult)
            dve.memset(t_weight, 0.0)
            dve.memset(t_place, -1e9)
            dve.drain()
            for t in range(NT):
                w = t_weight[:, t, 0:N_EXP]
                dve.tensor_scalar(w, place, top8[:, t, 0:1], top_w[:, t, 0:1], ALU.is_equal, ALU.mult)
                dve.tensor_scalar(chosen1, place, top8[:, t, 1:2], top_w[:, t, 1:2], ALU.is_equal, ALU.mult)
                dve.drain()
                dve.tensor_tensor(w, w, chosen1, ALU.add)
                dve.drain()
            need(dve, "places")
            dve.tensor_reduce(turns_f, PSB[:, 1, 16:24], AX.X, ALU.max)
            for t in range(NT):
                c1 = t_place[:, t, 0:N_EXP]
                dve.scalar_tensor_tensor(c1, PSB[:, 1, 8 * t:8 * t + 8], 1e6, chosen[:, t, :], ALU.add, ALU.mult)
                dve.drain()
                dve.tensor_scalar(c1, c1, -1e6, None, ALU.add)
            dve.drain().then_inc(sem("places_taken"), 1)
            dve.tensor_copy(t_weight[:, :, N_EXP:2 * N_EXP], t_weight[:, :, 0:N_EXP])
            dve.tensor_scalar(t_place[:, :, N_EXP:2 * N_EXP], t_place[:, :, 0:N_EXP], float(-P), None, ALU.add)
            dve.tensor_scalar(turns_f, turns_f, P + 0.5, float(N_EXP), ALU.is_gt, ALU.mult)
            dve.drain()
            dve.tensor_scalar(turns_f, turns_f, float(N_EXP), None, ALU.add)
            dve.drain()
            dve.tensor_copy(turns_i.bitcast(I32), turns_f)
            dve.memset(ACC, 0.0)
            dve.memset(YG, 0.0)
            dve.memset(SELT, 0.0)
            dve_select(dve, SEL, 0, False)
            dve.drain().then_inc(sem("select"), 1)
            dve.drain().then_inc(sem("turns"), 1)

        def turn_count(eng):
            eng.wait_ge(sem("turns"), 1)
            return eng.value_load(turns_i[0:1, :].bitcast(I32), min_val=N_EXP, max_val=2 * N_EXP)

        def dve_select(dve, dst, turn, weighted):
            for t in range(NT):
                col = bass.ds(turn, 1)
                if weighted:
                    dve.tensor_scalar(dst[:, t, :], CF[:, C_SLOT:C_SLOT + P], t_place[:, t, col], t_weight[:, t, col],
                                      ALU.is_equal, ALU.mult)
                else:
                    dve.tensor_scalar(dst[:, t, :], CF[:, C_SLOT:C_SLOT + P], t_place[:, t, col], None, ALU.is_equal)

        def pe_gather(pe):
            for c in range(KC):
                for t in range(NT):
                    mm = pe.matmul(PSA[:, 1, P * c:P * c + P], H2[:, t, P * c:P * c + P], SEL[:, t, :],
                                   start=(t == 0), stop=(t == NT - 1))
            mm.then_inc(sem("gathered"), 1)

        def pe_scatter(pe, t, name):
            for hf in range(2):
                mm = pe.matmul(PSA[:, 1, 512 * hf:512 * hf + 512], SELT[:, t, :], YG[:, 512 * hf:512 * hf + 512],
                               start=True, stop=True)
            mm.then_inc(sem(name), 1)

        def dve_add(dve, t):
            return dve.tensor_tensor(ACC[:, t, :], ACC[:, t, :], PSA[:, 1, :], ALU.add)

        CHUNKS = FFN // P

        def pe_expert(pe, l, e, turn):
            fs = L2[l]["ffn"]
            moe = l == 1
            xT, width = (HTG, P) if moe else (HT[:, :, :], S)

            def load(n):
                pe.wait_ge(sem(f"slot_loaded{items[n][1]}"), 16 * (items[n][3] + 1) + 48 * turn)

            def down(k):
                g, q = k // 4, k % 4
                if q == 0:
                    load(fs[g][2])
                W = view(fs[g][2])
                pe.wait_ge(sem("hidden"), e * CHUNKS + k + 1)
                if k == 0 and moe:
                    pe.wait_ge(sem("rows_kept"), turn + 1)
                for n in range(2 if moe else 4):
                    t, hf = n // 2, n % 2
                    mm = pe.matmul(PSA[:, t, 512 * hf:512 * hf + 512], HID[k % 2][:, P * t:P * t + P],
                                   W[:, q, 512 * hf:512 * hf + 512], start=(k == 0), stop=(k == CHUNKS - 1))
                    if q == 2 and n < 2:
                        mm.then_inc(sem("item_used"), 1)
                    if q == 3 and n == (1 if moe else 3):
                        mm.then_inc(sem("item_used"), 1)

            if moe:
                pe.wait_ge(sem("tokens_taken"), turn + 1)
            for k in range(CHUNKS):
                g, q = k // 4, k % 4
                for which, name, free in ((0, "ffn_gate", "ffn_silu"), (1, "ffn_up", "hidden")):
                    if q == 0:
                        load(fs[g][which])
                    W = view(fs[g][which])
                    if moe or k >= 2:
                        pe.wait_ge(sem(free), e * CHUNKS + k - 1)
                    for c in range(KC):
                        mm = pe.matmul(PSB[:, 2 * which + k % 2, 0:width], W[:, c, P * q:P * q + P], xT[:, c, :],
                                       start=(c == 0), stop=(c == KC - 1))
                    mm.then_inc(sem(name), 1)
                if k >= 1:
                    down(k - 1)
                if moe and k == 3:
                    pe_scatter(pe, 0, "scattered")
                if moe and k == 6:
                    pe.wait_ge(sem("added"), 2 * turn + 1)
                    pe_scatter(pe, 1, "scattered")
                if moe and k == 11:
                    pe.wait_ge(sem("added"), 2 * turn + 2)
                    pe.wait_ge(sem("select_w"), turn + 1)
                    for t in range(NT):
                        mm = pe.transpose(PSA[:, 1, P * t:P * t + P], SELW[:, t, :], ident)
                    mm.then_inc(sem("select_turned"), 1)
                if moe and k == 15:
                    pe.wait_ge(sem("select_t"), turn + 1)
                    pe.wait_ge(sem("select"), turn + 2)
                    pe_gather(pe)
            down(CHUNKS - 1)

        def act_expert(act, l, e, turn):
            moe = l == 1
            width = P if moe else S
            for k in range(CHUNKS):
                act.wait_ge(sem("ffn_gate"), e * CHUNKS + k + 1)
                if moe or k >= 2:
                    act.wait_ge(sem("hidden"), e * CHUNKS + k - 1)
                act.activation(SILU[k % 2][:, 0:width], PSB[:, k % 2, 0:width], ACT.Silu).then_inc(sem("ffn_silu"), 1)
                if moe and k == 12:
                    act.wait_ge(sem("select_turned"), turn + 1)
                    act.activation(SELT.rearrange("p t q -> p (t q)"), PSA[:, 1, 0:S], ACT.Copy).then_inc(sem("select_t"), 1)
            if moe:
                act.wait_ge(sem("gathered"), turn + 2)
                act.wait_ge(sem("ffn_up"), (e + 1) * CHUNKS)
                act_tokens(act)
                act.wait_ge(sem("item_used"), turn * PER_EXPERT + (L2[1]["ffn"][-1][2] + 1))
                act.activation(YG, PSA[:, 0, :], ACT.Copy).then_inc(sem("rows_kept"), 1)

        def act_tokens(act):
            act.activation(HTG.rearrange("p k s -> p (k s)"), PSA[:, 1, :], ACT.Copy).then_inc(sem("tokens_taken"), 1)

        def dve_expert(dve, l, e, turn):
            moe = l == 1
            width = P if moe else S
            for k in range(CHUNKS):
                dve.wait_ge(sem("ffn_silu"), e * CHUNKS + k + 1)
                dve.wait_ge(sem("ffn_up"), e * CHUNKS + k + 1)
                dve.tensor_tensor(HID[k % 2][:, 0:width], SILU[k % 2][:, 0:width], PSB[:, 2 + k % 2, 0:width], ALU.mult)\
                    .then_inc(sem("hidden"), 1)
                if moe and k in (4, 7):
                    t = (k - 4) // 3
                    dve.wait_ge(sem("scattered"), 2 * turn + 1 + t)
                    dve_add(dve, t).then_inc(sem("added"), 1)
                if moe and k == 9:
                    dve_select(dve, SELW, turn, True)
                    dve.drain().then_inc(sem("select_w"), 1)
                if moe and k == 13:
                    dve_select(dve, SEL, turn + 1, False)
                    dve.drain().then_inc(sem("select"), 1)
            if not moe:
                dve.wait_ge(sem("item_used"), L2[0]["ffn"][-1][2] + 1)
                for t in range(NT):
                    dve.tensor_copy(ACC[:, t, :], PSA[:, t, :])
                dve.drain()

        def dve_ffn_end(dve):
            for t in range(NT):
                dve.tensor_tensor(ACC[:, t, :], ACC[:, t, :], MODB[:, 2 * D:3 * D], ALU.mult)
            dve.drain()
            dve.tensor_tensor(X[:, :, :], X[:, :, :], ACC, ALU.add)
            phase(dve, "ffn done")


        PAIRS_BEFORE = 10 + 15

        def pe_block2(pe):
            for l in range(DEPTH):
                pe_ada(pe, L2[l]["ada"])
                pe_delta(pe, l)
                pe_nsa(pe, l)
                pe_join(pe, l)
                pe_ada(pe, L2[l]["ada_f"])
                if l == 0:
                    phase(pe, "ffn")
                    pe_expert(pe, 0, 0, 0)
                else:
                    pe_router(pe)
                    phase(pe, "ffn")
                    n_turns = turn_count(pe)
                    need(pe, "select")
                    pe_gather(pe)
                    with pe.Fori(0, n_turns) as turn:
                        pe_expert(pe, 1, turn + 1, turn)
                    phase(pe, "experts done")
                    pe_scatter(pe, 0, "last_rows")
                    need(pe, "last_added")
                    pe_scatter(pe, 1, "last_rows")
                phase(pe, "ffn done")

        def act_block2(act):
            for l in range(DEPTH):
                act_ada(act, L2[l]["ada"])
                act_delta(act, l)
                act_nsa(act, l)
                act_join(act, l)
                act_ada(act, L2[l]["ada_f"])
                if l == 0:
                    phase(act, "ffn")
                    act_expert(act, 0, 0, 0)
                else:
                    act_router(act)
                    phase(act, "ffn")
                    n_turns = turn_count(act)
                    act.wait_ge(sem("gathered"), 1)
                    act_tokens(act)
                    with act.Fori(0, n_turns) as turn:
                        act_expert(act, 1, turn + 1, turn)
                    phase(act, "experts done")
                phase(act, "ffn done")

        def dve_block2(dve):
            for l in range(DEPTH):
                dve_ada(dve, L2[l]["ada"][l:], R_MIX[l])
                dve_delta(dve, l)
                dve_nsa(dve, l)
                dve_join(dve, l)
                dve_ada(dve, L2[l]["ada_f"][2:], R_FFN[l])
                if l == 0:
                    phase(dve, "ffn")
                    dve_expert(dve, 0, 0, 0)
                    dve_ada_sums(dve, L2[l + 1]["ada"][0:1])
                else:
                    dve_router(dve)
                    phase(dve, "ffn")
                    dve.drain().then_inc(sem("rows_kept"), 1)
                    n_turns = turn_count(dve)
                    with dve.Fori(0, n_turns) as turn:
                        dve_expert(dve, 1, turn + 1, turn)
                    phase(dve, "experts done")
                    for t in range(NT):
                        need(dve, "last_rows")
                        dve_add(dve, t).then_inc(sem("last_added"), 1)
                    dve.drain()
                dve_ffn_end(dve)

        consts = [(lr_w[:, :, :], w_ab[:, 3584:3616].rearrange("(k p) n -> p k n", p=P)),
                  (up_w[:, :, :], I["gla_gate_up"][0].rearrange("d r n -> r d n"))]
        for d in range(2):
            consts.append((gate_bias[:, 4 * d:4 * d + 4], I["gla_gate_bias"][0, d].rearrange("(h p) -> p h", p=P)))
            consts.append((lower[:, d, :], I["hgrn_lower_bounds"][d].rearrange("(h p) -> p h", p=P)))
        N_CONST = len(consts)
        later = [(cT, I["c_2"][0].rearrange("(k p) -> p k", p=P)),
                 (pos_i[:, 0:2].bitcast(I32), I["positions_2"][0].rearrange("(t p) -> p t", p=P)),
                 (router_w[:, :, :], I["w_router_2"][0].rearrange("(k p) e -> p k e", p=P))]
        ends = I["positions_2"][0:1, CMP_LEN - 1:CMP_LEN + CMP_STRIDE * (N_CMP - 1):CMP_STRIDE].rearrange("a j -> j a")
        for g in range(NSA_G):
            later.append((pos_i[N_CMP * g:N_CMP * g + N_CMP, 2:3].bitcast(I32), ends))
        for l in range(DEPTH):
            later.append((ab_w[:, l, :, :], I["w_in_2"][l, :, 2048:2064].rearrange("(k p) n -> p k n", p=P)))
            for w in range(CONV_W):
                later.append((conv_w[:, l, :, w], I["conv_w_2"][l, w].rearrange("(c p) -> p c", p=P)))
            for k, name in enumerate(("a_log_2", "dt_bias_2")):
                later.append((dn_prm[:, l, k, :], I[name][l:l + 1, :].broadcast_to([P, DN_H])))
            for r, src in enumerate([I["q_norm_2"][l:l + 1, :]] + [I["k_norm_2"][l, j:j + 1, :] for j in range(3)]
                                    + [I["dn_norm_2"][l:l + 1, :]]):
                later.append((norm_rows[:, l, r, :], src.broadcast_to([P, 64])))
            for k in range(2):
                later.append((cmp_prm[:, l, 32 * k:32 * k + 32], I["cmp_pos_2"][l, k].rearrange("l d -> d l")))
                later.append((cmp_prm[:, l, 64 + 64 * k:128 + 64 * k], I["w_cmp2_2"][l, k]))

        block = ctx.enter_context(nc.Block())

        @block.sync
        def _(sp):
            sp.dma_start(X[:, :, :], I["x"][0].rearrange("(t p) f -> p t f", p=P)).then_inc(sem("x_loaded"), 16)
            free = 0
            for n, (src, slot, before, _) in enumerate(items):
                if before is not None:
                    sp.wait_ge(sem("item_used"), before + 1)
                for l in range(DEPTH):
                    if n == L2[l]["ffn"][0][0]:
                        free = l + 1
                if slot >= MIX_SLOTS:
                    sp.wait_ge(sem("scratch_free"), free)
                sp.dma_start(view(n), src).then_inc(sem(f"slot_loaded{slot}"), 16)
            first = L2[1]["ffn"][0][0]
            moe = [I[name][0] for name in ("w1_moe_2", "w3_moe_2", "w2_moe_2")]
            n_turns = turn_count(sp)
            expert_reg = sp.alloc_register("expert")
            with sp.Fori(1, n_turns) as turn:
                sp.reg_mov(expert_reg, turn & (N_EXP - 1))
                e = sp.snap(expert_reg, min_val=0, max_val=N_EXP - 1)
                for j in range(PER_EXPERT):
                    g, which = j // 3, j % 3
                    w = moe[which][bass.ds(e, 1)]
                    if which < 2:
                        src = w[:, :, 512 * g:512 * g + 512].rearrange("a (k p) n -> p (a k) n", p=P)
                    else:
                        src = w[:, 512 * g:512 * g + 512, :].rearrange("a (k p) n -> p (a k) n", p=P)
                    sp.wait_ge(sem("item_used"), turn * PER_EXPERT + (first + j - SLOTS + 1))
                    sp.dma_start(view(first + j), src).then_inc(sem(f"slot_loaded{j % SLOTS}"), 16)
            sp.wait_ge(sem("result"), 1)
            sp.dma_start(out[0].rearrange("(t p) f -> p t f", p=P), X[:, :, :]).then_inc(sem("out_stored"), 16)
            sp.wait_ge(sem("out_stored"), 16)

        @block.gpsimd
        def _(pool):
            for dst, src in consts:
                pool.dma_start(dst, src, allow_slow_non_contiguous=True).then_inc(sem("consts"), 16)
            pool.wait_ge(sem("bias_row_taken"), 1)
            pool.dma_start(bias_dram[:, :], tab_sb).then_inc(sem("bias_stored"), 16)
            pool.wait_ge(sem("bias_stored"), 16)
            src = bass.AP(tensor=bias_dram, offset=1, ap=[[1, P], [DIST, A_HEADS], [1, 3 * P]])
            pool.dma_start(bias_t, src).then_inc(sem("bias_spread"), 16)
            pool.memset(pos_i.bitcast(I32), 0)
            pool.drain()
            for dst, src in later:
                pool.dma_start(dst, src, allow_slow_non_contiguous=True).then_inc(sem("later"), 16)
            pool_first(pool)

        @block.scalar
        def _(act):
            act_first(act)
            act_second(act)
            act_block2(act)

        @block.vector
        def _(dve):
            dve_first(dve)
            dve_second(dve)
            dve_block2(dve)
            dve.drain().then_inc(sem("result"), 1)

        @block.tensor
        def _(pe):
            pe_first(pe)
            pe_second(pe)
            pe.wait_ge(sem("later"), 16 * len(later))
            pe_block2(pe)


def kernel(**inputs):
    from concourse import bacc
    from concourse.bass_utils import run_bass_kernel_spmd

    nc = bacc.Bacc("TRN2", target_bir_lowering=False, num_devices=1)
    arrays = {f"in_{name}": np.ascontiguousarray(inputs[name]) for name in INS}
    arrays.update(zip(("const_f", "const_m", "const_hot", "const_times"), constants()))
    aps = {n: nc.dram_tensor(n, a.shape, mybir.dt.from_np(a.dtype), kind="ExternalInput").ap() for n, a in arrays.items()}
    result = nc.dram_tensor("result", (1, S, D), F32, kind="ExternalOutput").ap()
    network(nc, {name: aps[f"in_{name}"] for name in INS}, aps["const_f"], aps["const_m"], aps["const_hot"],
            aps["const_times"], result)
    ran = run_bass_kernel_spmd(nc, [arrays], core_ids=[0])
    return ran.results[0]["result"]
```
